# Optimizing a Trainium2 kernel written in Bass

```python
import jax, jax.numpy as jnp
from jax import lax
import numpy as np

D_MODEL = 1024
BATCH = 1
SEQ = 128
DEPTH = 2
DEC_BATCH = 1
DEC_SEQ = 512
PAST_LEN = 128

GRID_W = 64
CONV_K = 31
MLA_HEADS = 16
QK_NOPE = 64
QK_ROPE = 32
V_HEAD = 64
Q_LORA = 512
KV_LORA = 256
ROPE_THETA = 10000.0
PEER_HEADS = 8
PEER_QDIM = 256
N_KEYS = 128
N_EXPERTS = N_KEYS * N_KEYS
PEER_TOPK = 16
Q_BLOCK = 128
TOKEN_BLOCK = 128
EPS = 1e-6
N_CONV_LAYERS = (DEPTH + 1) // 2
N_ATTN_LAYERS = DEPTH // 2

kernel_name = "hybrid_conv_mla_peer_diffusion_step"

def rmsnorm(x, g):
    xf = x.astype(jnp.float32)
    y = xf * lax.rsqrt(jnp.mean(xf * xf, axis=-1, keepdims=True) + EPS)
    return (y * g.astype(jnp.float32)).astype(x.dtype)

def modulation(cond, w, b):
    m = jax.nn.silu(cond) @ w + b
    return jnp.split(m[:, None, :], 6, axis=-1)

def modulate(x, g, shift, scale):
    return rmsnorm(x, g) * (1 + scale) + shift

def conv_module(x, w_in, b_in, dw, dw_b, norm_g, w_out, b_out):
    h = x @ w_in + b_in
    a, gt = jnp.split(h, 2, axis=-1)
    h = a * jax.nn.sigmoid(gt)
    h = lax.conv_general_dilated(h, dw[:, None, :], window_strides=(1,),
                                 padding=[(CONV_K // 2, CONV_K // 2)],
                                 dimension_numbers=('NWC', 'WIO', 'NWC'),
                                 feature_group_count=D_MODEL) + dw_b
    h = jax.nn.silu(rmsnorm(h, norm_g))
    return h @ w_out + b_out

def axial_rope_tables(seq_len):
    rows = seq_len // GRID_W
    row = jnp.repeat(jnp.arange(rows), GRID_W).astype(jnp.float32)
    col = jnp.tile(jnp.arange(GRID_W), rows).astype(jnp.float32)
    half = QK_ROPE // 2
    inv = ROPE_THETA ** (-(jnp.arange(half // 2, dtype=jnp.float32) * 2.0 / half))
    ang = jnp.concatenate([row[:, None] * inv, col[:, None] * inv], axis=-1)
    return jnp.cos(ang), jnp.sin(ang)

def apply_rope(x, cos, sin):
    xf = x.astype(jnp.float32).reshape(x.shape[:-1] + (-1, 2))
    x1, x2 = xf[..., 0], xf[..., 1]
    out = jnp.stack([x1 * cos - x2 * sin, x1 * sin + x2 * cos], axis=-1).reshape(x.shape)
    return out.astype(x.dtype)

def rope_tail(x, cos, sin):
    return jnp.concatenate([x[..., :QK_NOPE], apply_rope(x[..., QK_NOPE:], cos, sin)], axis=-1)

def mla_queries(x, q_a_w, q_a_norm, q_b_w, q_norm):
    B, S, _ = x.shape
    q = (rmsnorm(x @ q_a_w, q_a_norm) @ q_b_w).reshape(B, S, MLA_HEADS, QK_NOPE + QK_ROPE)
    return rmsnorm(q, q_norm)

def mla_latent(x, kv_a_w, kv_a_norm):
    kv = x @ kv_a_w
    return rmsnorm(kv[..., :KV_LORA], kv_a_norm), kv[..., KV_LORA:]

def mla_keys_values(ckv, kpe, kv_b_w, k_norm):
    B, S, _ = ckv.shape
    kv = (ckv @ kv_b_w).reshape(B, S, MLA_HEADS, QK_NOPE + V_HEAD)
    k_nope, v = kv[..., :QK_NOPE], kv[..., QK_NOPE:]
    k_pe = jnp.broadcast_to(kpe[:, :, None, :], (B, S, MLA_HEADS, QK_ROPE))
    k = rmsnorm(jnp.concatenate([k_nope, k_pe], axis=-1), k_norm)
    return k, v

def blocked_attention(q, k, v):
    B, Sq, H, Dk = q.shape
    nblk = Sq // Q_BLOCK
    qb = q.reshape(B, nblk, Q_BLOCK, H, Dk).transpose(1, 0, 2, 3, 4)
    scale = Dk ** -0.5

    def one(qblk):
        s = jnp.einsum('bqhd,bkhd->bhqk', qblk, k).astype(jnp.float32) * scale
        p = jax.nn.softmax(s, axis=-1).astype(v.dtype)
        return jnp.einsum('bhqk,bkhd->bqhd', p, v)

    o = lax.map(one, qb)
    return o.transpose(1, 0, 2, 3, 4).reshape(B, Sq, H * v.shape[-1])

def peer_ffn(x, wq, keys, u, v):
    B, S, D = x.shape
    xt = x.reshape(-1, TOKEN_BLOCK, D)

    def one(xb):
        T = xb.shape[0]
        q = (xb @ wq).reshape(T, PEER_HEADS, 2, PEER_QDIM // 2)
        s = jnp.einsum('thpd,pnd->thpn', q, keys).astype(jnp.float32)
        sv, si = lax.top_k(s, PEER_TOPK)
        cand = sv[:, :, 0, :, None] + sv[:, :, 1, None, :]
        cidx = si[:, :, 0, :, None] * N_KEYS + si[:, :, 1, None, :]
        top_s, top_pos = lax.top_k(cand.reshape(T, PEER_HEADS, PEER_TOPK * PEER_TOPK), PEER_TOPK)
        eidx = jnp.take_along_axis(cidx.reshape(T, PEER_HEADS, PEER_TOPK * PEER_TOPK), top_pos, axis=-1)
        g = jax.nn.softmax(top_s, axis=-1)
        ue = u[eidx]
        ve = v[eidx]
        act = jax.nn.gelu(jnp.einsum('thkd,td->thk', ue, xb).astype(jnp.float32), approximate=False)
        w = (g * act).astype(xb.dtype)
        return jnp.einsum('thk,thkd->td', w, ve)

    return lax.map(one, xt).reshape(B, S, D)

def setup_inputs(seed: int = 0) -> dict:
    key = jax.random.key(seed)
    ks = iter(jax.random.split(key, 40))

    def nrm(shape, scale):
        return jax.random.normal(next(ks), shape, jnp.float32) * scale

    def gain(shape):
        return 1.0 + nrm(shape, 0.02)

    D = D_MODEL
    NC, NA = N_CONV_LAYERS, N_ATTN_LAYERS
    QK = QK_NOPE + QK_ROPE
    return {
        "x_prompt": nrm((BATCH, SEQ, D), 1.0),
        "x_sample": nrm((DEC_BATCH, DEC_SEQ, D), 1.0),
        "cache_ckv": nrm((DEC_BATCH, NA, PAST_LEN, KV_LORA), 1.0),
        "cache_kpe": nrm((DEC_BATCH, NA, PAST_LEN, QK_ROPE), 1.0),
        "c": nrm((DEC_BATCH, D), 1.0),
        "c_ctx": nrm((D,), 1.0),
        "mod_w": nrm((DEPTH, D, 6 * D), 0.5 * D ** -0.5),
        "mod_b": nrm((DEPTH, 6 * D), 0.02),
        "norm1_g": gain((DEPTH, D)),
        "norm2_g": gain((DEPTH, D)),
        "conv_w_in": nrm((NC, D, 2 * D), D ** -0.5),
        "conv_b_in": nrm((NC, 2 * D), 0.02),
        "conv_dw": nrm((NC, CONV_K, D), CONV_K ** -0.5),
        "conv_dw_b": nrm((NC, D), 0.02),
        "conv_norm_g": gain((NC, D)),
        "conv_w_out": nrm((NC, D, D), D ** -0.5),
        "conv_b_out": nrm((NC, D), 0.02),
        "q_a_w": nrm((NA, D, Q_LORA), D ** -0.5),
        "q_a_norm": gain((NA, Q_LORA)),
        "q_b_w": nrm((NA, Q_LORA, MLA_HEADS * QK), Q_LORA ** -0.5),
        "kv_a_w": nrm((NA, D, KV_LORA + QK_ROPE), D ** -0.5),
        "kv_a_norm": gain((NA, KV_LORA)),
        "kv_b_w": nrm((NA, KV_LORA, MLA_HEADS * (QK_NOPE + V_HEAD)), KV_LORA ** -0.5),
        "q_norm": gain((NA, QK)),
        "k_norm": gain((NA, QK)),
        "o_w": nrm((NA, MLA_HEADS * V_HEAD, D), (MLA_HEADS * V_HEAD) ** -0.5),
        "peer_wq": nrm((DEPTH, D, PEER_HEADS * PEER_QDIM), D ** -0.5),
        "peer_keys": nrm((DEPTH, 2, N_KEYS, PEER_QDIM // 2), (PEER_QDIM // 2) ** -0.5),
        "peer_u": nrm((DEPTH, N_EXPERTS, D), D ** -0.5),
        "peer_v": nrm((DEPTH, N_EXPERTS, D), PEER_HEADS ** -0.5),
    }

def reference(x_prompt, x_sample, cache_ckv, cache_kpe, c, c_ctx, mod_w, mod_b, norm1_g, norm2_g,
              conv_w_in, conv_b_in, conv_dw, conv_dw_b, conv_norm_g, conv_w_out, conv_b_out,
              q_a_w, q_a_norm, q_b_w, kv_a_w, kv_a_norm, kv_b_w, q_norm, k_norm, o_w,
              peer_wq, peer_keys, peer_u, peer_v):
    n_prompt = x_prompt.shape[0]
    cond_p = jnp.broadcast_to(c_ctx[None, :], (n_prompt, D_MODEL))
    cos, sin = axial_rope_tables(x_sample.shape[1])
    cos_h, sin_h = cos[:, None, :], sin[:, None, :]
    h_p, h_s = x_prompt, x_sample
    new_ckv, new_kpe = [], []
    for i in range(DEPTH):
        sh1_p, sc1_p, g1_p, sh2_p, sc2_p, g2_p = modulation(cond_p, mod_w[i], mod_b[i])
        sh1_s, sc1_s, g1_s, sh2_s, sc2_s, g2_s = modulation(c, mod_w[i], mod_b[i])
        n_p = modulate(h_p, norm1_g[i], sh1_p, sc1_p)
        n_s = modulate(h_s, norm1_g[i], sh1_s, sc1_s)
        j = i // 2
        if i % 2 == 0:
            out_p = conv_module(n_p, conv_w_in[j], conv_b_in[j], conv_dw[j], conv_dw_b[j],
                                conv_norm_g[j], conv_w_out[j], conv_b_out[j])
            out_s = conv_module(n_s, conv_w_in[j], conv_b_in[j], conv_dw[j], conv_dw_b[j],
                                conv_norm_g[j], conv_w_out[j], conv_b_out[j])
        else:
            ckv_p, kpe_p = mla_latent(n_p, kv_a_w[j], kv_a_norm[j])
            new_ckv.append(ckv_p)
            new_kpe.append(kpe_p)
            k_p, v_p = mla_keys_values(ckv_p, kpe_p, kv_b_w[j], k_norm[j])
            q_p = mla_queries(n_p, q_a_w[j], q_a_norm[j], q_b_w[j], q_norm[j])
            out_p = blocked_attention(q_p, k_p, v_p) @ o_w[j]
            k_c, v_c = mla_keys_values(cache_ckv[:, j], cache_kpe[:, j], kv_b_w[j], k_norm[j])
            ckv_s, kpe_s = mla_latent(n_s, kv_a_w[j], kv_a_norm[j])
            k_s, v_s = mla_keys_values(ckv_s, kpe_s, kv_b_w[j], k_norm[j])
            q_s = mla_queries(n_s, q_a_w[j], q_a_norm[j], q_b_w[j], q_norm[j])
            q_s = rope_tail(q_s, cos_h, sin_h)
            k_s = rope_tail(k_s, cos_h, sin_h)
            out_s = blocked_attention(q_s, jnp.concatenate([k_c, k_s], axis=1),
                                      jnp.concatenate([v_c, v_s], axis=1)) @ o_w[j]
        h_p = h_p + g1_p * out_p
        h_s = h_s + g1_s * out_s
        n_p = modulate(h_p, norm2_g[i], sh2_p, sc2_p)
        n_s = modulate(h_s, norm2_g[i], sh2_s, sc2_s)
        h_p = h_p + g2_p * peer_ffn(n_p, peer_wq[i], peer_keys[i], peer_u[i], peer_v[i])
        h_s = h_s + g2_s * peer_ffn(n_s, peer_wq[i], peer_keys[i], peer_u[i], peer_v[i])
    new_ckv_arr = jnp.stack(new_ckv, axis=1)
    new_kpe_arr = jnp.stack(new_kpe, axis=1)
    return (h_p, h_s, new_ckv_arr, new_kpe_arr)


_drawn_inputs = setup_inputs


def setup_inputs(seed=0):
    import zlib

    import numpy as np

    out = dict(_drawn_inputs(seed))
    spreads = {}
    factors = {'cache_ckv': 5.632,
     'cache_kpe': 8.0,
     'norm1_g': 2.792,
     'norm2_g': 4.754,
     'conv_b_in': 7.918,
     'conv_dw_b': 5.492,
     'conv_norm_g': 7.784,
     'conv_b_out': 5.903,
     'q_a_norm': 8.0,
     'kv_a_norm': 2.891,
     'q_norm': 8.0,
     'k_norm': 8.0}
    for name, (base, spread) in spreads.items():
        noise = np.random.default_rng([zlib.crc32(name.encode()), seed]).standard_normal(out[name].shape)
        drawn = base * np.exp(spread * noise) if base else spread * noise
        out[name] = __import__('jax').numpy.asarray(drawn.astype(out[name].dtype))
    for name, factor in factors.items():
        out[name] = (out[name] * factor).astype(out[name].dtype)
    return out
```

```python
from contextlib import ExitStack

import concourse.bass as bass
from concourse import mybir

F32, BF16, I32, U32 = mybir.dt.float32, mybir.dt.bfloat16, mybir.dt.int32, mybir.dt.uint32
ALU = mybir.AluOpType
ACT = mybir.ActivationFunctionType
AX = mybir.AxisListType

P = 128
BANK = 512
HALF_BANK = BANK // 2
D = 1024
KD = D // P
SEQ, DEC_SEQ, PAST_LEN = 128, 512, 128
SAMPLE_TILES = DEC_SEQ // P
TILES = SAMPLE_TILES + SEQ // P
GRID_W, ROPE_THETA, DEPTH = 64, 10000.0, 2
CONV_K = 31
PAD = CONV_K // 2
HEADS, NOPE, ROPE, VH = 16, 64, 32, 64
QK = NOPE + ROPE
Q_LORA, KV_LORA = 512, 256
PEER_HEADS, PEER_QDIM, N_KEYS, TOPK = 8, 256, 128, 16
EPS = 1e-6
LOWEST = -3.4028234663852886e38
RING = 8
DIAGS = 4
MOD_BUFS = 4


def done(eng, ins):
    eng.drain()
    return ins


def clear_semaphores(nc, sems):
    with nc.Block() as block:
        @block.gpsimd
        def _(eng):
            for s in sems:
                eng.sem_clear(s)


def modulation_stage(nc, dram, layer, mod_rows):
    chunks = 6 * D // BANK
    w = dram["mod_w"][layer].rearrange("(p j) n -> p j n", j=KD)
    bias = dram["mod_b"][layer:layer + 1, :]
    with ExitStack() as ctx:
        def sb(name, shape, dt=F32):
            return ctx.enter_context(nc.sbuf_tensor(f"mod{layer}_{name}", shape, dt))

        sems = []

        def sem(name):
            sems.append(ctx.enter_context(nc.semaphore(f"m{layer}_{name}")))
            return sems[-1]

        cond = sb("cond", [P, 2, KD])
        silu = sb("silu", [P, 2, KD])
        w_sb = [sb(f"w{b}", [P, KD, BANK]) for b in range(MOD_BUFS)]
        bias_sb = [sb(f"bias{b}", [2, BANK]) for b in range(MOD_BUFS)]
        rows = [sb(f"rows{b}", [2, BANK]) for b in range(MOD_BUFS)]
        ps = [ctx.enter_context(nc.psum_tensor(f"mod{layer}_ps{b}", [P, BANK], F32)) for b in range(MOD_BUFS)]
        cond_in, silu_done = sem("cond_in"), sem("silu")
        w_in = [sem(f"w_in{b}") for b in range(MOD_BUFS)]
        w_free, mm_done, row_done = sem("w_free"), sem("mm"), sem("row")
        stored = [sem(f"st{b}") for b in range(MOD_BUFS)]
        ctx.callback(clear_semaphores, nc, sems)
        block = ctx.enter_context(nc.Block())

        @block.sync
        def _(eng):
            eng.dma_start(cond[:, 0, :], dram["c"].rearrange("a (p j) -> (a p) j", j=KD)).then_inc(cond_in, 16)
            eng.dma_start(cond[:, 1, :], dram["c_ctx"].rearrange("(p j) -> p j", j=KD)).then_inc(cond_in, 16)

            def load(c, b):
                eng.dma_start(w_sb[b][:, :, :], w[:, :, bass.ds(c * BANK, BANK)]).then_inc(w_in[b], 16)
                eng.dma_start(bias_sb[b][:, :], bias[:, bass.ds(c * BANK, BANK)].broadcast_to([2, BANK])).then_inc(w_in[b], 16)

            for b in range(MOD_BUFS):
                load(b, b)
            with eng.Fori(1, chunks // MOD_BUFS) as i:
                for b in range(MOD_BUFS):
                    eng.wait_ge(row_done, i * MOD_BUFS - MOD_BUFS + b + 1)
                    load(i * MOD_BUFS + b, b)

        @block.scalar
        def _(eng):
            eng.wait_ge(cond_in, 32)
            eng.activation(silu[:, :, :], cond[:, :, :], ACT.Silu).then_inc(silu_done, 1)
            with eng.Fori(0, chunks // MOD_BUFS) as i:
                for b in range(MOD_BUFS):
                    c = i * MOD_BUFS + b
                    eng.wait_ge(row_done, c + 1)
                    eng.dma_start(mod_rows[layer, :, bass.ds(c * BANK, BANK)], rows[b][:, :]).then_inc(stored[b], 16)
            for b in range(MOD_BUFS):
                eng.wait_ge(stored[b], 16 * (chunks // MOD_BUFS))

        @block.tensor
        def _(eng):
            eng.wait_ge(silu_done, 1)
            with eng.Fori(0, chunks // MOD_BUFS) as i:
                for b in range(MOD_BUFS):
                    eng.wait_ge(w_in[b], 32 * i + 32)
                    for j in range(KD):
                        last = eng.matmul(ps[b][0:2, :], silu[:, :, j], w_sb[b][:, j, :], start=(j == 0), stop=(j == KD - 1))
                    last.then_inc(mm_done, 1)

        @block.vector
        def _(eng):
            def add_bias(c, b):
                eng.wait_ge(mm_done, c + 1)
                eng.tensor_tensor(rows[b][:, :], ps[b][0:2, :], bias_sb[b][:, :], ALU.add).then_inc(row_done, 1)

            for b in range(MOD_BUFS):
                add_bias(b, b)
            with eng.Fori(1, chunks // MOD_BUFS) as i:
                for b in range(MOD_BUFS):
                    eng.wait_ge(stored[b], 16 * i)
                    add_bias(i * MOD_BUFS + b, b)


def conv_stage(nc, dram, layer, j, h, ident, mod_rows):
    w_in_d = dram["conv_w_in"][j].rearrange("(k p) n -> p k n", p=P)
    w_out_d = dram["conv_w_out"][j].rearrange("(k p) n -> p k n", p=P)
    T = TILES * P
    PROMPT_AT = DEC_SEQ + PAD
    OUT_LEN = PROMPT_AT + SEQ
    IN_LEN = OUT_LEN + 2 * PAD
    SEGMENTS = ((0, DEC_SEQ, 0), (DEC_SEQ, SEQ, PROMPT_AT))
    with ExitStack() as ctx:
        def sb(name, shape, dt=F32):
            return ctx.enter_context(nc.sbuf_tensor(f"conv_{name}", shape, dt))

        sems = []

        def sem(name):
            sems.append(ctx.enter_context(nc.semaphore(f"c_{name}")))
            return sems[-1]

        xT = sb("xT", [P, KD, T])
        x = [sb(f"x{b}", [P, D]) for b in range(2)]
        w_ag = [sb(f"w_ag{b}", [P, 2, KD, P]) for b in range(2)]
        w_out = sb("w_out", [P, KD, D])
        sig = [sb(f"sig{b}", [P, T]) for b in range(2)]
        glu = [sb(f"glu{b}", [P, IN_LEN]) for b in range(2)]
        mixed = sb("mixed", [P, KD, OUT_LEN])
        square = [sb(f"square{b}", [P, OUT_LEN]) for b in range(2)]
        rstd = sb("rstd", [P, 2, T])
        ones = sb("ones", [P, P])
        rows = sb("rows", [32, P])
        cols = sb("cols", [P, 32])
        taps_rows = sb("taps_rows", [CONV_K, D])
        taps = sb("taps", [P, KD, CONV_K])
        rms = sb("rms", [P, TILES, 4])
        gain = [sb(f"gain{g}", [P, D]) for g in range(2)]
        shift = [sb(f"shift{g}", [P, D]) for g in range(2)]
        gate = [sb(f"gate{g}", [P, D]) for g in range(2)]
        norm_g = sb("norm_g", [P, D])
        b_out = sb("b_out", [P, D])
        B_A, DW_B, NORM_G = 0, 16, 24

        psum = [ctx.enter_context(nc.psum_tensor(f"conv_ps{b}", [P, 2 * BANK], F32)) for b in range(4)]
        a_ps, g_ps = (psum[0], psum[1]), (psum[2], psum[3])
        small_ps = psum[3]

        vec_in, small_in, w_out_in = sem("vec_in"), sem("small_in"), sem("w_out_in")
        w_in = [sem(f"w_in{b}") for b in range(2)]
        gains_made, ones_made, pads_made = sem("gains"), sem("ones"), sem("pads")
        small_tr, small_ev = sem("small_tr"), sem("small_ev")
        ssq_done, std_done, rms_done, x_ready, xT_tr, xT_ready = (sem(n) for n in ("ssq", "std", "rms", "x_ready", "xT_tr", "xT_ready"))
        ag_mm, sig_done, glu_done, conv_done = (sem(n) for n in ("ag_mm", "sig", "glu", "conv"))
        sq_done, sq_used, var_done, csd_done, rstd_done = (sem(n) for n in ("sq", "sq_used", "var", "csd", "rstd"))
        scaled, swish_done, out_mm, out_used = (sem(n) for n in ("scaled", "swish", "out_mm", "out_used"))

        ctx.callback(clear_semaphores, nc, sems)
        block = ctx.enter_context(nc.Block())

        def group_of(tile):
            return 1 if tile == TILES - 1 else 0

        @block.sync
        def _(eng):
            eng.dma_start(norm_g[:, :], dram["norm1_g"][layer:layer + 1, :].broadcast_to([P, D])).then_inc(vec_in, 16)
            for g in range(2):
                for dst, part in ((shift, 0), (gain, 1), (gate, 2)):
                    eng.dma_start(dst[g][:, :], mod_rows[layer, g:g + 1, part * D:(part + 1) * D].broadcast_to([P, D])).then_inc(vec_in, 16)
            eng.dma_start(rows[0:16, :], dram["conv_b_in"][j].rearrange("(r p) -> r p", p=P)).then_inc(small_in, 16)
            eng.dma_start(rows[16:24, :], dram["conv_dw_b"][j].rearrange("(r p) -> r p", p=P)).then_inc(small_in, 16)
            eng.dma_start(rows[24:32, :], dram["conv_norm_g"][j].rearrange("(r p) -> r p", p=P)).then_inc(small_in, 16)
            eng.dma_start(taps_rows[:, :], dram["conv_dw"][j]).then_inc(small_in, 16)

            def load(c, b):
                for half in range(2):
                    eng.dma_start(w_ag[b][:, half, :, :], w_in_d[:, :, bass.ds(half * D + c * P, P)]).then_inc(w_in[b], 16)

            load(0, 0)
            load(1, 1)
            eng.dma_start(b_out[:, :], dram["conv_b_out"][j:j + 1, :].broadcast_to([P, D])).then_inc(w_out_in, 16)
            for k in range(KD):
                eng.dma_start(w_out[:, k, :], w_out_d[:, k, :]).then_inc(w_out_in, 16)
            with eng.Fori(1, KD // 2) as i:
                for b in range(2):
                    eng.wait_ge(ag_mm, 2 * i + b - 1)
                    load(2 * i + b, b)

        @block.gpsimd
        def _(eng):
            eng.memset(ones[:, :], 1.0).then_inc(ones_made, 1)
            for b in range(2):
                for at in (0, PAD + DEC_SEQ, IN_LEN - PAD):
                    eng.memset(glu[b][:, at:at + PAD], 0.0).then_inc(pads_made, 1)
            eng.sem_inc(glu_done, 2)

        @block.vector
        def _(eng):
            eng.wait_ge(vec_in, 16 * 7)
            for g in range(2):
                eng.scalar_tensor_tensor(out=gain[g][:, :], in0=gain[g][:, :], scalar=1.0, in1=norm_g[:, :], op0=ALU.add, op1=ALU.mult)
            eng.drain()
            for tile in range(TILES):
                xb, g = x[tile % 2][:, :], group_of(tile)
                eng.wait_ge(ssq_done, tile + 1)
                eng.tensor_scalar(rms[:, tile, 1:2], rms[:, tile, 0:1], 1.0 / D, EPS, ALU.mult, ALU.add).then_inc(rms_done, 1)
                eng.wait_ge(std_done, tile + 1)
                done(eng, eng.reciprocal(rms[:, tile, 3:4], rms[:, tile, 2:3]))
                if tile >= 2:
                    eng.wait_ge(xT_tr, 2 * (tile - 1))
                done(eng, eng.scalar_tensor_tensor(out=xb, in0=h[:, tile, :], scalar=rms[:, tile, 3:4], in1=gain[g][:, :], op0=ALU.mult, op1=ALU.mult))
                eng.tensor_tensor(xb, xb, shift[g][:, :], ALU.add).then_inc(x_ready, 1)

            eng.wait_ge(pads_made, 6)
            eng.wait_ge(small_ev, 2)
            with eng.Fori(0, KD // 2) as i:
                for b in range(2):
                    c = 2 * i + b
                    eng.wait_ge(sig_done, c + 1)
                    for start, n, at in SEGMENTS:
                        last = eng.scalar_tensor_tensor(out=glu[b][:, PAD + at:PAD + at + n], in0=a_ps[b][:, start:start + n],
                                                        scalar=cols[:, bass.ds(c + B_A, 1)], in1=sig[b][:, start:start + n],
                                                        op0=ALU.add, op1=ALU.mult)
                    last.then_inc(glu_done, 1)
                    eng.drain()
                    out = mixed[:, bass.ds(c, 1), :].rearrange("p a n -> p (a n)")
                    tap = taps[:, bass.ds(c, 1), :].rearrange("p a k -> p (a k)")
                    done(eng, eng.tensor_scalar(out, glu[b][:, 0:OUT_LEN], tap[:, 0:1], cols[:, bass.ds(c + DW_B, 1)], ALU.mult, ALU.add))
                    for k in range(1, CONV_K):
                        last = done(eng, eng.scalar_tensor_tensor(out=out, in0=glu[b][:, k:k + OUT_LEN], scalar=tap[:, k:k + 1], in1=out,
                                                                  op0=ALU.mult, op1=ALU.add))
                    last.then_inc(conv_done, 1)

            eng.wait_ge(sq_used, KD)
            eng.tensor_scalar(rstd[:, 0, :], psum[2][:, 0:T], 1.0 / D, EPS, ALU.mult, ALU.add).then_inc(var_done, 1)
            eng.wait_ge(csd_done, 1)
            done(eng, eng.reciprocal(rstd[:, 0, :], rstd[:, 1, :]))
            for c in range(KD):
                for start, n, at in SEGMENTS:
                    last = eng.tensor_tensor(mixed[:, c, at:at + n], mixed[:, c, at:at + n], rstd[:, 0, start:start + n], ALU.mult)
                last.then_inc(scaled, 1)

            eng.wait_ge(w_out_in, 16 * (KD + 1))
            for tile in range(TILES):
                g, tmp = group_of(tile), x[tile % 2][:, :]
                eng.wait_ge(out_mm, tile + 1)
                eng.tensor_tensor(tmp, psum[tile % 2][:, :], b_out[:, :], ALU.add).then_inc(out_used, 1)
                eng.drain()
                done(eng, eng.tensor_tensor(tmp, tmp, gate[g][:, :], ALU.mult))
                eng.tensor_tensor(h[:, tile, :], h[:, tile, :], tmp, ALU.add)

        @block.scalar
        def _(eng):
            for tile in range(TILES):
                if tile >= 2:
                    eng.wait_ge(xT_tr, 2 * (tile - 1))
                eng.activation(x[tile % 2][:, :], h[:, tile, :], ACT.Square, accum_out=rms[:, tile, 0:1]).then_inc(ssq_done, 1)
                eng.wait_ge(rms_done, tile + 1)
                eng.activation(rms[:, tile, 2:3], rms[:, tile, 1:2], ACT.Sqrt).then_inc(std_done, 1)
                for half in range(2):
                    eng.wait_ge(xT_tr, 2 * tile + half + 1)
                    eng.activation(xT[:, 4 * half:4 * half + 4, tile * P:(tile + 1) * P],
                                   psum[half][:, 0:BANK].rearrange("p (k t) -> p k t", k=4), ACT.Copy).then_inc(xT_ready, 1)
                if tile == 0:
                    eng.wait_ge(small_tr, 1)
                    eng.activation(cols[:, :], small_ps[:, 0:32], ACT.Copy).then_inc(small_ev, 1)
                    eng.activation(taps[:, :, :], small_ps[:, BANK:BANK + KD * 32].rearrange("p (c k) -> p c k", c=KD)[:, :, 0:CONV_K], ACT.Copy).then_inc(small_ev, 1)
            eng.drain()
            with eng.Fori(0, KD // 2) as i:
                for b in range(2):
                    c = 2 * i + b
                    eng.wait_ge(ag_mm, c + 1)
                    eng.wait_ge(glu_done, c + 1)
                    eng.activation(sig[b][:, :], g_ps[b][:, 0:T], ACT.Sigmoid, bias=cols[:, bass.ds(c + B_A + KD, 1)]).then_inc(sig_done, 1)
            for c in range(KD):
                eng.wait_ge(conv_done, c + 1)
                if c >= 2:
                    eng.wait_ge(sq_used, c - 1)
                eng.activation(square[c % 2][:, :], mixed[:, c, :], ACT.Square).then_inc(sq_done, 1)
            eng.wait_ge(var_done, 1)
            eng.activation(rstd[:, 1, :], rstd[:, 0, :], ACT.Sqrt).then_inc(csd_done, 1)
            for c in range(KD):
                eng.wait_ge(scaled, c + 1)
                for start, n, at in SEGMENTS:
                    last = eng.activation(xT[:, c, start:start + n], mixed[:, c, at:at + n], ACT.Silu, scale=cols[:, NORM_G + c:NORM_G + c + 1])
                last.then_inc(swish_done, 1)

        @block.tensor
        def _(eng):
            for tile in range(TILES):
                eng.wait_ge(x_ready, tile + 1)
                for half in range(2):
                    if tile:
                        eng.wait_ge(xT_ready, 2 * tile - 1 + half)
                    for k in range(4):
                        last = eng.transpose(psum[half][:, k * P:(k + 1) * P], x[tile % 2][:, (4 * half + k) * P:(4 * half + k + 1) * P], ident[:, :])
                    last.then_inc(xT_tr, 1)
                if tile == 0:
                    eng.wait_ge(small_in, 64)
                    eng.transpose(small_ps[:, 0:32], rows[:, :], ident[0:32, 0:32])
                    for c in range(KD):
                        last = eng.transpose(small_ps[:, BANK + c * 32:BANK + c * 32 + CONV_K], taps_rows[:, c * P:(c + 1) * P], ident[0:CONV_K, 0:CONV_K])
                    last.then_inc(small_tr, 1)
            eng.wait_ge(xT_ready, 2 * TILES)
            eng.wait_ge(small_ev, 2)
            with eng.Fori(0, KD // 2) as i:
                for b in range(2):
                    c = 2 * i + b
                    eng.wait_ge(w_in[b], 32 * i + 32)
                    eng.wait_ge(glu_done, c + 1)
                    for half, ps in ((0, a_ps[b]), (1, g_ps[b])):
                        for start, n, _ in SEGMENTS:
                            for k in range(KD):
                                last = eng.matmul(ps[:, start:start + n], w_ag[b][:, half, k, :], xT[:, k, start:start + n],
                                                  start=(k == 0), stop=(k == KD - 1))
                    last.then_inc(ag_mm, 1)
            eng.wait_ge(ones_made, 1)
            for c in range(KD):
                eng.wait_ge(sq_done, c + 1)
                for start, n, at in SEGMENTS:
                    last = eng.matmul(psum[2][:, start:start + n], ones[:, :], square[c % 2][:, at:at + n], start=(c == 0), stop=(c == KD - 1))
                last.then_inc(sq_used, 1)
            eng.wait_ge(swish_done, KD)
            eng.wait_ge(w_out_in, 16 * (KD + 1))
            for tile in range(TILES):
                if tile >= 2:
                    eng.wait_ge(out_used, tile - 1)
                for half in range(2):
                    for k in range(KD):
                        last = eng.matmul(psum[tile % 2][:, half * BANK:(half + 1) * BANK], xT[:, k, tile * P:(tile + 1) * P],
                                          w_out[:, k, half * BANK:(half + 1) * BANK], start=(k == 0), stop=(k == KD - 1))
                last.then_inc(out_mm, 1)


def attention_stage(nc, dram, layer, j, h, ident, mod_rows, ckv_out, kpe_out):
    HALVES, HH = 2, HEADS // 2
    CACHE_KT, PROMPT_KT = SAMPLE_TILES, SAMPLE_TILES + 1
    KEY_TILES = SAMPLE_TILES + 2
    KV_W = NOPE + VH
    SCALE = float(QK) ** -0.5
    KQ, KL = Q_LORA // P, KV_LORA // P

    def group_of(tile):
        return 1 if tile == TILES - 1 else 0

    def key_tile(tile):
        return PROMPT_KT if tile == TILES - 1 else tile

    def keys_of(tile):
        return (PROMPT_KT * P, P) if tile == TILES - 1 else (0, (SAMPLE_TILES + 1) * P)

    with ExitStack() as ctx:
        def sb(name, shape, dt=F32):
            return ctx.enter_context(nc.sbuf_tensor(f"attn_{name}", shape, dt))

        sems = []

        def sem(name):
            sems.append(ctx.enter_context(nc.semaphore(f"a_{name}")))
            return sems[-1]

        gain = [sb(f"gain{g}", [P, D]) for g in range(2)]
        shift = [sb(f"shift{g}", [P, D]) for g in range(2)]
        gate = [sb(f"gate{g}", [P, D]) for g in range(2)]
        x = sb("x", [P, D])
        xT = sb("xT", [P, KD, P])
        lat_w = sb("lat_w", [P, KD * (Q_LORA + KV_LORA + ROPE)])
        q_a = lat_w[:, 0:KD * Q_LORA].rearrange("p (k n) -> p k n", k=KD)
        kv_a = lat_w[:, KD * Q_LORA:].rearrange("p (k n) -> p k n", k=KD)
        out_heads = lat_w[:, 0:TILES * HEADS * VH].rearrange("p (t n) -> p t n", t=TILES)
        q_b = sb("q_b", [P, KQ, HH * QK])
        kv_b = sb("kv_b", [P, KL, HH * KV_W])
        o_w = sb("o_w", [P, KD, BANK])
        q_a_norm = sb("q_a_norm", [P, Q_LORA])
        kv_a_norm = sb("kv_a_norm", [P, KV_LORA])
        qk_gain = sb("qk_gain", [P, 2, QK])
        cos = sb("cos", [P, SAMPLE_TILES, ROPE // 2])
        sin = sb("sin", [P, SAMPLE_TILES, ROPE // 2])
        rms = sb("rms", [P, TILES, 12])
        lat_q = sb("lat_q", [P, Q_LORA])
        lat_kv = sb("lat_kv", [P, KV_LORA])
        cache_kv = sb("cache_kv", [P, KV_LORA])
        latT_q = sb("latT_q", [P, TILES, KQ, P])
        latT_kv = sb("latT_kv", [P, KEY_TILES, KL, P])
        kpe = sb("kpe", [P, KEY_TILES, ROPE])
        heads_sb = sb("heads", [P, HH, QK])
        heads_sq = sb("heads_sq", [P, HH, QK])
        head_ms = sb("head_ms", [P, 3, HH])
        rope_tmp = sb("rope_tmp", [P, 4, HH, ROPE // 2])
        kT = sb("kT", [QK, HH, KEY_TILES * P])
        qT = sb("qT", [QK, HH, P])
        v = sb("v", [P, KEY_TILES, HH, VH])
        probs = [sb(f"probs{b}", [P, 5 * P]) for b in range(2)]
        probsT = [sb(f"probsT{b}", [P, 5, P]) for b in range(2)]
        neg_max = [sb(f"neg_max{b}", [P, 2]) for b in range(2)]
        sums = sb("sums", [P, 2, HH])
        outT = xT

        s_ps = [ctx.enter_context(nc.psum_tensor(f"attn_s{b}", [P, 2 * BANK], F32)) for b in range(2)]
        pT_ps = ctx.enter_context(nc.psum_tensor("attn_pT", [P, 2 * BANK], F32))
        o_ps = ctx.enter_context(nc.psum_tensor("attn_o", [P, BANK], F32))
        spare_ps = ctx.enter_context(nc.psum_tensor("attn_spare", [P, BANK], F32))

        vec_in, lat_w_in, small_in, cache_in, ow_in = (sem(n) for n in ("vec_in", "lat_w", "small_in", "cache_in", "ow_in"))
        half_w_in, half_w_used = sem("half_w"), sem("half_w_used")
        ssq_done, std_done, rms_done, x_ready, xT_tr, xT_ready = (sem(n) for n in ("ssq", "std", "rms", "x_ready", "xT_tr", "xT_ready"))
        lat_mm, lat_sq, lat_ms, lat_std, lat_ready, lat_tr, lat_ev = (sem(n) for n in ("lat_mm", "lat_sq", "lat_ms", "lat_std", "lat_ready", "lat_tr", "lat_ev"))
        new_stored, gains_made = sem("new_stored"), sem("gains")
        hd_mm, hd_copied, hd_sq, hd_ms, hd_std, hd_ready, hd_tr, hd_ev = (sem(n) for n in ("hd_mm", "hd_cp", "hd_sq", "hd_ms", "hd_std", "hd_ready", "hd_tr", "hd_ev"))
        s_mm, max_done, exp_done, p_tr, p_ev, pv_mm, o_used = (sem(n) for n in ("s_mm", "max", "exp", "p_tr", "p_ev", "pv", "o_used"))
        oT_tr, oT_ev, out_mm, out_used = (sem(n) for n in ("oT_tr", "oT_ev", "out_mm", "out_used"))

        ctx.callback(clear_semaphores, nc, sems)
        block = ctx.enter_context(nc.Block())
        STEPS = KEY_TILES + TILES

        @block.sync
        def _(eng):
            eng.dma_start(x[:, :], dram["norm1_g"][layer:layer + 1, :].broadcast_to([P, D])).then_inc(vec_in, 16)
            for g in range(2):
                for dst, part in ((shift, 0), (gain, 1), (gate, 2)):
                    eng.dma_start(dst[g][:, :], mod_rows[layer, g:g + 1, part * D:(part + 1) * D].broadcast_to([P, D])).then_inc(vec_in, 16)
            eng.dma_start(q_a[:, :, :], dram["q_a_w"][j].rearrange("(k p) n -> p k n", p=P)).then_inc(lat_w_in, 16)
            eng.dma_start(kv_a[:, :, :], dram["kv_a_w"][j].rearrange("(k p) n -> p k n", p=P)).then_inc(lat_w_in, 16)
            eng.dma_start(q_a_norm[:, :], dram["q_a_norm"][j:j + 1, :].broadcast_to([P, Q_LORA])).then_inc(small_in, 16)
            eng.dma_start(kv_a_norm[:, :], dram["kv_a_norm"][j:j + 1, :].broadcast_to([P, KV_LORA])).then_inc(small_in, 16)
            eng.dma_start(qk_gain[:, 0, :], dram["q_norm"][j:j + 1, :].broadcast_to([P, QK])).then_inc(small_in, 16)
            eng.dma_start(qk_gain[:, 1, :], dram["k_norm"][j:j + 1, :].broadcast_to([P, QK])).then_inc(small_in, 16)
            eng.dma_start(cos[:, :, :], dram["rope_cos"].rearrange("(t p) f -> p t f", p=P)).then_inc(small_in, 16)
            eng.dma_start(sin[:, :, :], dram["rope_sin"].rearrange("(t p) f -> p t f", p=P)).then_inc(small_in, 16)
            eng.dma_start(cache_kv[:, :], dram["cache_ckv"][0, j]).then_inc(cache_in, 16)
            eng.dma_start(kpe[:, CACHE_KT, :], dram["cache_kpe"][0, j]).then_inc(cache_in, 16)

            def load_half(hh):
                eng.dma_start(q_b[:, :, :], dram["q_b_w"][j].rearrange("(k p) n -> p k n", p=P)[:, :, bass.ds(hh * (HH * QK), HH * QK)]).then_inc(half_w_in, 16)
                eng.dma_start(kv_b[:, :, :], dram["kv_b_w"][j].rearrange("(k p) n -> p k n", p=P)[:, :, bass.ds(hh * (HH * KV_W), HH * KV_W)]).then_inc(half_w_in, 16)

            load_half(0)
            eng.dma_start(o_w[:, :, :], dram["o_w"][j].rearrange("(k p) n -> p k n", p=P)[:, :, 0:BANK]).then_inc(ow_in, 16)
            eng.wait_ge(lat_ready, TILES)
            eng.dma_start(ckv_out, lat_kv[:, :]).then_inc(new_stored, 16)
            eng.dma_start(kpe_out, kpe[:, PROMPT_KT, :]).then_inc(new_stored, 16)
            eng.wait_ge(half_w_used, 1)
            load_half(1)
            eng.wait_ge(out_mm, TILES)
            eng.dma_start(o_w[:, :, :], dram["o_w"][j].rearrange("(k p) n -> p k n", p=P)[:, :, BANK:D]).then_inc(ow_in, 16)
            eng.wait_ge(new_stored, 32)

        @block.tensor
        def _(eng):
            eng.wait_ge(lat_w_in, 32)
            eng.wait_ge(cache_in, 32)
            for tile in range(TILES):
                eng.wait_ge(x_ready, tile + 1)
                if tile:
                    eng.wait_ge(xT_ready, 2 * tile)
                for half in range(2):
                    for k in range(4 * half, 4 * half + 4):
                        last = eng.transpose(s_ps[0][:, k * P:(k + 1) * P], x[:, k * P:(k + 1) * P], ident[:, :])
                    last.then_inc(xT_tr, 1)
                eng.wait_ge(xT_ready, 2 * tile + 2)
                if tile:
                    eng.wait_ge(lat_ready, tile)
                for k in range(KD):
                    eng.matmul(s_ps[1][:, 0:Q_LORA], xT[:, k, :], q_a[:, k, :], start=(k == 0), stop=(k == KD - 1))
                for k in range(KD):
                    last = eng.matmul(s_ps[1][:, BANK:BANK + KV_LORA + ROPE], xT[:, k, :], kv_a[:, k, :], start=(k == 0), stop=(k == KD - 1))
                last.then_inc(lat_mm, 1)
                eng.wait_ge(lat_ready, tile + 1)
                if tile:
                    eng.wait_ge(lat_ev, 2 * tile)
                for k in range(KQ):
                    eng.transpose(pT_ps[:, k * P:(k + 1) * P], lat_q[:, k * P:(k + 1) * P], ident[:, :])
                for k in range(KL):
                    last = eng.transpose(pT_ps[:, BANK + k * P:BANK + (k + 1) * P], lat_kv[:, k * P:(k + 1) * P], ident[:, :])
                last.then_inc(lat_tr, 1)
            eng.wait_ge(lat_ev, 2 * TILES)
            for k in range(KL):
                last = eng.transpose(pT_ps[:, BANK + k * P:BANK + (k + 1) * P], cache_kv[:, k * P:(k + 1) * P], ident[:, :])
            last.then_inc(lat_tr, 1)
            eng.wait_ge(lat_ev, 2 * TILES + 1)

            with eng.Fori(0, HALVES) as hh:
                def transpose_heads(step):
                    eng.wait_ge(hd_ready, step + 1)
                    for n in range(HH):
                        last = eng.transpose(s_ps[1][0:QK, n * P:(n + 1) * P], heads_sb[:, n, :], ident[:, :])
                    last.then_inc(hd_tr, 1)
                    eng.wait_ge(hd_ev, step + 1)

                eng.wait_ge(half_w_in, 32 * hh + 32)
                for kt in range(KEY_TILES):
                    step = hh * STEPS + kt
                    for c in range(2):
                        for k in range(KL):
                            last = eng.matmul(s_ps[0][:, c * BANK:(c + 1) * BANK], latT_kv[:, kt, k, :], kv_b[:, k, c * BANK:(c + 1) * BANK],
                                              start=(k == 0), stop=(k == KL - 1))
                    last.then_inc(hd_mm, 1)
                    transpose_heads(step)

                for tile in range(TILES):
                    step = hh * STEPS + KEY_TILES + tile
                    for c in range(2):
                        for k in range(KQ):
                            last = eng.matmul(s_ps[0][:, c * BANK:c * BANK + HH * QK // 2], latT_q[:, tile, k, :],
                                              q_b[:, k, c * (HH * QK // 2):(c + 1) * (HH * QK // 2)], start=(k == 0), stop=(k == KQ - 1))
                    last.then_inc(hd_mm, 1)
                    transpose_heads(step)
                    first_key, n_keys = keys_of(tile)
                    at = (hh * TILES + tile) * HH

                    def scores(n):
                        if n >= 2:
                            eng.wait_ge(exp_done, at + n - 1)
                        for c in range(0, n_keys, BANK):
                            m = min(BANK, n_keys - c)
                            last = eng.matmul(s_ps[n % 2][:, c:c + m], qT[:, n, :], kT[:, n, first_key + c:first_key + c + m], start=True, stop=True)
                        last.then_inc(s_mm, 1)

                    def transpose_probs(n):
                        eng.wait_ge(exp_done, at + n + 1)
                        if n:
                            eng.wait_ge(p_ev, at + n)
                        for c in range(n_keys // P):
                            last = eng.transpose(pT_ps[:, c * P:(c + 1) * P], probs[n % 2][:, c * P:(c + 1) * P], ident[:, :])
                        last.then_inc(p_tr, 1)

                    def weigh_values(n):
                        eng.wait_ge(p_ev, at + n + 1)
                        for c in range(n_keys // P):
                            last = eng.matmul(o_ps[:, n * VH:(n + 1) * VH], probsT[n % 2][:, c, :], v[:, first_key // P + c, n, :],
                                              start=(c == 0), stop=(c == n_keys // P - 1))
                        last.then_inc(pv_mm, 1)

                    scores(0)
                    for n in range(HH):
                        if n + 1 < HH:
                            scores(n + 1)
                        transpose_probs(n)
                        if n:
                            weigh_values(n - 1)
                    weigh_values(HH - 1)
                    eng.wait_ge(o_used, hh * TILES + tile + 1)
                eng.nop().then_inc(half_w_used, 1)

            for c in range(2):
                eng.wait_ge(ow_in, 16 * (c + 1))
                for tile in range(TILES):
                    n = c * TILES + tile
                    if n:
                        eng.wait_ge(oT_ev, 2 * n)
                    for half in range(2):
                        for k in range(4 * half, 4 * half + 4):
                            last = eng.transpose(s_ps[0][:, k * P:(k + 1) * P], out_heads[:, tile, k * P:(k + 1) * P], ident[:, :])
                        last.then_inc(oT_tr, 1)
                    eng.wait_ge(oT_ev, 2 * n + 2)
                    if n >= 2:
                        eng.wait_ge(out_used, n - 1)
                    for k in range(KD):
                        last = eng.matmul(s_ps[1][:, (n % 2) * BANK:(n % 2 + 1) * BANK], outT[:, k, :], o_w[:, k, :], start=(k == 0), stop=(k == KD - 1))
                    last.then_inc(out_mm, 1)

        @block.scalar
        def _(eng):
            for tile in range(TILES):
                if tile:
                    eng.wait_ge(xT_tr, 2 * tile)
                else:
                    eng.wait_ge(gains_made, 1)
                eng.activation(x[:, :], h[:, tile, :], ACT.Square, accum_out=rms[:, tile, 0:1]).then_inc(ssq_done, 1)
                eng.wait_ge(rms_done, tile + 1)
                eng.activation(rms[:, tile, 2:3], rms[:, tile, 1:2], ACT.Sqrt).then_inc(std_done, 1)
                for half in range(2):
                    eng.wait_ge(xT_tr, 2 * tile + half + 1)
                    if tile:
                        eng.wait_ge(lat_mm, tile)
                    eng.activation(xT[:, 4 * half:4 * half + 4, :].rearrange("p k t -> p (k t)"),
                                   s_ps[0][:, half * BANK:(half + 1) * BANK], ACT.Copy).then_inc(xT_ready, 1)
                eng.wait_ge(lat_mm, tile + 1)
                if tile:
                    eng.wait_ge(lat_tr, tile)
                eng.activation(lat_q[:, :], s_ps[1][:, 0:Q_LORA], ACT.Square, accum_out=rms[:, tile, 4:5]).then_inc(lat_sq, 1)
                eng.activation(lat_kv[:, :], s_ps[1][:, BANK:BANK + KV_LORA], ACT.Square, accum_out=rms[:, tile, 5:6]).then_inc(lat_sq, 1)
                eng.wait_ge(lat_ms, tile + 1)
                eng.activation(rms[:, tile, 8:10], rms[:, tile, 6:8], ACT.Sqrt).then_inc(lat_std, 1)
                eng.wait_ge(lat_tr, tile + 1)
                eng.activation(latT_q[:, tile, :, :].rearrange("p k t -> p (k t)"), pT_ps[:, 0:Q_LORA], ACT.Copy).then_inc(lat_ev, 1)
                eng.activation(latT_kv[:, key_tile(tile), :, :].rearrange("p k t -> p (k t)"), pT_ps[:, BANK:BANK + KV_LORA], ACT.Copy).then_inc(lat_ev, 1)
            eng.wait_ge(lat_tr, TILES + 1)
            eng.activation(latT_kv[:, CACHE_KT, :, :].rearrange("p k t -> p (k t)"), pT_ps[:, BANK:BANK + KV_LORA], ACT.Copy).then_inc(lat_ev, 1)

            with eng.Fori(0, HALVES) as hh:
                for s in range(STEPS):
                    step = hh * STEPS + s
                    is_key = s < KEY_TILES
                    eng.wait_ge(hd_copied, step + 1)
                    if is_key:
                        eng.activation(v[:, s, :, :], s_ps[0][:, :].rearrange("p (n w) -> p n w", n=HH)[:, :, NOPE:KV_W], ACT.Copy)
                    eng.activation(heads_sq[:, :, :], heads_sb[:, :, :], ACT.Square).then_inc(hd_sq, 1)
                    eng.wait_ge(hd_ms, step + 1)
                    eng.activation(head_ms[:, 2, :], head_ms[:, 1, :], ACT.Sqrt).then_inc(hd_std, 1)
                    eng.wait_ge(hd_tr, step + 1)
                    source = s_ps[1][0:QK, :].rearrange("p (n t) -> p n t", n=HH)
                    target = kT[:, :, s * P:(s + 1) * P] if is_key else qT[:, :, :]
                    eng.activation(target, source, ACT.Copy).then_inc(hd_ev, 1)
                    if is_key:
                        continue
                    tile = s - KEY_TILES
                    _, n_keys = keys_of(tile)
                    at = (hh * TILES + tile) * HH

                    def exponentials(n):
                        eng.wait_ge(max_done, at + n + 1)
                        if n >= 2:
                            eng.wait_ge(p_tr, at + n - 1)
                        eng.activation(probs[n % 2][:, 0:n_keys], s_ps[n % 2][:, 0:n_keys], ACT.Exp, bias=neg_max[n % 2][:, 1:2],
                                       scale=SCALE, accum_out=sums[:, 0, n:n + 1]).then_inc(exp_done, 1)

                    def copy_probs(n):
                        eng.wait_ge(p_tr, at + n + 1)
                        if n >= 2:
                            eng.wait_ge(pv_mm, at + n - 1)
                        eng.activation(probsT[n % 2][:, 0:n_keys // P, :].rearrange("p c t -> p (c t)"), pT_ps[:, 0:n_keys], ACT.Copy).then_inc(p_ev, 1)

                    exponentials(0)
                    for n in range(HH):
                        if n + 1 < HH:
                            exponentials(n + 1)
                        copy_probs(n)

            for n in range(2 * TILES):
                for half in range(2):
                    eng.wait_ge(oT_tr, 2 * n + half + 1)
                    if n:
                        eng.wait_ge(out_mm, n)
                    eng.activation(outT[:, 4 * half:4 * half + 4, :].rearrange("p k t -> p (k t)"),
                                   s_ps[0][:, half * BANK:(half + 1) * BANK], ACT.Copy).then_inc(oT_ev, 1)

        @block.vector
        def _(eng):
            eng.wait_ge(vec_in, 16 * 7)
            eng.wait_ge(small_in, 16 * 6)
            for g in range(2):
                last = eng.scalar_tensor_tensor(out=gain[g][:, :], in0=gain[g][:, :], scalar=1.0, in1=x[:, :], op0=ALU.add, op1=ALU.mult)
            last.then_inc(gains_made, 1)
            eng.drain()
            eng.wait_ge(cache_in, 32)
            for tile in range(TILES):
                g = group_of(tile)
                eng.wait_ge(ssq_done, tile + 1)
                eng.tensor_scalar(rms[:, tile, 1:2], rms[:, tile, 0:1], 1.0 / D, EPS, ALU.mult, ALU.add).then_inc(rms_done, 1)
                eng.wait_ge(std_done, tile + 1)
                done(eng, eng.reciprocal(rms[:, tile, 3:4], rms[:, tile, 2:3]))
                done(eng, eng.scalar_tensor_tensor(out=x[:, :], in0=h[:, tile, :], scalar=rms[:, tile, 3:4], in1=gain[g][:, :], op0=ALU.mult, op1=ALU.mult))
                eng.tensor_tensor(x[:, :], x[:, :], shift[g][:, :], ALU.add).then_inc(x_ready, 1)
                eng.wait_ge(lat_sq, 2 * tile + 2)
                eng.tensor_scalar(rms[:, tile, 6:7], rms[:, tile, 4:5], 1.0 / Q_LORA, EPS, ALU.mult, ALU.add)
                eng.tensor_scalar(rms[:, tile, 7:8], rms[:, tile, 5:6], 1.0 / KV_LORA, EPS, ALU.mult, ALU.add).then_inc(lat_ms, 1)
                eng.wait_ge(lat_std, tile + 1)
                done(eng, eng.reciprocal(rms[:, tile, 10:12], rms[:, tile, 8:10]))
                eng.tensor_copy(kpe[:, key_tile(tile), :], s_ps[1][:, BANK + KV_LORA:BANK + KV_LORA + ROPE])
                eng.scalar_tensor_tensor(out=lat_q[:, :], in0=s_ps[1][:, 0:Q_LORA], scalar=rms[:, tile, 10:11], in1=q_a_norm[:, :], op0=ALU.mult, op1=ALU.mult)
                eng.scalar_tensor_tensor(out=lat_kv[:, :], in0=s_ps[1][:, BANK:BANK + KV_LORA], scalar=rms[:, tile, 11:12], in1=kv_a_norm[:, :],
                                         op0=ALU.mult, op1=ALU.mult).then_inc(lat_ready, 1)
                eng.drain()

            def over_heads(row):
                return row.unsqueeze(1).broadcast_to([P, HH, row.shape[1]])

            def over_dims(col, n):
                return col.unsqueeze(2).broadcast_to([P, HH, n])

            with eng.Fori(0, HALVES) as hh:
                for s in range(STEPS):
                    step = hh * STEPS + s
                    is_key = s < KEY_TILES
                    eng.wait_ge(hd_mm, step + 1)
                    if is_key:
                        eng.tensor_copy(heads_sb[:, :, 0:NOPE], s_ps[0][:, :].rearrange("p (n w) -> p n w", n=HH)[:, :, 0:NOPE])
                        eng.tensor_copy(heads_sb[:, :, NOPE:QK], over_heads(kpe[:, s, :])).then_inc(hd_copied, 1)
                    else:
                        for c in range(2):
                            last = eng.tensor_copy(heads_sb[:, c * HH // 2:(c + 1) * HH // 2, :].rearrange("p n w -> p (n w)"),
                                                   s_ps[0][:, c * BANK:c * BANK + HH * QK // 2])
                        last.then_inc(hd_copied, 1)
                    eng.wait_ge(hd_sq, step + 1)
                    done(eng, eng.tensor_reduce(head_ms[:, 0, :], heads_sq[:, :, :], AX.X, ALU.add))
                    eng.tensor_scalar(head_ms[:, 1, :], head_ms[:, 0, :], 1.0 / QK, EPS, ALU.mult, ALU.add).then_inc(hd_ms, 1)
                    eng.wait_ge(hd_std, step + 1)
                    done(eng, eng.reciprocal(head_ms[:, 0, :], head_ms[:, 2, :]))
                    done(eng, eng.tensor_tensor(heads_sb[:, :, :], heads_sb[:, :, :], over_dims(head_ms[:, 0, :], QK), ALU.mult))
                    tile = s if is_key else s - KEY_TILES
                    scaled = eng.tensor_tensor(heads_sb[:, :, :], heads_sb[:, :, :], over_heads(qk_gain[:, int(is_key), :]), ALU.mult)
                    if tile < SAMPLE_TILES:
                        eng.drain()
                        pairs = heads_sb[:, :, NOPE:QK].rearrange("p n (f two) -> p n f two", two=2)
                        x1, x2 = pairs[:, :, :, 0], pairs[:, :, :, 1]
                        c, d = over_heads(cos[:, tile, :]), over_heads(sin[:, tile, :])
                        eng.tensor_tensor(rope_tmp[:, 0, :, :], x1, c, ALU.mult)
                        eng.tensor_tensor(rope_tmp[:, 1, :, :], x2, d, ALU.mult)
                        eng.tensor_tensor(rope_tmp[:, 2, :, :], x1, d, ALU.mult)
                        done(eng, eng.tensor_tensor(rope_tmp[:, 3, :, :], x2, c, ALU.mult))
                        eng.tensor_tensor(x1, rope_tmp[:, 0, :, :], rope_tmp[:, 1, :, :], ALU.subtract)
                        scaled = eng.tensor_tensor(x2, rope_tmp[:, 2, :, :], rope_tmp[:, 3, :, :], ALU.add)
                    scaled.then_inc(hd_ready, 1)
                    eng.drain()
                    if is_key:
                        eng.wait_ge(hd_tr, step + 1)
                        continue
                    _, n_keys = keys_of(tile)
                    at = (hh * TILES + tile) * HH
                    for n in range(HH):
                        eng.wait_ge(s_mm, at + n + 1)
                        done(eng, eng.tensor_reduce(neg_max[n % 2][:, 0:1], s_ps[n % 2][:, 0:n_keys], AX.X, ALU.max))
                        eng.tensor_scalar(neg_max[n % 2][:, 1:2], neg_max[n % 2][:, 0:1], -SCALE, None, ALU.mult).then_inc(max_done, 1)
                    eng.wait_ge(pv_mm, at + HH)
                    done(eng, eng.reciprocal(sums[:, 1, :], sums[:, 0, :]))
                    eng.tensor_tensor(out_heads[:, tile, bass.ds(hh * (HH * VH), HH * VH)].rearrange("p (n w) -> p n w", n=HH),
                                      o_ps[:, :].rearrange("p (n w) -> p n w", n=HH), over_dims(sums[:, 1, :], VH), ALU.mult).then_inc(o_used, 1)

            for c in range(2):
                for tile in range(TILES):
                    n, g = c * TILES + tile, group_of(tile)
                    tmp = x[:, (n % 2) * BANK:(n % 2 + 1) * BANK]
                    eng.wait_ge(out_mm, n + 1)
                    eng.tensor_tensor(tmp, s_ps[1][:, (n % 2) * BANK:(n % 2 + 1) * BANK], gate[g][:, c * BANK:(c + 1) * BANK], ALU.mult).then_inc(out_used, 1)
                    eng.drain()
                    done(eng, eng.tensor_tensor(h[:, tile, c * BANK:(c + 1) * BANK], h[:, tile, c * BANK:(c + 1) * BANK], tmp, ALU.add))


def peer_stage(nc, dram, layer, h, ident, mod_rows, y_out):
    wq = dram["peer_wq"][layer].rearrange("(k p) n -> p k n", p=P)
    u_rows, v_rows = (dram[n].rearrange("l e d -> (l e) d") for n in ("peer_u", "peer_v"))
    first_row = layer * N_KEYS * N_KEYS
    with ExitStack() as ctx:
        def sb(name, shape, dt=F32):
            return ctx.enter_context(nc.sbuf_tensor(f"peer{layer}_{name}", shape, dt))

        def pb(name, shape, dt=F32):
            return ctx.enter_context(nc.psum_tensor(f"peer{layer}_{name}", shape, dt))

        sems = []

        def sem(name):
            sems.append(ctx.enter_context(nc.semaphore(f"p{layer}_{name}")))
            return sems[-1]

        wq_sb = sb("wq", [P, KD, PEER_HEADS * PEER_QDIM])
        u_ring = [sb(f"u{k}", [P, D]) for k in range(RING)]
        v_ring = [sb(f"v{k}", [P, D]) for k in range(RING)]
        x = [sb(f"x{b}", [P, D]) for b in range(2)]
        xT = sb("xT", [P, KD, P])
        product = sb("product", [P, D], BF16)
        gain = [sb(f"gain{g}", [P, D]) for g in range(2)]
        shift = [sb(f"shift{g}", [P, D]) for g in range(2)]
        gate = [sb(f"gate{g}", [P, D]) for g in range(2)]
        keys_sb = sb("keys", [P, 2, P])
        keysT = sb("keysT", [P, 2, P])
        iota = sb("iota", [P, TOPK])
        zeros = sb("zeros", [P, HALF_BANK * 2], BF16)
        rms = sb("rms", [P, 4])
        q_sb = sb("q", [P, 2 * P])
        qT_sb = sb("qT", [P, 2, P])
        s_sb = sb("s", [P, 2, P])
        s_rest = sb("s_rest", [P, 2, P])
        top = sb("top", [P, 2, TOPK])
        top_at = sb("top_at", [P, 2, TOPK], U32)
        top_atf = sb("top_atf", [P, 2, TOPK])
        cand = sb("cand", [P, TOPK * TOPK])
        cand_rest = sb("cand_rest", [P, TOPK * TOPK])
        best = sb("best", [P, TOPK])
        best_at = sb("best_at", [P, TOPK], U32)
        side_at = sb("side_at", [P, TOPK, 2], U32)
        one_hot = sb("one_hot", [P, TOPK, 2, TOPK])
        picked = sb("picked", [P, TOPK, 2])
        expert = [sb(f"expert{b}", [P, TOPK], I32) for b in range(2)]
        neg_max = sb("neg_max", [P, 1])
        exps = [sb(f"exps{b}", [P, TOPK]) for b in range(2)]
        exp_sum = [sb(f"exp_sum{b}", [P, 1]) for b in range(2)]
        inv_sum = sb("inv_sum", [P, 1])
        dots = [sb(f"dots{b}", [P, RING]) for b in range(2)]
        gelus = [sb(f"gelus{b}", [P, RING]) for b in range(2)]
        weight = [sb(f"weight{b}", [P, RING]) for b in range(2)]
        diag = [sb(f"diag{b}", [P, P]) for b in range(DIAGS)]

        acc = pb("acc", [P, D])
        q_ps = pb("q_ps", [P, HALF_BANK * 2])
        qT_ps = pb("qT_ps", [P, HALF_BANK * 2])
        s_ps = pb("s_ps", [P, HALF_BANK * 2])
        xT_ps = pb("xT_ps", [P, KD, P])

        wq_in, keys_in, gain_in, mod_in = sem("wq_in"), sem("keys_in"), sem("gain_in"), sem("mod_in")
        gains_made, consts = sem("gains_made"), sem("consts")
        keys_tr, keys_ev = sem("keys_tr"), sem("keys_ev")
        ssq_done, std_done, rms_done = sem("ssq"), sem("std"), sem("rms")
        x_ready, xT_tr, xT_ready = sem("x_ready"), sem("xT_tr"), sem("xT_ready")
        q_mm, q_ev, qT_tr, qT_ev, s_mm, s_ev = (sem(n) for n in ("q_mm", "q_ev", "qT_tr", "qT_ev", "s_mm", "s_ev"))
        best_done, exp_done, expert_done = sem("best"), sem("exp"), sem("expert")
        u_free, v_free = sem("u_free"), sem("v_free")
        gather_go = sem("gather_go")
        u_in = [sem(f"u_in{k}") for k in range(RING)]
        v_in = [sem(f"v_in{k}") for k in range(RING)]
        gelu_done, weight_done, diag_done = sem("gelu"), sem("weight"), sem("diag")
        acc_done, acc_used, y_done, y_stored = sem("acc_done"), sem("acc_used"), sem("y_done"), sem("y_st")

        ctx.callback(clear_semaphores, nc, sems)
        block = ctx.enter_context(nc.Block())

        @block.sync
        def _(eng):
            for side in range(2):
                eng.dma_start(keys_sb[:, side, :], dram["peer_keys"][layer, side]).then_inc(keys_in, 16)
            eng.dma_start(x[1][:, :], dram["norm2_g"][layer:layer + 1, :].broadcast_to([P, D])).then_inc(gain_in, 16)
            for g in range(2):
                for dst, part in ((shift, 3), (gain, 4), (gate, 5)):
                    eng.dma_start(dst[g][:, :], mod_rows[layer, g:g + 1, part * D:(part + 1) * D].broadcast_to([P, D])).then_inc(mod_in, 16)
            for k in range(KD):
                eng.dma_start(wq_sb[:, k, :], wq[:, k, :]).then_inc(wq_in, 16)
            if y_out is not None:
                for tile in range(TILES):
                    eng.wait_ge(y_done, tile + 1)
                    eng.dma_start(y_out[tile], h[:, tile, :]).then_inc(y_stored, 16)
                eng.wait_ge(y_stored, 16 * TILES)

        @block.gpsimd
        def _(eng):
            eng.iota(iota[:, :], [[1, TOPK]], base=0, channel_multiplier=0, allow_small_or_imprecise_dtypes=True).then_inc(consts, 1)
            eng.memset(zeros[:, :], 0.0).then_inc(consts, 1)
            eng.sem_inc(u_free, RING)
            eng.sem_inc(v_free, RING)

            def head(g, par):
                eng.wait_ge(expert_done, g + 1)
                eng.sem_inc(gather_go, 1)
                for half in range(2):
                    for rows, ring, free, landed in ((u_rows, u_ring, u_free, u_in), (v_rows, v_ring, v_free, v_in)):
                        for k in range(RING):
                            slot = half * RING + k
                            eng.wait_ge(free, g * TOPK + slot + 1)
                            eng.sem_inc(gather_go, 1)
                            eng.indirect_dma_start(
                                out=ring[k][:, :], out_offset=None, in_=rows,
                                in_offset=bass.IndirectOffsetOnAxis(ap=expert[par][:, slot:slot + 1], axis=0),
                            ).then_inc(landed[k], 16)

            with eng.Fori(0, TILES * PEER_HEADS // 2) as i:
                head(2 * i, 0)
                head(2 * i + 1, 1)

        def group_of(tile):
            return 1 if tile == TILES - 1 else 0

        @block.vector
        def _(eng):
            eng.wait_ge(gain_in, 16)
            eng.wait_ge(mod_in, 16 * 6)
            for g in range(2):
                ins = eng.scalar_tensor_tensor(out=gain[g][:, :], in0=gain[g][:, :], scalar=1.0, in1=x[1][:, :], op0=ALU.add, op1=ALU.mult)
                ins.then_inc(gains_made, 1)
            eng.wait_ge(gains_made, 2)

            def norm(tile):
                xb = x[tile % 2][:, :]
                eng.wait_ge(ssq_done, tile + 1)
                done(eng, eng.tensor_scalar(rms[:, 1:2], rms[:, 0:1], 1.0 / D, EPS, ALU.mult, ALU.add))
                eng.tensor_scalar(rms[:, 2:3], rms[:, 1:2], 1.0, None, ALU.mult).then_inc(rms_done, 1)
                eng.wait_ge(std_done, tile + 1)
                done(eng, eng.reciprocal(rms[:, 3:4], rms[:, 1:2]))
                done(eng, eng.scalar_tensor_tensor(out=xb, in0=h[:, tile, :], scalar=rms[:, 3:4], in1=gain[group_of(tile)][:, :], op0=ALU.mult, op1=ALU.mult))
                eng.tensor_tensor(xb, xb, shift[group_of(tile)][:, :], ALU.add).then_inc(x_ready, 1)
                eng.wait_ge(x_ready, tile + 1)

            def top16(values, rest, vals, at):
                done(eng, eng.max(vals[:, 0:8], values))
                done(eng, eng.match_replace(out=rest, in_to_replace=vals[:, 0:8], in_values=values, imm_value=LOWEST))
                eng.max_index(at[:, 0:8], vals[:, 0:8], values)
                done(eng, eng.max(vals[:, 8:16], rest))
                done(eng, eng.max_index(at[:, 8:16], vals[:, 8:16], rest))

            def route(r, par, first=False):
                eng.wait_ge(s_mm, r + 1)
                eng.tensor_copy(s_sb[:, :, :].rearrange("p s n -> p (s n)"), s_ps[:, 0:2 * P]).then_inc(s_ev, 1)
                eng.drain()
                for side in range(2):
                    top16(s_sb[:, side, :], s_rest[:, side, :], top[:, side, :], top_at[:, side, :])
                if not first:
                    eng.wait_ge(exp_done, r)
                eng.tensor_scalar(top_atf[:, 0, :], top_at[:, 0, :], float(N_KEYS), float(first_row), ALU.mult, ALU.add)
                done(eng, eng.tensor_copy(top_atf[:, 1, :], top_at[:, 1, :]))
                done(eng, eng.tensor_tensor(cand[:, :].rearrange("p (a b) -> p a b", a=TOPK),
                                           top[:, 0, :].unsqueeze(2).broadcast_to([P, TOPK, TOPK]),
                                           top[:, 1, :].unsqueeze(1).broadcast_to([P, TOPK, TOPK]), ALU.add))
                top16(cand[:, :], cand_rest[:, :], best[:, :], best_at[:, :])
                eng.tensor_scalar(neg_max[:, :], best[:, 0:1], -1.0, None, ALU.mult).then_inc(best_done, 1)
                done(eng, eng.tensor_scalar(side_at[:, :, 0], best_at[:, :], 4, None, ALU.logical_shift_right))
                done(eng, eng.tensor_scalar(side_at[:, :, 1], best_at[:, :], 15, None, ALU.bitwise_and))
                hot = one_hot[:, :, :, :].rearrange("p k s a -> p (k s) a")
                done(eng, eng.tensor_tensor(hot, iota[:, :].unsqueeze(1).broadcast_to([P, 2 * TOPK, TOPK]),
                                           side_at[:, :, :].rearrange("p k s -> p (k s)").unsqueeze(2).broadcast_to([P, 2 * TOPK, TOPK]),
                                           ALU.is_equal))
                done(eng, eng.tensor_tensor(one_hot[:, :, :, :].rearrange("p k s a -> p k (s a)"),
                                           one_hot[:, :, :, :].rearrange("p k s a -> p k (s a)"),
                                           top_atf[:, :, :].rearrange("p s a -> p (s a)").unsqueeze(1).broadcast_to([P, TOPK, 2 * TOPK]),
                                           ALU.mult))
                done(eng, eng.tensor_reduce(picked[:, :, :].rearrange("p k s -> p (k s)"), hot, AX.X, ALU.add))
                if not first:
                    eng.wait_ge(v_free, r * TOPK - TOPK + RING)
                eng.tensor_tensor(expert[par][:, :], picked[:, :, 0], picked[:, :, 1], ALU.add).then_inc(expert_done, 1)

            def half_head(g, par, half, b):
                for k in range(RING):
                    n = g * TOPK + half * RING + k
                    eng.wait_ge(u_in[k], (2 * g + half + 1) * 16)
                    eng.wait_ge(u_free, n + RING)
                    eng.tensor_tensor_reduce(out=product[:, :], in0=u_ring[k][:, :], in1=x[b][:, :], scale=1.0, scalar=0.0,
                                             op0=ALU.mult, op1=ALU.add, accum_out=dots[half][:, k:k + 1]).then_inc(u_free, 1)
                if half == 0:
                    eng.wait_ge(exp_done, g + 1)
                    done(eng, eng.reciprocal(inv_sum[:, :], exp_sum[par][:, :]))
                eng.wait_ge(gelu_done, 2 * g + half + 1)
                eng.scalar_tensor_tensor(out=weight[half][:, :], in0=gelus[half][:, :], scalar=inv_sum[:, :],
                                         in1=exps[par][:, half * RING:(half + 1) * RING],
                                         op0=ALU.mult, op1=ALU.mult).then_inc(weight_done, 1)
                eng.wait_ge(weight_done, 2 * g + half + 1)

            def finish_tile(tile):
                eng.wait_ge(acc_done, tile + 1)
                tmp = x[tile % 2][:, :]
                done(eng, eng.tensor_tensor(tmp, acc[:, :], gate[group_of(tile)][:, :], ALU.mult))
                eng.tensor_tensor(h[:, tile, :], h[:, tile, :], tmp, ALU.add).then_inc(y_done, 1)
                eng.wait_ge(y_done, tile + 1)

            eng.wait_ge(consts, 2)
            norm(0)
            route(0, 0, first=True)
            for tile in range(TILES):
                b = tile % 2
                if tile:
                    finish_tile(tile - 1)
                with eng.Fori(0, PEER_HEADS // 2 - 1) as i:
                    for par in range(2):
                        g = tile * PEER_HEADS + 2 * i + par
                        half_head(g, par, 0, b)
                        route(g + 1, 1 - par)
                        half_head(g, par, 1, b)
                for par in range(2):
                    g = tile * PEER_HEADS + PEER_HEADS - 2 + par
                    half_head(g, par, 0, b)
                    if g + 1 < TILES * PEER_HEADS:
                        route(g + 1, 1 - par)
                    half_head(g, par, 1, b)
                    if par == 0 and tile + 1 < TILES:
                        norm(tile + 1)
            finish_tile(TILES - 1)

        @block.scalar
        def _(eng):
            eng.wait_ge(keys_tr, 1)
            eng.activation(keysT[:, :, :].rearrange("p s n -> p (s n)"), qT_ps[:, 0:2 * P], ACT.Copy).then_inc(keys_ev, 1)

            def norm(tile):
                if tile == 1:
                    eng.wait_ge(gains_made, 2)
                eng.activation(x[tile % 2][:, :], h[:, tile, :], ACT.Square, accum_out=rms[:, 0:1]).then_inc(ssq_done, 1)
                eng.wait_ge(rms_done, tile + 1)
                eng.activation(rms[:, 1:2], rms[:, 2:3], ACT.Sqrt).then_inc(std_done, 1)
                for half in range(2):
                    eng.wait_ge(xT_tr, 2 * tile + half + 1)
                    eng.activation(xT[:, 4 * half:4 * half + 4, :].rearrange("p k t -> p (k t)"),
                                   xT_ps[:, 4 * half:4 * half + 4, :].rearrange("p k t -> p (k t)"), ACT.Copy).then_inc(xT_ready, 1)

            def route(r):
                eng.wait_ge(q_mm, r + 1)
                eng.activation(q_sb[:, :], q_ps[:, 0:2 * P], ACT.Copy).then_inc(q_ev, 1)
                eng.wait_ge(qT_tr, r + 1)
                eng.activation(qT_sb[:, :, :].rearrange("p s t -> p (s t)"), qT_ps[:, 0:2 * P], ACT.Copy).then_inc(qT_ev, 1)

            def softmax(r, par):
                eng.wait_ge(best_done, r + 1)
                eng.activation(exps[par][:, :], best[:, :], ACT.Exp, bias=neg_max[:, :], accum_out=exp_sum[par][:, :]).then_inc(exp_done, 1)

            def half_head(g, half):
                eng.wait_ge(u_free, g * TOPK + (half + 1) * RING + RING)
                eng.activation(gelus[half][:, :], dots[half][:, :], ACT.Gelu).then_inc(gelu_done, 1)
                eng.wait_ge(weight_done, 2 * g + half + 1)
                for k in range(RING):
                    n = g * TOPK + half * RING + k
                    eng.wait_ge(v_free, n - DIAGS + 1 + RING)
                    eng.activation(diag[k % DIAGS][:, :], ident[:, :], ACT.Copy, scale=weight[half][:, k:k + 1]).then_inc(diag_done, 1)

            norm(0)
            route(0)
            softmax(0, 0)
            for tile in range(TILES):
                with eng.Fori(0, PEER_HEADS // 2 - 1) as i:
                    for par in range(2):
                        g = tile * PEER_HEADS + 2 * i + par
                        route(g + 1)
                        half_head(g, 0)
                        softmax(g + 1, 1 - par)
                        half_head(g, 1)
                for par in range(2):
                    g = tile * PEER_HEADS + PEER_HEADS - 2 + par
                    more = g + 1 < TILES * PEER_HEADS
                    if more:
                        route(g + 1)
                    half_head(g, 0)
                    if more:
                        softmax(g + 1, 1 - par)
                    half_head(g, 1)
                    if par == 0 and tile + 1 < TILES:
                        norm(tile + 1)

        @block.tensor
        def _(eng):
            eng.wait_ge(keys_in, 32)
            for side in range(2):
                last = eng.transpose(qT_ps[:, side * P:(side + 1) * P], keys_sb[:, side, :], ident[:, :])
            last.then_inc(keys_tr, 1)
            eng.wait_ge(keys_ev, 1)

            def transpose_x(tile):
                eng.wait_ge(x_ready, tile + 1)
                for half in range(2):
                    if tile:
                        eng.wait_ge(xT_ready, 2 * tile - 1 + half)
                    for k in range(4 * half, 4 * half + 4):
                        last = eng.transpose(xT_ps[:, k, :], x[tile % 2][:, k * P:(k + 1) * P], ident[:, :])
                    last.then_inc(xT_tr, 1)

            def route(r, head, tile):
                if isinstance(head, int) and head == 0:
                    eng.wait_ge(xT_ready, 2 * tile + 2)
                first = isinstance(r, int) and r == 0
                if not first:
                    eng.wait_ge(q_ev, r)
                for k in range(KD):
                    last = eng.matmul(q_ps[:, 0:2 * P], xT[:, k, :], wq_sb[:, k, bass.ds(head * 2 * P, 2 * P)],
                                      start=(k == 0), stop=(k == KD - 1))
                last.then_inc(q_mm, 1)
                eng.wait_ge(q_ev, r + 1)
                if not first:
                    eng.wait_ge(qT_ev, r)
                for side in range(2):
                    last = eng.transpose(qT_ps[:, side * P:(side + 1) * P], q_sb[:, side * P:(side + 1) * P], ident[:, :])
                last.then_inc(qT_tr, 1)
                eng.wait_ge(qT_ev, r + 1)
                if not first:
                    eng.wait_ge(s_ev, r)
                for side in range(2):
                    last = eng.matmul(s_ps[:, side * P:(side + 1) * P], qT_sb[:, side, :], keysT[:, side, :], start=True, stop=True)
                last.then_inc(s_mm, 1)

            def half_head(g, half):
                for k in range(RING):
                    n = g * TOPK + half * RING + k
                    eng.wait_ge(v_in[k], (2 * g + half + 1) * 16)
                    eng.wait_ge(diag_done, n + 1)
                    for c in range(2):
                        last = eng.matmul(acc[:, c * BANK:(c + 1) * BANK], diag[k % DIAGS][:, :],
                                          v_ring[k][:, c * BANK:(c + 1) * BANK], start=False, stop=False)
                    last.then_inc(v_free, 1)

            def bound_sum(start):
                for c in range(2):
                    last = eng.matmul(acc[:, c * BANK:(c + 1) * BANK], zeros[:, 0:P], zeros[:, :], start=start, stop=not start)
                return last

            transpose_x(0)
            eng.wait_ge(consts, 2)
            eng.wait_ge(wq_in, 16 * KD)
            route(0, 0, 0)
            for tile in range(TILES):
                if tile:
                    eng.wait_ge(y_done, tile)
                bound_sum(True)
                with eng.Fori(0, PEER_HEADS // 2 - 1) as i:
                    for par in range(2):
                        g = tile * PEER_HEADS + 2 * i + par
                        route(g + 1, 2 * i + par + 1, tile)
                        half_head(g, 0)
                        half_head(g, 1)
                for par in range(2):
                    head = PEER_HEADS - 2 + par
                    g = tile * PEER_HEADS + head
                    if g + 1 < TILES * PEER_HEADS:
                        route(g + 1, (head + 1) % PEER_HEADS, tile + (head + 1) // PEER_HEADS)
                    half_head(g, 0)
                    half_head(g, 1)
                    if par == 0 and tile + 1 < TILES:
                        transpose_x(tile + 1)
                bound_sum(False).then_inc(acc_done, 1)
def build_program(nc, dram, outs):
    y_prompt, y_sample, new_ckv, new_kpe = outs
    mod_rows = nc.dram_tensor("modulation_rows", [DEPTH, 2, 6 * D], F32, kind="Internal").ap()
    with ExitStack() as ctx:
        h = ctx.enter_context(nc.sbuf_tensor("residual", [P, TILES, D], F32))
        ident = ctx.enter_context(nc.sbuf_tensor("identity", [P, P], F32))
        loaded = ctx.enter_context(nc.semaphore("loaded"))
        with nc.Block() as block:
            @block.sync
            def _(eng):
                eng.dma_start(h[:, 0:SAMPLE_TILES, :], dram["x_sample"][0].rearrange("(t p) d -> p t d", p=P)).then_inc(loaded, 16)
                eng.dma_start(h[:, SAMPLE_TILES, :], dram["x_prompt"][0]).then_inc(loaded, 16)
                eng.dma_start(ident[:, :], dram["identity"]).then_inc(loaded, 16)
                eng.wait_ge(loaded, 48)
        y_tiles = [y_sample[0, t * P:(t + 1) * P, :] for t in range(SAMPLE_TILES)] + [y_prompt[0]]
        modulation_stage(nc, dram, 0, mod_rows)
        conv_stage(nc, dram, 0, 0, h, ident, mod_rows)
        peer_stage(nc, dram, 0, h, ident, mod_rows, None)
        modulation_stage(nc, dram, 1, mod_rows)
        attention_stage(nc, dram, 1, 0, h, ident, mod_rows, new_ckv[0, 0], new_kpe[0, 0])
        peer_stage(nc, dram, 1, h, ident, mod_rows, y_tiles)


_INPUTS = ["x_prompt", "x_sample", "cache_ckv", "cache_kpe", "c", "c_ctx", "mod_w", "mod_b", "norm1_g", "norm2_g",
           "conv_w_in", "conv_b_in", "conv_dw", "conv_dw_b", "conv_norm_g", "conv_w_out", "conv_b_out",
           "q_a_w", "q_a_norm", "q_b_w", "kv_a_w", "kv_a_norm", "kv_b_w", "q_norm", "k_norm", "o_w",
           "peer_wq", "peer_keys", "peer_u", "peer_v"]
_OUTPUTS = [("y_prompt", (1, SEQ, D)), ("y_sample", (1, DEC_SEQ, D)), ("new_ckv", (1, 1, SEQ, KV_LORA)), ("new_kpe", (1, 1, SEQ, ROPE))]


def _shape_constants():
    import numpy as np

    half = ROPE // 2
    row = np.repeat(np.arange(DEC_SEQ // GRID_W), GRID_W).astype(np.float32)
    col = np.tile(np.arange(GRID_W), DEC_SEQ // GRID_W).astype(np.float32)
    inv = (np.float32(ROPE_THETA) ** (-(np.arange(half // 2, dtype=np.float32) * np.float32(2.0) / np.float32(half)))).astype(np.float32)
    angle = np.concatenate([row[:, None] * inv, col[:, None] * inv], axis=-1).astype(np.float32)
    return {"identity": np.eye(P, dtype=np.float32), "rope_cos": np.cos(angle).astype(np.float32), "rope_sin": np.sin(angle).astype(np.float32)}


def kernel(**inputs):
    import numpy as np
    import concourse.bacc as bacc
    from concourse.bass_utils import run_bass_kernel_spmd

    nc = bacc.Bacc("TRN2", target_bir_lowering=False, num_devices=1)
    arrays, dram = {}, {}
    given = {name: np.ascontiguousarray(inputs[name]) for name in _INPUTS}
    given.update(_shape_constants())
    for name, a in given.items():
        arrays[f"in_{name}"] = a
        dram[name] = nc.dram_tensor(f"in_{name}", a.shape, mybir.dt.from_np(a.dtype), kind="ExternalInput").ap()
    outs = [nc.dram_tensor(f"out_{name}", shape, F32, kind="ExternalOutput").ap() for name, shape in _OUTPUTS]
    build_program(nc, dram, outs)
    r = run_bass_kernel_spmd(nc, [arrays], core_ids=[0])
    return tuple(r.results[0][f"out_{name}"] for name, _ in _OUTPUTS)
```

```python
from contextlib import ExitStack

import concourse.bass as bass
from concourse import mybir

F32, BF16, I32, U32 = mybir.dt.float32, mybir.dt.bfloat16, mybir.dt.int32, mybir.dt.uint32
ALU = mybir.AluOpType
ACT = mybir.ActivationFunctionType
AX = mybir.AxisListType

P = 128
BANK = 512
HALF_BANK = BANK // 2
D = 1024
KD = D // P
SEQ, DEC_SEQ, PAST_LEN = 128, 512, 128
SAMPLE_TILES = DEC_SEQ // P
TILES = SAMPLE_TILES + SEQ // P
GRID_W, ROPE_THETA, DEPTH = 64, 10000.0, 2
CONV_K = 31
PAD = CONV_K // 2
HEADS, NOPE, ROPE, VH = 16, 64, 32, 64
QK = NOPE + ROPE
Q_LORA, KV_LORA = 512, 256
PEER_HEADS, PEER_QDIM, N_KEYS, TOPK = 8, 256, 128, 16
EPS = 1e-6
LOWEST = -3.4028234663852886e38
RING = 8
DIAGS = 4
MOD_BUFS = 4


def done(eng, ins):
    eng.drain()
    return ins


def clear_semaphores(nc, sems):
    with nc.Block() as block:
        @block.gpsimd
        def _(eng):
            for s in sems:
                eng.sem_clear(s)


def modulation_stage(nc, dram, layer, mod_rows):
    chunks = 6 * D // BANK
    w = dram["mod_w"][layer].rearrange("(p j) n -> p j n", j=KD)
    bias = dram["mod_b"][layer:layer + 1, :]
    with ExitStack() as ctx:
        def sb(name, shape, dt=F32):
            return ctx.enter_context(nc.sbuf_tensor(f"mod{layer}_{name}", shape, dt))

        sems = []

        def sem(name):
            sems.append(ctx.enter_context(nc.semaphore(f"m{layer}_{name}")))
            return sems[-1]

        cond = sb("cond", [P, 2, KD])
        silu = sb("silu", [P, 2, KD])
        w_sb = [sb(f"w{b}", [P, KD, BANK]) for b in range(MOD_BUFS)]
        bias_sb = [sb(f"bias{b}", [2, BANK]) for b in range(MOD_BUFS)]
        rows = [sb(f"rows{b}", [2, BANK]) for b in range(MOD_BUFS)]
        ps = [ctx.enter_context(nc.psum_tensor(f"mod{layer}_ps{b}", [P, BANK], F32)) for b in range(MOD_BUFS)]
        cond_in, silu_done = sem("cond_in"), sem("silu")
        w_in = [sem(f"w_in{b}") for b in range(MOD_BUFS)]
        w_free, mm_done, row_done = sem("w_free"), sem("mm"), sem("row")
        stored = [sem(f"st{b}") for b in range(MOD_BUFS)]
        ctx.callback(clear_semaphores, nc, sems)
        block = ctx.enter_context(nc.Block())

        @block.sync
        def _(eng):
            eng.dma_start(cond[:, 0, :], dram["c"].rearrange("a (p j) -> (a p) j", j=KD)).then_inc(cond_in, 16)
            eng.dma_start(cond[:, 1, :], dram["c_ctx"].rearrange("(p j) -> p j", j=KD)).then_inc(cond_in, 16)

            def load(c, b):
                eng.dma_start(w_sb[b][:, :, :], w[:, :, bass.ds(c * BANK, BANK)]).then_inc(w_in[b], 16)
                eng.dma_start(bias_sb[b][:, :], bias[:, bass.ds(c * BANK, BANK)].broadcast_to([2, BANK])).then_inc(w_in[b], 16)

            for b in range(MOD_BUFS):
                load(b, b)
            with eng.Fori(1, chunks // MOD_BUFS) as i:
                for b in range(MOD_BUFS):
                    eng.wait_ge(row_done, i * MOD_BUFS - MOD_BUFS + b + 1)
                    load(i * MOD_BUFS + b, b)

        @block.scalar
        def _(eng):
            eng.wait_ge(cond_in, 32)
            eng.activation(silu[:, :, :], cond[:, :, :], ACT.Silu).then_inc(silu_done, 1)
            with eng.Fori(0, chunks // MOD_BUFS) as i:
                for b in range(MOD_BUFS):
                    c = i * MOD_BUFS + b
                    eng.wait_ge(row_done, c + 1)
                    eng.dma_start(mod_rows[layer, :, bass.ds(c * BANK, BANK)], rows[b][:, :]).then_inc(stored[b], 16)
            for b in range(MOD_BUFS):
                eng.wait_ge(stored[b], 16 * (chunks // MOD_BUFS))

        @block.tensor
        def _(eng):
            eng.wait_ge(silu_done, 1)
            with eng.Fori(0, chunks // MOD_BUFS) as i:
                for b in range(MOD_BUFS):
                    eng.wait_ge(w_in[b], 32 * i + 32)
                    for j in range(KD):
                        last = eng.matmul(ps[b][0:2, :], silu[:, :, j], w_sb[b][:, j, :], start=(j == 0), stop=(j == KD - 1))
                    last.then_inc(mm_done, 1)

        @block.vector
        def _(eng):
            def add_bias(c, b):
                eng.wait_ge(mm_done, c + 1)
                eng.tensor_tensor(rows[b][:, :], ps[b][0:2, :], bias_sb[b][:, :], ALU.add).then_inc(row_done, 1)

            for b in range(MOD_BUFS):
                add_bias(b, b)
            with eng.Fori(1, chunks // MOD_BUFS) as i:
                for b in range(MOD_BUFS):
                    eng.wait_ge(stored[b], 16 * i)
                    add_bias(i * MOD_BUFS + b, b)


def conv_stage(nc, dram, layer, j, h, ident, mod_rows):
    w_in_d = dram["conv_w_in"][j].rearrange("(k p) n -> p k n", p=P)
    w_out_d = dram["conv_w_out"][j].rearrange("(k p) n -> p k n", p=P)
    T = TILES * P
    PROMPT_AT = DEC_SEQ + PAD
    OUT_LEN = PROMPT_AT + SEQ
    IN_LEN = OUT_LEN + 2 * PAD
    SEGMENTS = ((0, DEC_SEQ, 0), (DEC_SEQ, SEQ, PROMPT_AT))
    with ExitStack() as ctx:
        def sb(name, shape, dt=F32):
            return ctx.enter_context(nc.sbuf_tensor(f"conv_{name}", shape, dt))

        sems = []

        def sem(name):
            sems.append(ctx.enter_context(nc.semaphore(f"c_{name}")))
            return sems[-1]

        xT = sb("xT", [P, KD, T])
        x = [sb(f"x{b}", [P, D]) for b in range(2)]
        w_ag = [sb(f"w_ag{b}", [P, 2, KD, P]) for b in range(2)]
        w_out = sb("w_out", [P, KD, D])
        sig = [sb(f"sig{b}", [P, T]) for b in range(2)]
        glu = [sb(f"glu{b}", [P, IN_LEN]) for b in range(2)]
        mixed = sb("mixed", [P, KD, OUT_LEN])
        square = [sb(f"square{b}", [P, OUT_LEN]) for b in range(2)]
        rstd = sb("rstd", [P, 2, T])
        ones = sb("ones", [P, P])
        rows = sb("rows", [32, P])
        cols = sb("cols", [P, 32])
        taps_rows = sb("taps_rows", [CONV_K, D])
        taps = sb("taps", [P, KD, CONV_K])
        rms = sb("rms", [P, TILES, 4])
        gain = [sb(f"gain{g}", [P, D]) for g in range(2)]
        shift = [sb(f"shift{g}", [P, D]) for g in range(2)]
        gate = [sb(f"gate{g}", [P, D]) for g in range(2)]
        norm_g = sb("norm_g", [P, D])
        b_out = sb("b_out", [P, D])
        B_A, DW_B, NORM_G = 0, 16, 24

        psum = [ctx.enter_context(nc.psum_tensor(f"conv_ps{b}", [P, 2 * BANK], F32)) for b in range(4)]
        a_ps, g_ps = (psum[0], psum[1]), (psum[2], psum[3])
        small_ps = psum[3]

        vec_in, small_in, w_out_in = sem("vec_in"), sem("small_in"), sem("w_out_in")
        w_in = [sem(f"w_in{b}") for b in range(2)]
        gains_made, ones_made, pads_made = sem("gains"), sem("ones"), sem("pads")
        small_tr, small_ev = sem("small_tr"), sem("small_ev")
        ssq_done, std_done, rms_done, x_ready, xT_tr, xT_ready = (sem(n) for n in ("ssq", "std", "rms", "x_ready", "xT_tr", "xT_ready"))
        ag_mm, sig_done, glu_done, conv_done = (sem(n) for n in ("ag_mm", "sig", "glu", "conv"))
        sq_done, sq_used, var_done, csd_done, rstd_done = (sem(n) for n in ("sq", "sq_used", "var", "csd", "rstd"))
        scaled, swish_done, out_mm, out_used = (sem(n) for n in ("scaled", "swish", "out_mm", "out_used"))

        ctx.callback(clear_semaphores, nc, sems)
        block = ctx.enter_context(nc.Block())

        def group_of(tile):
            return 1 if tile == TILES - 1 else 0

        @block.sync
        def _(eng):
            eng.dma_start(norm_g[:, :], dram["norm1_g"][layer:layer + 1, :].broadcast_to([P, D])).then_inc(vec_in, 16)
            for g in range(2):
                for dst, part in ((shift, 0), (gain, 1), (gate, 2)):
                    eng.dma_start(dst[g][:, :], mod_rows[layer, g:g + 1, part * D:(part + 1) * D].broadcast_to([P, D])).then_inc(vec_in, 16)
            eng.dma_start(rows[0:16, :], dram["conv_b_in"][j].rearrange("(r p) -> r p", p=P)).then_inc(small_in, 16)
            eng.dma_start(rows[16:24, :], dram["conv_dw_b"][j].rearrange("(r p) -> r p", p=P)).then_inc(small_in, 16)
            eng.dma_start(rows[24:32, :], dram["conv_norm_g"][j].rearrange("(r p) -> r p", p=P)).then_inc(small_in, 16)
            eng.dma_start(taps_rows[:, :], dram["conv_dw"][j]).then_inc(small_in, 16)

            def load(c, b):
                for half in range(2):
                    eng.dma_start(w_ag[b][:, half, :, :], w_in_d[:, :, bass.ds(half * D + c * P, P)]).then_inc(w_in[b], 16)

            load(0, 0)
            load(1, 1)
            eng.dma_start(b_out[:, :], dram["conv_b_out"][j:j + 1, :].broadcast_to([P, D])).then_inc(w_out_in, 16)
            for k in range(KD):
                eng.dma_start(w_out[:, k, :], w_out_d[:, k, :]).then_inc(w_out_in, 16)
            with eng.Fori(1, KD // 2) as i:
                for b in range(2):
                    eng.wait_ge(ag_mm, 2 * i + b - 1)
                    load(2 * i + b, b)

        @block.gpsimd
        def _(eng):
            eng.memset(ones[:, :], 1.0).then_inc(ones_made, 1)
            for b in range(2):
                for at in (0, PAD + DEC_SEQ, IN_LEN - PAD):
                    eng.memset(glu[b][:, at:at + PAD], 0.0).then_inc(pads_made, 1)
            eng.sem_inc(glu_done, 2)

        @block.vector
        def _(eng):
            eng.wait_ge(vec_in, 16 * 7)
            for g in range(2):
                eng.scalar_tensor_tensor(out=gain[g][:, :], in0=gain[g][:, :], scalar=1.0, in1=norm_g[:, :], op0=ALU.add, op1=ALU.mult)
            eng.drain()
            for tile in range(TILES):
                xb, g = x[tile % 2][:, :], group_of(tile)
                eng.wait_ge(ssq_done, tile + 1)
                eng.tensor_scalar(rms[:, tile, 1:2], rms[:, tile, 0:1], 1.0 / D, EPS, ALU.mult, ALU.add).then_inc(rms_done, 1)
                eng.wait_ge(std_done, tile + 1)
                done(eng, eng.reciprocal(rms[:, tile, 3:4], rms[:, tile, 2:3]))
                if tile >= 2:
                    eng.wait_ge(xT_tr, 2 * (tile - 1))
                done(eng, eng.scalar_tensor_tensor(out=xb, in0=h[:, tile, :], scalar=rms[:, tile, 3:4], in1=gain[g][:, :], op0=ALU.mult, op1=ALU.mult))
                eng.tensor_tensor(xb, xb, shift[g][:, :], ALU.add).then_inc(x_ready, 1)

            eng.wait_ge(pads_made, 6)
            eng.wait_ge(small_ev, 2)
            with eng.Fori(0, KD // 2) as i:
                for b in range(2):
                    c = 2 * i + b
                    eng.wait_ge(sig_done, c + 1)
                    for start, n, at in SEGMENTS:
                        last = eng.scalar_tensor_tensor(out=glu[b][:, PAD + at:PAD + at + n], in0=a_ps[b][:, start:start + n],
                                                        scalar=cols[:, bass.ds(c + B_A, 1)], in1=sig[b][:, start:start + n],
                                                        op0=ALU.add, op1=ALU.mult)
                    last.then_inc(glu_done, 1)
                    eng.drain()
                    out = mixed[:, bass.ds(c, 1), :].rearrange("p a n -> p (a n)")
                    tap = taps[:, bass.ds(c, 1), :].rearrange("p a k -> p (a k)")
                    done(eng, eng.tensor_scalar(out, glu[b][:, 0:OUT_LEN], tap[:, 0:1], cols[:, bass.ds(c + DW_B, 1)], ALU.mult, ALU.add))
                    for k in range(1, CONV_K):
                        last = done(eng, eng.scalar_tensor_tensor(out=out, in0=glu[b][:, k:k + OUT_LEN], scalar=tap[:, k:k + 1], in1=out,
                                                                  op0=ALU.mult, op1=ALU.add))
                    last.then_inc(conv_done, 1)

            eng.wait_ge(sq_used, KD)
            eng.tensor_scalar(rstd[:, 0, :], psum[2][:, 0:T], 1.0 / D, EPS, ALU.mult, ALU.add).then_inc(var_done, 1)
            eng.wait_ge(csd_done, 1)
            done(eng, eng.reciprocal(rstd[:, 0, :], rstd[:, 1, :]))
            for c in range(KD):
                for start, n, at in SEGMENTS:
                    last = eng.tensor_tensor(mixed[:, c, at:at + n], mixed[:, c, at:at + n], rstd[:, 0, start:start + n], ALU.mult)
                last.then_inc(scaled, 1)

            eng.wait_ge(w_out_in, 16 * (KD + 1))
            for tile in range(TILES):
                g, tmp = group_of(tile), x[tile % 2][:, :]
                eng.wait_ge(out_mm, tile + 1)
                eng.tensor_tensor(tmp, psum[tile % 2][:, :], b_out[:, :], ALU.add).then_inc(out_used, 1)
                eng.drain()
                done(eng, eng.tensor_tensor(tmp, tmp, gate[g][:, :], ALU.mult))
                eng.tensor_tensor(h[:, tile, :], h[:, tile, :], tmp, ALU.add)

        @block.scalar
        def _(eng):
            for tile in range(TILES):
                if tile >= 2:
                    eng.wait_ge(xT_tr, 2 * (tile - 1))
                eng.activation(x[tile % 2][:, :], h[:, tile, :], ACT.Square, accum_out=rms[:, tile, 0:1]).then_inc(ssq_done, 1)
                eng.wait_ge(rms_done, tile + 1)
                eng.activation(rms[:, tile, 2:3], rms[:, tile, 1:2], ACT.Sqrt).then_inc(std_done, 1)
                for half in range(2):
                    eng.wait_ge(xT_tr, 2 * tile + half + 1)
                    eng.activation(xT[:, 4 * half:4 * half + 4, tile * P:(tile + 1) * P],
                                   psum[half][:, 0:BANK].rearrange("p (k t) -> p k t", k=4), ACT.Copy).then_inc(xT_ready, 1)
                if tile == 0:
                    eng.wait_ge(small_tr, 1)
                    eng.activation(cols[:, :], small_ps[:, 0:32], ACT.Copy).then_inc(small_ev, 1)
                    eng.activation(taps[:, :, :], small_ps[:, BANK:BANK + KD * 32].rearrange("p (c k) -> p c k", c=KD)[:, :, 0:CONV_K], ACT.Copy).then_inc(small_ev, 1)
            eng.drain()
            with eng.Fori(0, KD // 2) as i:
                for b in range(2):
                    c = 2 * i + b
                    eng.wait_ge(ag_mm, c + 1)
                    eng.wait_ge(glu_done, c + 1)
                    eng.activation(sig[b][:, :], g_ps[b][:, 0:T], ACT.Sigmoid, bias=cols[:, bass.ds(c + B_A + KD, 1)]).then_inc(sig_done, 1)
            for c in range(KD):
                eng.wait_ge(conv_done, c + 1)
                if c >= 2:
                    eng.wait_ge(sq_used, c - 1)
                eng.activation(square[c % 2][:, :], mixed[:, c, :], ACT.Square).then_inc(sq_done, 1)
            eng.wait_ge(var_done, 1)
            eng.activation(rstd[:, 1, :], rstd[:, 0, :], ACT.Sqrt).then_inc(csd_done, 1)
            for c in range(KD):
                eng.wait_ge(scaled, c + 1)
                for start, n, at in SEGMENTS:
                    last = eng.activation(xT[:, c, start:start + n], mixed[:, c, at:at + n], ACT.Silu, scale=cols[:, NORM_G + c:NORM_G + c + 1])
                last.then_inc(swish_done, 1)

        @block.tensor
        def _(eng):
            for tile in range(TILES):
                eng.wait_ge(x_ready, tile + 1)
                for half in range(2):
                    if tile:
                        eng.wait_ge(xT_ready, 2 * tile - 1 + half)
                    for k in range(4):
                        last = eng.transpose(psum[half][:, k * P:(k + 1) * P], x[tile % 2][:, (4 * half + k) * P:(4 * half + k + 1) * P], ident[:, :])
                    last.then_inc(xT_tr, 1)
                if tile == 0:
                    eng.wait_ge(small_in, 64)
                    eng.transpose(small_ps[:, 0:32], rows[:, :], ident[0:32, 0:32])
                    for c in range(KD):
                        last = eng.transpose(small_ps[:, BANK + c * 32:BANK + c * 32 + CONV_K], taps_rows[:, c * P:(c + 1) * P], ident[0:CONV_K, 0:CONV_K])
                    last.then_inc(small_tr, 1)
            eng.wait_ge(xT_ready, 2 * TILES)
            eng.wait_ge(small_ev, 2)
            with eng.Fori(0, KD // 2) as i:
                for b in range(2):
                    c = 2 * i + b
                    eng.wait_ge(w_in[b], 32 * i + 32)
                    eng.wait_ge(glu_done, c + 1)
                    for half, ps in ((0, a_ps[b]), (1, g_ps[b])):
                        for start, n, _ in SEGMENTS:
                            for k in range(KD):
                                last = eng.matmul(ps[:, start:start + n], w_ag[b][:, half, k, :], xT[:, k, start:start + n],
                                                  start=(k == 0), stop=(k == KD - 1))
                    last.then_inc(ag_mm, 1)
            eng.wait_ge(ones_made, 1)
            for c in range(KD):
                eng.wait_ge(sq_done, c + 1)
                for start, n, at in SEGMENTS:
                    last = eng.matmul(psum[2][:, start:start + n], ones[:, :], square[c % 2][:, at:at + n], start=(c == 0), stop=(c == KD - 1))
                last.then_inc(sq_used, 1)
            eng.wait_ge(swish_done, KD)
            eng.wait_ge(w_out_in, 16 * (KD + 1))
            for tile in range(TILES):
                if tile >= 2:
                    eng.wait_ge(out_used, tile - 1)
                for half in range(2):
                    for k in range(KD):
                        last = eng.matmul(psum[tile % 2][:, half * BANK:(half + 1) * BANK], xT[:, k, tile * P:(tile + 1) * P],
                                          w_out[:, k, half * BANK:(half + 1) * BANK], start=(k == 0), stop=(k == KD - 1))
                last.then_inc(out_mm, 1)


def attention_stage(nc, dram, layer, j, h, ident, mod_rows, ckv_out, kpe_out):
    HALVES, HH = 2, HEADS // 2
    CACHE_KT, PROMPT_KT = SAMPLE_TILES, SAMPLE_TILES + 1
    KEY_TILES = SAMPLE_TILES + 2
    KV_W = NOPE + VH
    SCALE = float(QK) ** -0.5
    KQ, KL = Q_LORA // P, KV_LORA // P

    def group_of(tile):
        return 1 if tile == TILES - 1 else 0

    def key_tile(tile):
        return PROMPT_KT if tile == TILES - 1 else tile

    def keys_of(tile):
        return (PROMPT_KT * P, P) if tile == TILES - 1 else (0, (SAMPLE_TILES + 1) * P)

    with ExitStack() as ctx:
        def sb(name, shape, dt=F32):
            return ctx.enter_context(nc.sbuf_tensor(f"attn_{name}", shape, dt))

        sems = []

        def sem(name):
            sems.append(ctx.enter_context(nc.semaphore(f"a_{name}")))
            return sems[-1]

        wide = sb("wide", [P, 5 * D])
        gain = [wide[:, g * D:(g + 1) * D] for g in range(2)]
        shift = [wide[:, (2 + g) * D:(3 + g) * D] for g in range(2)]
        gate = [sb(f"gate{g}", [P, D]) for g in range(2)]
        q_a = sb("q_a", [P, KD, Q_LORA])
        kv_a = sb("kv_a", [P, KD, KV_LORA + ROPE])
        half_w = sb("half_w", [P, KQ * HH * QK + KL * HH * KV_W])
        q_b = half_w[:, 0:KQ * HH * QK].rearrange("p (k n) -> p k n", k=KQ)
        kv_b = half_w[:, KQ * HH * QK:].rearrange("p (k n) -> p k n", k=KL)
        o_w = [sb("o_w", [P, KD, BANK])[:, :, :], half_w[:, 0:KD * BANK].rearrange("p (k n) -> p k n", k=KD)]
        q_a_norm = sb("q_a_norm", [P, Q_LORA])
        kv_a_norm = sb("kv_a_norm", [P, KV_LORA])
        qk_gain = sb("qk_gain", [P, 2, QK])
        cos = sb("cos", [P, SAMPLE_TILES, ROPE // 2])
        sin = sb("sin", [P, SAMPLE_TILES, ROPE // 2])
        rms = sb("rms", [P, TILES, 12])
        lat_q = [sb(f"lat_q{b}", [P, Q_LORA]) for b in range(2)]
        lat_kv = [sb(f"lat_kv{b}", [P, KV_LORA]) for b in range(2)]
        latT_q = sb("latT_q", [P, TILES, KQ, P])
        latT_kv = sb("latT_kv", [P, KEY_TILES, KL, P])
        kpe = sb("kpe", [P, KEY_TILES, ROPE])
        heads_sb = [sb(f"heads{b}", [P, HH, QK]) for b in range(2)]
        heads_sq = [sb(f"heads_sq{b}", [P, HH, QK]) for b in range(2)]
        head_ms = [sb(f"head_ms{b}", [P, 3, HH]) for b in range(2)]
        rope_tmp = sb("rope_tmp", [P, 4, HH, ROPE // 2])
        kT = sb("kT", [QK, HH, KEY_TILES * P])
        qT = wide[0:QK, :].rearrange("p (t n q) -> p t n q", t=TILES, n=HH)
        v = sb("v", [P, KEY_TILES, HH, VH])
        probs = [sb(f"probs{b}", [P, 5 * P]) for b in range(2)]
        probsT = [sb(f"probsT{b}", [P, 5, P]) for b in range(2)]
        neg_max = [sb(f"neg_max{b}", [P, 2]) for b in range(2)]
        sums = [sb(f"sums{b}", [P, 2, HH]) for b in range(2)]
        out_a = q_a[:, :, :].rearrange("p k n -> p (k n)")
        out_heads = [out_a[:, t * D:(t + 1) * D] for t in range(4)] + [kv_a[:, :, :].rearrange("p k n -> p (k n)")[:, 0:D]]
        v_flat = v[:, :, :, :].rearrange("p a n w -> p (a n w)")
        x = [wide[:, 4 * D:5 * D], v_flat[:, 0:D]]
        xT = [sb("xT", [P, KD, P])[:, :, :], v_flat[:, D:2 * D].rearrange("p (k t) -> p k t", k=KD)]
        cache_kv = v_flat[:, 2 * D:2 * D + KV_LORA]

        def bank_pair(name):
            return ctx.enter_context(nc.psum_tensor(f"attn_{name}", [P, 2 * BANK], F32))

        ps_a, ps_b, ps_c, ps_d = (bank_pair(n) for n in "abcd")
        ps_ab, ps_cd = (ps_a, ps_b), (ps_c, ps_d)

        vec_in = [sem(f"vec_in{g}") for g in range(2)]
        lat_w_in, small_in, cache_in = (sem(n) for n in ("lat_w", "small_in", "cache_in"))
        ow_in = [sem(f"ow_in{b}") for b in range(2)]
        half_w_in, half_w_used = sem("half_w"), sem("half_w_used")
        ssq_done, std_done, rms_done, x_ready, xT_tr, xT_ready = (sem(n) for n in ("ssq", "std", "rms", "x_ready", "xT_tr", "xT_ready"))
        lat_mm, lat_sq, lat_ms, lat_std, lat_ready, lat_tr, lat_ev = (sem(n) for n in ("lat_mm", "lat_sq", "lat_ms", "lat_std", "lat_ready", "lat_tr", "lat_ev"))
        new_stored, gains_made = sem("new_stored"), sem("gains")
        hd_mm, hd_sq, v_copied, hd_ms, hd_std, hd_scaled, hd_ready, hd_tr, hd_ev = (sem(n) for n in ("hd_mm", "hd_sq", "v_cp", "hd_ms", "hd_std", "hd_scaled", "hd_ready", "hd_tr", "hd_ev"))
        s_mm, max_done, exp_done, p_tr, p_ev, pv_mm, o_used = (sem(n) for n in ("s_mm", "max", "exp", "p_tr", "p_ev", "pv", "o_used"))
        oT_tr, oT_ev, out_mm, out_used = (sem(n) for n in ("oT_tr", "oT_ev", "out_mm", "out_used"))

        ctx.callback(clear_semaphores, nc, sems)
        block = ctx.enter_context(nc.Block())
        STEPS = KEY_TILES + TILES
        RUNS = TILES * HH

        @block.sync
        def _(eng):
            eng.dma_start(x[1], dram["norm1_g"][layer:layer + 1, :].broadcast_to([P, D])).then_inc(vec_in[0], 16)
            for g in range(2):
                for dst, part in ((gain, 1), (shift, 0)):
                    eng.dma_start(dst[g], mod_rows[layer, g:g + 1, part * D:(part + 1) * D].broadcast_to([P, D])).then_inc(vec_in[g], 16)
                if g == 0:
                    eng.dma_start(q_a[:, :, :], dram["q_a_w"][j].rearrange("(k p) n -> p k n", p=P)).then_inc(lat_w_in, 16)
                    eng.dma_start(kv_a[:, :, :], dram["kv_a_w"][j].rearrange("(k p) n -> p k n", p=P)).then_inc(lat_w_in, 16)
                    eng.dma_start(q_a_norm[:, :], dram["q_a_norm"][j:j + 1, :].broadcast_to([P, Q_LORA])).then_inc(small_in, 16)
                    eng.dma_start(kv_a_norm[:, :], dram["kv_a_norm"][j:j + 1, :].broadcast_to([P, KV_LORA])).then_inc(small_in, 16)
            eng.dma_start(qk_gain[:, 0, :], dram["q_norm"][j:j + 1, :].broadcast_to([P, QK])).then_inc(small_in, 16)
            eng.dma_start(qk_gain[:, 1, :], dram["k_norm"][j:j + 1, :].broadcast_to([P, QK])).then_inc(small_in, 16)
            eng.dma_start(cos[:, :, :], dram["rope_cos"].rearrange("(t p) f -> p t f", p=P)).then_inc(small_in, 16)
            eng.dma_start(sin[:, :, :], dram["rope_sin"].rearrange("(t p) f -> p t f", p=P)).then_inc(small_in, 16)
            eng.dma_start(cache_kv, dram["cache_ckv"][0, j]).then_inc(cache_in, 16)
            eng.dma_start(kpe[:, CACHE_KT, :], dram["cache_kpe"][0, j]).then_inc(cache_in, 16)

            def load_half(hh):
                eng.dma_start(kv_b, dram["kv_b_w"][j].rearrange("(k p) n -> p k n", p=P)[:, :, hh * HH * KV_W:(hh + 1) * HH * KV_W]).then_inc(half_w_in, 16)
                eng.dma_start(q_b, dram["q_b_w"][j].rearrange("(k p) n -> p k n", p=P)[:, :, hh * HH * QK:(hh + 1) * HH * QK]).then_inc(half_w_in, 16)

            def load_output(c):
                eng.dma_start(o_w[c], dram["o_w"][j].rearrange("(k p) n -> p k n", p=P)[:, :, c * BANK:(c + 1) * BANK]).then_inc(ow_in[c], 16)

            load_half(0)
            for g in range(2):
                eng.dma_start(gate[g][:, :], mod_rows[layer, g:g + 1, 2 * D:3 * D].broadcast_to([P, D])).then_inc(ow_in[0], 16)
            load_output(0)
            eng.wait_ge(lat_ready, TILES)
            eng.dma_start(ckv_out, lat_kv[(TILES - 1) % 2][:, :]).then_inc(new_stored, 16)
            eng.dma_start(kpe_out, kpe[:, PROMPT_KT, :]).then_inc(new_stored, 16)
            eng.wait_ge(half_w_used, 1)
            load_half(1)
            eng.wait_ge(half_w_used, 2)
            load_output(1)
            eng.wait_ge(new_stored, 32)

        @block.tensor
        def _(eng):
            def transpose_x(tile):
                eng.wait_ge(x_ready, tile + 1)
                for half in range(2):
                    if tile:
                        eng.wait_ge(xT_ready, 2 * tile - 1 + half)
                    for k in range(4 * half, 4 * half + 4):
                        last = eng.transpose(ps_c[:, k * P:(k + 1) * P], x[tile % 2][:, k * P:(k + 1) * P], ident[:, :])
                    last.then_inc(xT_tr, 1)

            def latents(tile):
                eng.wait_ge(xT_ready, 2 * tile + 2)
                if tile >= 2:
                    eng.wait_ge(lat_ready, tile - 1)
                out = ps_ab[tile % 2]
                for k in range(KD):
                    eng.matmul(out[:, 0:Q_LORA], xT[tile % 2][:, k, :], q_a[:, k, :], start=(k == 0), stop=(k == KD - 1))
                for k in range(KD):
                    last = eng.matmul(out[:, BANK:BANK + KV_LORA + ROPE], xT[tile % 2][:, k, :], kv_a[:, k, :], start=(k == 0), stop=(k == KD - 1))
                last.then_inc(lat_mm, 1)

            def transpose_latents(tile):
                eng.wait_ge(lat_ready, tile + 1)
                if tile:
                    eng.wait_ge(lat_ev, 2 * tile)
                for k in range(KQ):
                    eng.transpose(ps_d[:, k * P:(k + 1) * P], lat_q[tile % 2][:, k * P:(k + 1) * P], ident[:, :])
                for k in range(KL):
                    last = eng.transpose(ps_d[:, BANK + k * P:BANK + (k + 1) * P], lat_kv[tile % 2][:, k * P:(k + 1) * P], ident[:, :])
                last.then_inc(lat_tr, 1)

            transpose_x(0)
            eng.wait_ge(lat_w_in, 32)
            for tile in range(TILES):
                latents(tile)
                if tile + 1 < TILES:
                    transpose_x(tile + 1)
                if tile:
                    transpose_latents(tile - 1)
            transpose_latents(TILES - 1)
            eng.wait_ge(cache_in, 32)
            eng.wait_ge(lat_ev, 2 * TILES)
            for k in range(KL):
                last = eng.transpose(ps_d[:, BANK + k * P:BANK + (k + 1) * P], cache_kv[:, k * P:(k + 1) * P], ident[:, :])
            last.then_inc(lat_tr, 1)
            eng.wait_ge(lat_ev, 2 * TILES + 1)

            with eng.Fori(0, HALVES) as hh:
                def project(s):
                    out = ps_ab[s % 2]
                    if s >= 2:
                        eng.wait_ge(hd_scaled, hh * STEPS + s - 1)
                        eng.wait_ge(v_copied, hh * KEY_TILES + min(s - 1, KEY_TILES))
                    for c in range(2):
                        if s < KEY_TILES:
                            for k in range(KL):
                                last = eng.matmul(out[:, c * BANK:(c + 1) * BANK], latT_kv[:, s, k, :], kv_b[:, k, c * BANK:(c + 1) * BANK],
                                                  start=(k == 0), stop=(k == KL - 1))
                        else:
                            n = HH * QK // 2
                            for k in range(KQ):
                                last = eng.matmul(out[:, c * BANK:c * BANK + n], latT_q[:, s - KEY_TILES, k, :], q_b[:, k, c * n:(c + 1) * n],
                                                  start=(k == 0), stop=(k == KQ - 1))
                    last.then_inc(hd_mm, 1)

                def transpose_heads(s):
                    eng.wait_ge(hd_ready, hh * STEPS + s + 1)
                    if s >= 2:
                        eng.wait_ge(hd_ev, hh * STEPS + s - 1)
                    for n in range(HH):
                        last = eng.transpose(ps_cd[s % 2][0:QK, n * P:(n + 1) * P], heads_sb[s % 2][:, n, :], ident[:, :])
                    last.then_inc(hd_tr, 1)

                eng.wait_ge(half_w_in, 32 * hh + 32)
                project(0)
                for s in range(STEPS):
                    if s + 1 < STEPS:
                        project(s + 1)
                    transpose_heads(s)
                eng.wait_ge(hd_ev, hh * STEPS + STEPS)
                eng.sem_inc(half_w_used, 1)

                def scores(r):
                    tile, n = r // HH, r % HH
                    first_key, n_keys = keys_of(tile)
                    if r >= 2:
                        eng.wait_ge(exp_done, hh * RUNS + r - 1)
                    for c in range(0, n_keys, BANK):
                        m = min(BANK, n_keys - c)
                        last = eng.matmul(ps_ab[r % 2][:, c:c + m], qT[:, tile, n, :], kT[:, n, first_key + c:first_key + c + m], start=True, stop=True)
                    last.then_inc(s_mm, 1)

                def transpose_probs(r):
                    _, n_keys = keys_of(r // HH)
                    eng.wait_ge(exp_done, hh * RUNS + r + 1)
                    if r:
                        eng.wait_ge(p_ev, hh * RUNS + r)
                    for c in range(n_keys // P):
                        last = eng.transpose(ps_c[:, c * P:(c + 1) * P], probs[r % 2][:, c * P:(c + 1) * P], ident[:, :])
                    last.then_inc(p_tr, 1)

                def weigh_values(r):
                    tile, n = r // HH, r % HH
                    first_key, n_keys = keys_of(tile)
                    if n == 0 and tile >= 2:
                        eng.wait_ge(o_used, hh * TILES + tile - 1)
                    eng.wait_ge(p_ev, hh * RUNS + r + 1)
                    at = (tile % 2) * BANK + n * VH
                    for c in range(n_keys // P):
                        last = eng.matmul(ps_d[:, at:at + VH], probsT[r % 2][:, c, :], v[:, first_key // P + c, n, :],
                                          start=(c == 0), stop=(c == n_keys // P - 1))
                    last.then_inc(pv_mm, 1)

                scores(0)
                for r in range(RUNS):
                    if r + 1 < RUNS:
                        scores(r + 1)
                    transpose_probs(r)
                    if r:
                        weigh_values(r - 1)
                weigh_values(RUNS - 1)
                eng.wait_ge(o_used, hh * TILES + TILES)

            def transpose_outputs(tile):
                if tile >= 2:
                    eng.wait_ge(oT_ev, 2 * (tile - 1))
                for half in range(2):
                    for k in range(4 * half, 4 * half + 4):
                        last = eng.transpose(ps_cd[tile % 2][:, k * P:(k + 1) * P], out_heads[tile][:, k * P:(k + 1) * P], ident[:, :])
                    last.then_inc(oT_tr, 1)

            transpose_outputs(0)
            eng.wait_ge(ow_in[0], 48)
            eng.wait_ge(ow_in[1], 16)
            for tile in range(TILES):
                if tile + 1 < TILES:
                    transpose_outputs(tile + 1)
                eng.wait_ge(oT_ev, 2 * tile + 2)
                if tile >= 2:
                    eng.wait_ge(out_used, tile - 1)
                for c in range(2):
                    for k in range(KD):
                        last = eng.matmul(ps_ab[tile % 2][:, c * BANK:(c + 1) * BANK], xT[tile % 2][:, k, :], o_w[c][:, k, :], start=(k == 0), stop=(k == KD - 1))
                last.then_inc(out_mm, 1)

        @block.scalar
        def _(eng):
            def copy_xT(tile, dst, src, transposed, copied, older):
                for half in range(2):
                    eng.wait_ge(transposed, 2 * tile + half + 1)
                    if tile >= 2:
                        eng.wait_ge(older, tile - 1)
                    eng.activation(dst[:, 4 * half:4 * half + 4, :].rearrange("p k t -> p (k t)"),
                                   src[:, half * BANK:(half + 1) * BANK], ACT.Copy).then_inc(copied, 1)

            def norm(tile):
                if tile >= 2:
                    eng.wait_ge(xT_tr, 2 * (tile - 1))
                if tile == 1:
                    eng.wait_ge(gains_made, 1)
                eng.activation(x[tile % 2], h[:, tile, :], ACT.Square, accum_out=rms[:, tile, 0:1]).then_inc(ssq_done, 1)
                eng.wait_ge(rms_done, tile + 1)
                eng.activation(rms[:, tile, 2:3], rms[:, tile, 1:2], ACT.Sqrt).then_inc(std_done, 1)
                copy_xT(tile, xT[tile % 2], ps_c, xT_tr, xT_ready, lat_mm)

            def square_latents(tile):
                eng.wait_ge(lat_mm, tile + 1)
                if tile >= 2:
                    eng.wait_ge(lat_tr, tile - 1)
                eng.activation(lat_q[tile % 2][:, :], ps_ab[tile % 2][:, 0:Q_LORA], ACT.Square, accum_out=rms[:, tile, 4:5]).then_inc(lat_sq, 1)
                eng.activation(lat_kv[tile % 2][:, :], ps_ab[tile % 2][:, BANK:BANK + KV_LORA], ACT.Square, accum_out=rms[:, tile, 5:6]).then_inc(lat_sq, 1)
                eng.wait_ge(lat_ms, tile + 1)
                eng.activation(rms[:, tile, 8:10], rms[:, tile, 6:8], ACT.Sqrt).then_inc(lat_std, 1)

            def copy_latents(tile):
                eng.wait_ge(lat_tr, tile + 1)
                eng.activation(latT_q[:, tile, :, :].rearrange("p k t -> p (k t)"), ps_d[:, 0:Q_LORA], ACT.Copy).then_inc(lat_ev, 1)
                eng.activation(latT_kv[:, key_tile(tile), :, :].rearrange("p k t -> p (k t)"), ps_d[:, BANK:BANK + KV_LORA], ACT.Copy).then_inc(lat_ev, 1)

            norm(0)
            for tile in range(TILES):
                if tile + 1 < TILES:
                    norm(tile + 1)
                if tile:
                    copy_latents(tile - 1)
                square_latents(tile)
            copy_latents(TILES - 1)
            eng.wait_ge(lat_tr, TILES + 1)
            eng.activation(latT_kv[:, CACHE_KT, :, :].rearrange("p k t -> p (k t)"), ps_d[:, BANK:BANK + KV_LORA], ACT.Copy).then_inc(lat_ev, 1)

            with eng.Fori(0, HALVES) as hh:
                def square_heads(s):
                    eng.wait_ge(hd_mm, hh * STEPS + s + 1)
                    if s < KEY_TILES:
                        heads = ps_ab[s % 2][:, :].rearrange("p (n w) -> p n w", n=HH)
                        eng.activation(heads_sq[s % 2][:, :, 0:NOPE], heads[:, :, 0:NOPE], ACT.Square)
                        eng.activation(heads_sq[s % 2][:, :, NOPE:QK], kpe[:, s, :].unsqueeze(1).broadcast_to([P, HH, ROPE]), ACT.Square).then_inc(hd_sq, 1)
                        eng.activation(v[:, s, :, :], heads[:, :, NOPE:KV_W], ACT.Copy).then_inc(v_copied, 1)
                    else:
                        eng.activation(heads_sq[s % 2][:, :, :].rearrange("p (c n) w -> p c (n w)", c=2),
                                       ps_ab[s % 2][:, :].rearrange("p (c n) -> p c n", c=2)[:, :, 0:HH * QK // 2], ACT.Square).then_inc(hd_sq, 1)

                def copy_heads(s):
                    eng.wait_ge(hd_tr, hh * STEPS + s + 1)
                    target = kT[:, :, s * P:(s + 1) * P] if s < KEY_TILES else qT[:, s - KEY_TILES, :, :]
                    eng.activation(target, ps_cd[s % 2][0:QK, :].rearrange("p (n t) -> p n t", n=HH), ACT.Copy).then_inc(hd_ev, 1)

                square_heads(0)
                for s in range(STEPS):
                    eng.wait_ge(hd_ms, hh * STEPS + s + 1)
                    eng.activation(head_ms[s % 2][:, 2, :], head_ms[s % 2][:, 1, :], ACT.Sqrt).then_inc(hd_std, 1)
                    if s + 1 < STEPS:
                        square_heads(s + 1)
                    if s:
                        copy_heads(s - 1)
                copy_heads(STEPS - 1)

                def exponentials(r):
                    _, n_keys = keys_of(r // HH)
                    eng.wait_ge(max_done, hh * RUNS + r + 1)
                    if r >= 2:
                        eng.wait_ge(p_tr, hh * RUNS + r - 1)
                    eng.activation(probs[r % 2][:, 0:n_keys], ps_ab[r % 2][:, 0:n_keys], ACT.Exp, bias=neg_max[r % 2][:, 1:2],
                                   scale=SCALE, accum_out=sums[(r // HH) % 2][:, 0, r % HH:r % HH + 1]).then_inc(exp_done, 1)

                def copy_probs(r):
                    _, n_keys = keys_of(r // HH)
                    eng.wait_ge(p_tr, hh * RUNS + r + 1)
                    if r >= 2:
                        eng.wait_ge(pv_mm, hh * RUNS + r - 1)
                    eng.activation(probsT[r % 2][:, 0:n_keys // P, :].rearrange("p c t -> p (c t)"), ps_c[:, 0:n_keys], ACT.Copy).then_inc(p_ev, 1)

                exponentials(0)
                for r in range(RUNS):
                    if r + 1 < RUNS:
                        tile = (r + 1) // HH
                        if (r + 1) % HH == 0 and tile >= 2:
                            eng.wait_ge(o_used, hh * TILES + tile - 1)
                        exponentials(r + 1)
                    copy_probs(r)

            for tile in range(TILES):
                copy_xT(tile, xT[tile % 2], ps_cd[tile % 2], oT_tr, oT_ev, out_mm)

        @block.vector
        def _(eng):
            def make_gain(g):
                eng.wait_ge(vec_in[g], 48 if g == 0 else 32)
                return eng.scalar_tensor_tensor(out=gain[g], in0=gain[g], scalar=1.0, in1=x[1], op0=ALU.add, op1=ALU.mult)

            def norm(tile):
                g, xb = group_of(tile), x[tile % 2]
                eng.wait_ge(ssq_done, tile + 1)
                eng.tensor_scalar(rms[:, tile, 1:2], rms[:, tile, 0:1], 1.0 / D, EPS, ALU.mult, ALU.add).then_inc(rms_done, 1)
                eng.wait_ge(std_done, tile + 1)
                done(eng, eng.reciprocal(rms[:, tile, 3:4], rms[:, tile, 2:3]))
                done(eng, eng.scalar_tensor_tensor(out=xb, in0=h[:, tile, :], scalar=rms[:, tile, 3:4], in1=gain[g], op0=ALU.mult, op1=ALU.mult))
                eng.tensor_tensor(xb, xb, shift[g], ALU.add).then_inc(x_ready, 1)

            def latents(tile):
                ps, b = ps_ab[tile % 2], tile % 2
                eng.wait_ge(lat_sq, 2 * tile + 2)
                eng.tensor_scalar(rms[:, tile, 6:7], rms[:, tile, 4:5], 1.0 / Q_LORA, EPS, ALU.mult, ALU.add)
                eng.tensor_scalar(rms[:, tile, 7:8], rms[:, tile, 5:6], 1.0 / KV_LORA, EPS, ALU.mult, ALU.add).then_inc(lat_ms, 1)
                eng.tensor_copy(kpe[:, key_tile(tile), :], ps[:, BANK + KV_LORA:BANK + KV_LORA + ROPE])
                eng.wait_ge(lat_std, tile + 1)
                done(eng, eng.reciprocal(rms[:, tile, 10:12], rms[:, tile, 8:10]))
                eng.scalar_tensor_tensor(out=lat_q[b][:, :], in0=ps[:, 0:Q_LORA], scalar=rms[:, tile, 10:11], in1=q_a_norm[:, :], op0=ALU.mult, op1=ALU.mult)
                eng.scalar_tensor_tensor(out=lat_kv[b][:, :], in0=ps[:, BANK:BANK + KV_LORA], scalar=rms[:, tile, 11:12], in1=kv_a_norm[:, :],
                                         op0=ALU.mult, op1=ALU.mult).then_inc(lat_ready, 1)

            make_gain(0)
            eng.drain()
            norm(0)
            make_gain(1).then_inc(gains_made, 1)
            eng.wait_ge(small_in, 16 * 6)
            for tile in range(TILES):
                if tile + 1 < TILES:
                    norm(tile + 1)
                latents(tile)
            eng.drain()

            def over_heads(row):
                return row.unsqueeze(1).broadcast_to([P, HH, row.shape[1]])

            def over_dims(col, n):
                return col.unsqueeze(2).broadcast_to([P, HH, n])

            with eng.Fori(0, HALVES) as hh:
                for s in range(STEPS):
                    is_key, ps, out, ms = s < KEY_TILES, ps_ab[s % 2], heads_sb[s % 2], head_ms[s % 2]
                    eng.wait_ge(hd_sq, hh * STEPS + s + 1)
                    done(eng, eng.tensor_reduce(ms[:, 0, :], heads_sq[s % 2][:, :, :], AX.X, ALU.add))
                    eng.tensor_scalar(ms[:, 1, :], ms[:, 0, :], 1.0 / QK, EPS, ALU.mult, ALU.add).then_inc(hd_ms, 1)
                    eng.wait_ge(hd_std, hh * STEPS + s + 1)
                    done(eng, eng.reciprocal(ms[:, 0, :], ms[:, 2, :]))
                    if s >= 2:
                        eng.wait_ge(hd_tr, hh * STEPS + s - 1)
                    if is_key:
                        eng.tensor_tensor(out[:, :, NOPE:QK], over_heads(kpe[:, s, :]), over_dims(ms[:, 0, :], ROPE), ALU.mult)
                        eng.tensor_tensor(out[:, :, 0:NOPE], ps[:, :].rearrange("p (n w) -> p n w", n=HH)[:, :, 0:NOPE],
                                          over_dims(ms[:, 0, :], NOPE), ALU.mult).then_inc(hd_scaled, 1)
                    else:
                        for c in range(2):
                            m = HH // 2
                            last = eng.tensor_tensor(out[:, c * m:(c + 1) * m, :], ps[:, c * BANK:c * BANK + m * QK].rearrange("p (n w) -> p n w", n=m),
                                                     ms[:, 0, c * m:(c + 1) * m].unsqueeze(2).broadcast_to([P, m, QK]), ALU.mult)
                        last.then_inc(hd_scaled, 1)
                    eng.drain()
                    tile = s if is_key else s - KEY_TILES
                    ready = eng.tensor_tensor(out[:, :, :], out[:, :, :], over_heads(qk_gain[:, int(is_key), :]), ALU.mult)
                    if tile < SAMPLE_TILES:
                        eng.drain()
                        pairs = out[:, :, NOPE:QK].rearrange("p n (f two) -> p n f two", two=2)
                        x1, x2 = pairs[:, :, :, 0], pairs[:, :, :, 1]
                        c, d = over_heads(cos[:, tile, :]), over_heads(sin[:, tile, :])
                        eng.tensor_tensor(rope_tmp[:, 0, :, :], x1, c, ALU.mult)
                        eng.tensor_tensor(rope_tmp[:, 1, :, :], x2, d, ALU.mult)
                        eng.tensor_tensor(rope_tmp[:, 2, :, :], x1, d, ALU.mult)
                        done(eng, eng.tensor_tensor(rope_tmp[:, 3, :, :], x2, c, ALU.mult))
                        eng.tensor_tensor(x1, rope_tmp[:, 0, :, :], rope_tmp[:, 1, :, :], ALU.subtract)
                        ready = eng.tensor_tensor(x2, rope_tmp[:, 2, :, :], rope_tmp[:, 3, :, :], ALU.add)
                    ready.then_inc(hd_ready, 1)
                    eng.drain()

                def finish_heads(tile):
                    eng.wait_ge(pv_mm, hh * RUNS + (tile + 1) * HH)
                    done(eng, eng.reciprocal(sums[tile % 2][:, 1, :], sums[tile % 2][:, 0, :]))
                    eng.tensor_tensor(out_heads[tile][:, bass.ds(hh * (HH * VH), HH * VH)].rearrange("p (n w) -> p n w", n=HH),
                                      ps_d[:, (tile % 2) * BANK:(tile % 2 + 1) * BANK].rearrange("p (n w) -> p n w", n=HH),
                                      over_dims(sums[tile % 2][:, 1, :], VH), ALU.mult).then_inc(o_used, 1)

                for r in range(RUNS):
                    _, n_keys = keys_of(r // HH)
                    eng.wait_ge(s_mm, hh * RUNS + r + 1)
                    done(eng, eng.tensor_reduce(neg_max[r % 2][:, 0:1], ps_ab[r % 2][:, 0:n_keys], AX.X, ALU.max))
                    eng.tensor_scalar(neg_max[r % 2][:, 1:2], neg_max[r % 2][:, 0:1], -SCALE, None, ALU.mult).then_inc(max_done, 1)
                    if r % HH == 2 and r > HH:
                        finish_heads(r // HH - 1)
                finish_heads(TILES - 1)

            eng.wait_ge(ow_in[0], 48)
            for tile in range(TILES):
                tmp = heads_sq[tile % 2][:, :, :].rearrange("p n w -> p (n w)")[:, 0:BANK]
                eng.wait_ge(out_mm, tile + 1)
                for c in range(2):
                    cols = slice(c * BANK, (c + 1) * BANK)
                    last = eng.tensor_tensor(tmp, ps_ab[tile % 2][:, cols], gate[group_of(tile)][:, cols], ALU.mult)
                    if c == 1:
                        last.then_inc(out_used, 1)
                    eng.drain()
                    done(eng, eng.tensor_tensor(h[:, tile, cols], h[:, tile, cols], tmp, ALU.add))


def peer_stage(nc, dram, layer, h, ident, mod_rows, y_out):
    wq = dram["peer_wq"][layer].rearrange("(k p) n -> p k n", p=P)
    u_rows, v_rows = (dram[n].rearrange("l e d -> (l e) d") for n in ("peer_u", "peer_v"))
    first_row = layer * N_KEYS * N_KEYS
    with ExitStack() as ctx:
        def sb(name, shape, dt=F32):
            return ctx.enter_context(nc.sbuf_tensor(f"peer{layer}_{name}", shape, dt))

        def pb(name, shape, dt=F32):
            return ctx.enter_context(nc.psum_tensor(f"peer{layer}_{name}", shape, dt))

        sems = []

        def sem(name):
            sems.append(ctx.enter_context(nc.semaphore(f"p{layer}_{name}")))
            return sems[-1]

        wq_sb = sb("wq", [P, KD, PEER_HEADS * PEER_QDIM])
        u_ring = [sb(f"u{k}", [P, D]) for k in range(RING)]
        v_ring = [sb(f"v{k}", [P, D]) for k in range(RING)]
        x = [sb(f"x{b}", [P, D]) for b in range(2)]
        xT = sb("xT", [P, KD, P])
        product = sb("product", [P, D], BF16)
        gain = [sb(f"gain{g}", [P, D]) for g in range(2)]
        shift = [sb(f"shift{g}", [P, D]) for g in range(2)]
        gate = [sb(f"gate{g}", [P, D]) for g in range(2)]
        keys_sb = sb("keys", [P, 2, P])
        keysT = sb("keysT", [P, 2, P])
        iota = sb("iota", [P, TOPK])
        zeros = sb("zeros", [P, HALF_BANK * 2], BF16)
        rms = sb("rms", [P, 4])
        q_sb = sb("q", [P, 2 * P])
        qT_sb = sb("qT", [P, 2, P])
        s_sb = sb("s", [P, 2, P])
        s_rest = sb("s_rest", [P, 2, P])
        top = sb("top", [P, 2, TOPK])
        top_at = sb("top_at", [P, 2, TOPK], U32)
        top_atf = sb("top_atf", [P, 2, TOPK])
        cand = sb("cand", [P, TOPK * TOPK])
        cand_rest = sb("cand_rest", [P, TOPK * TOPK])
        best = sb("best", [P, TOPK])
        best_at = sb("best_at", [P, TOPK], U32)
        side_at = sb("side_at", [P, TOPK, 2], U32)
        one_hot = sb("one_hot", [P, TOPK, 2, TOPK])
        picked = sb("picked", [P, TOPK, 2])
        expert = [sb(f"expert{b}", [P, TOPK], I32) for b in range(2)]
        neg_max = sb("neg_max", [P, 1])
        exps = [sb(f"exps{b}", [P, TOPK]) for b in range(2)]
        exp_sum = [sb(f"exp_sum{b}", [P, 1]) for b in range(2)]
        inv_sum = sb("inv_sum", [P, 1])
        dots = [sb(f"dots{b}", [P, RING]) for b in range(2)]
        gelus = [sb(f"gelus{b}", [P, RING]) for b in range(2)]
        weight = [sb(f"weight{b}", [P, RING]) for b in range(2)]
        diag = [sb(f"diag{b}", [P, P]) for b in range(DIAGS)]

        acc = pb("acc", [P, D])
        q_ps = pb("q_ps", [P, HALF_BANK * 2])
        qT_ps = pb("qT_ps", [P, HALF_BANK * 2])
        s_ps = pb("s_ps", [P, HALF_BANK * 2])
        xT_ps = pb("xT_ps", [P, KD, P])

        wq_in, keys_in, gain_in, mod_in = sem("wq_in"), sem("keys_in"), sem("gain_in"), sem("mod_in")
        gains_made, consts = sem("gains_made"), sem("consts")
        keys_tr, keys_ev = sem("keys_tr"), sem("keys_ev")
        ssq_done, std_done, rms_done = sem("ssq"), sem("std"), sem("rms")
        x_ready, xT_tr, xT_ready = sem("x_ready"), sem("xT_tr"), sem("xT_ready")
        q_mm, q_ev, qT_tr, qT_ev, s_mm, s_ev = (sem(n) for n in ("q_mm", "q_ev", "qT_tr", "qT_ev", "s_mm", "s_ev"))
        best_done, exp_done, expert_done = sem("best"), sem("exp"), sem("expert")
        u_free, v_free = sem("u_free"), sem("v_free")
        gather_go = sem("gather_go")
        u_in = [sem(f"u_in{k}") for k in range(RING)]
        v_in = [sem(f"v_in{k}") for k in range(RING)]
        gelu_done, weight_done, diag_done = sem("gelu"), sem("weight"), sem("diag")
        acc_done, acc_used, y_done, y_stored = sem("acc_done"), sem("acc_used"), sem("y_done"), sem("y_st")

        ctx.callback(clear_semaphores, nc, sems)
        block = ctx.enter_context(nc.Block())

        @block.sync
        def _(eng):
            for side in range(2):
                eng.dma_start(keys_sb[:, side, :], dram["peer_keys"][layer, side]).then_inc(keys_in, 16)
            eng.dma_start(x[1][:, :], dram["norm2_g"][layer:layer + 1, :].broadcast_to([P, D])).then_inc(gain_in, 16)
            for g in range(2):
                for dst, part in ((shift, 3), (gain, 4), (gate, 5)):
                    eng.dma_start(dst[g][:, :], mod_rows[layer, g:g + 1, part * D:(part + 1) * D].broadcast_to([P, D])).then_inc(mod_in, 16)
            for k in range(KD):
                eng.dma_start(wq_sb[:, k, :], wq[:, k, :]).then_inc(wq_in, 16)
            if y_out is not None:
                for tile in range(TILES):
                    eng.wait_ge(y_done, tile + 1)
                    eng.dma_start(y_out[tile], h[:, tile, :]).then_inc(y_stored, 16)
                eng.wait_ge(y_stored, 16 * TILES)

        @block.gpsimd
        def _(eng):
            eng.iota(iota[:, :], [[1, TOPK]], base=0, channel_multiplier=0, allow_small_or_imprecise_dtypes=True).then_inc(consts, 1)
            eng.memset(zeros[:, :], 0.0).then_inc(consts, 1)
            eng.sem_inc(u_free, RING)
            eng.sem_inc(v_free, RING)

            def head(g, par):
                eng.wait_ge(expert_done, g + 1)
                eng.sem_inc(gather_go, 1)
                for half in range(2):
                    for rows, ring, free, landed in ((u_rows, u_ring, u_free, u_in), (v_rows, v_ring, v_free, v_in)):
                        for k in range(RING):
                            slot = half * RING + k
                            eng.wait_ge(free, g * TOPK + slot + 1)
                            eng.sem_inc(gather_go, 1)
                            eng.indirect_dma_start(
                                out=ring[k][:, :], out_offset=None, in_=rows,
                                in_offset=bass.IndirectOffsetOnAxis(ap=expert[par][:, slot:slot + 1], axis=0),
                            ).then_inc(landed[k], 16)

            with eng.Fori(0, TILES * PEER_HEADS // 2) as i:
                head(2 * i, 0)
                head(2 * i + 1, 1)

        def group_of(tile):
            return 1 if tile == TILES - 1 else 0

        @block.vector
        def _(eng):
            eng.wait_ge(gain_in, 16)
            eng.wait_ge(mod_in, 16 * 6)
            for g in range(2):
                ins = eng.scalar_tensor_tensor(out=gain[g][:, :], in0=gain[g][:, :], scalar=1.0, in1=x[1][:, :], op0=ALU.add, op1=ALU.mult)
                ins.then_inc(gains_made, 1)
            eng.wait_ge(gains_made, 2)

            def norm(tile):
                xb = x[tile % 2][:, :]
                eng.wait_ge(ssq_done, tile + 1)
                done(eng, eng.tensor_scalar(rms[:, 1:2], rms[:, 0:1], 1.0 / D, EPS, ALU.mult, ALU.add))
                eng.tensor_scalar(rms[:, 2:3], rms[:, 1:2], 1.0, None, ALU.mult).then_inc(rms_done, 1)
                eng.wait_ge(std_done, tile + 1)
                done(eng, eng.reciprocal(rms[:, 3:4], rms[:, 1:2]))
                done(eng, eng.scalar_tensor_tensor(out=xb, in0=h[:, tile, :], scalar=rms[:, 3:4], in1=gain[group_of(tile)][:, :], op0=ALU.mult, op1=ALU.mult))
                eng.tensor_tensor(xb, xb, shift[group_of(tile)][:, :], ALU.add).then_inc(x_ready, 1)
                eng.wait_ge(x_ready, tile + 1)

            def top16(values, rest, vals, at):
                done(eng, eng.max(vals[:, 0:8], values))
                done(eng, eng.match_replace(out=rest, in_to_replace=vals[:, 0:8], in_values=values, imm_value=LOWEST))
                eng.max_index(at[:, 0:8], vals[:, 0:8], values)
                done(eng, eng.max(vals[:, 8:16], rest))
                done(eng, eng.max_index(at[:, 8:16], vals[:, 8:16], rest))

            def route(r, par, first=False):
                eng.wait_ge(s_mm, r + 1)
                eng.tensor_copy(s_sb[:, :, :].rearrange("p s n -> p (s n)"), s_ps[:, 0:2 * P]).then_inc(s_ev, 1)
                eng.drain()
                for side in range(2):
                    top16(s_sb[:, side, :], s_rest[:, side, :], top[:, side, :], top_at[:, side, :])
                if not first:
                    eng.wait_ge(exp_done, r)
                eng.tensor_scalar(top_atf[:, 0, :], top_at[:, 0, :], float(N_KEYS), float(first_row), ALU.mult, ALU.add)
                done(eng, eng.tensor_copy(top_atf[:, 1, :], top_at[:, 1, :]))
                done(eng, eng.tensor_tensor(cand[:, :].rearrange("p (a b) -> p a b", a=TOPK),
                                           top[:, 0, :].unsqueeze(2).broadcast_to([P, TOPK, TOPK]),
                                           top[:, 1, :].unsqueeze(1).broadcast_to([P, TOPK, TOPK]), ALU.add))
                top16(cand[:, :], cand_rest[:, :], best[:, :], best_at[:, :])
                eng.tensor_scalar(neg_max[:, :], best[:, 0:1], -1.0, None, ALU.mult).then_inc(best_done, 1)
                done(eng, eng.tensor_scalar(side_at[:, :, 0], best_at[:, :], 4, None, ALU.logical_shift_right))
                done(eng, eng.tensor_scalar(side_at[:, :, 1], best_at[:, :], 15, None, ALU.bitwise_and))
                hot = one_hot[:, :, :, :].rearrange("p k s a -> p (k s) a")
                done(eng, eng.tensor_tensor(hot, iota[:, :].unsqueeze(1).broadcast_to([P, 2 * TOPK, TOPK]),
                                           side_at[:, :, :].rearrange("p k s -> p (k s)").unsqueeze(2).broadcast_to([P, 2 * TOPK, TOPK]),
                                           ALU.is_equal))
                done(eng, eng.tensor_tensor(one_hot[:, :, :, :].rearrange("p k s a -> p k (s a)"),
                                           one_hot[:, :, :, :].rearrange("p k s a -> p k (s a)"),
                                           top_atf[:, :, :].rearrange("p s a -> p (s a)").unsqueeze(1).broadcast_to([P, TOPK, 2 * TOPK]),
                                           ALU.mult))
                done(eng, eng.tensor_reduce(picked[:, :, :].rearrange("p k s -> p (k s)"), hot, AX.X, ALU.add))
                if not first:
                    eng.wait_ge(v_free, r * TOPK - TOPK + RING)
                eng.tensor_tensor(expert[par][:, :], picked[:, :, 0], picked[:, :, 1], ALU.add).then_inc(expert_done, 1)

            def half_head(g, par, half, b):
                for k in range(RING):
                    n = g * TOPK + half * RING + k
                    eng.wait_ge(u_in[k], (2 * g + half + 1) * 16)
                    eng.wait_ge(u_free, n + RING)
                    eng.tensor_tensor_reduce(out=product[:, :], in0=u_ring[k][:, :], in1=x[b][:, :], scale=1.0, scalar=0.0,
                                             op0=ALU.mult, op1=ALU.add, accum_out=dots[half][:, k:k + 1]).then_inc(u_free, 1)
                if half == 0:
                    eng.wait_ge(exp_done, g + 1)
                    done(eng, eng.reciprocal(inv_sum[:, :], exp_sum[par][:, :]))
                eng.wait_ge(gelu_done, 2 * g + half + 1)
                eng.scalar_tensor_tensor(out=weight[half][:, :], in0=gelus[half][:, :], scalar=inv_sum[:, :],
                                         in1=exps[par][:, half * RING:(half + 1) * RING],
                                         op0=ALU.mult, op1=ALU.mult).then_inc(weight_done, 1)
                eng.wait_ge(weight_done, 2 * g + half + 1)

            def finish_tile(tile):
                eng.wait_ge(acc_done, tile + 1)
                tmp = x[tile % 2][:, :]
                done(eng, eng.tensor_tensor(tmp, acc[:, :], gate[group_of(tile)][:, :], ALU.mult))
                eng.tensor_tensor(h[:, tile, :], h[:, tile, :], tmp, ALU.add).then_inc(y_done, 1)
                eng.wait_ge(y_done, tile + 1)

            eng.wait_ge(consts, 2)
            norm(0)
            route(0, 0, first=True)
            for tile in range(TILES):
                b = tile % 2
                if tile:
                    finish_tile(tile - 1)
                with eng.Fori(0, PEER_HEADS // 2 - 1) as i:
                    for par in range(2):
                        g = tile * PEER_HEADS + 2 * i + par
                        half_head(g, par, 0, b)
                        route(g + 1, 1 - par)
                        half_head(g, par, 1, b)
                for par in range(2):
                    g = tile * PEER_HEADS + PEER_HEADS - 2 + par
                    half_head(g, par, 0, b)
                    if g + 1 < TILES * PEER_HEADS:
                        route(g + 1, 1 - par)
                    half_head(g, par, 1, b)
                    if par == 0 and tile + 1 < TILES:
                        norm(tile + 1)
            finish_tile(TILES - 1)

        @block.scalar
        def _(eng):
            eng.wait_ge(keys_tr, 1)
            eng.activation(keysT[:, :, :].rearrange("p s n -> p (s n)"), qT_ps[:, 0:2 * P], ACT.Copy).then_inc(keys_ev, 1)

            def norm(tile):
                if tile == 1:
                    eng.wait_ge(gains_made, 2)
                eng.activation(x[tile % 2][:, :], h[:, tile, :], ACT.Square, accum_out=rms[:, 0:1]).then_inc(ssq_done, 1)
                eng.wait_ge(rms_done, tile + 1)
                eng.activation(rms[:, 1:2], rms[:, 2:3], ACT.Sqrt).then_inc(std_done, 1)
                for half in range(2):
                    eng.wait_ge(xT_tr, 2 * tile + half + 1)
                    eng.activation(xT[:, 4 * half:4 * half + 4, :].rearrange("p k t -> p (k t)"),
                                   xT_ps[:, 4 * half:4 * half + 4, :].rearrange("p k t -> p (k t)"), ACT.Copy).then_inc(xT_ready, 1)

            def route(r):
                eng.wait_ge(q_mm, r + 1)
                eng.activation(q_sb[:, :], q_ps[:, 0:2 * P], ACT.Copy).then_inc(q_ev, 1)
                eng.wait_ge(qT_tr, r + 1)
                eng.activation(qT_sb[:, :, :].rearrange("p s t -> p (s t)"), qT_ps[:, 0:2 * P], ACT.Copy).then_inc(qT_ev, 1)

            def softmax(r, par):
                eng.wait_ge(best_done, r + 1)
                eng.activation(exps[par][:, :], best[:, :], ACT.Exp, bias=neg_max[:, :], accum_out=exp_sum[par][:, :]).then_inc(exp_done, 1)

            def half_head(g, half):
                eng.wait_ge(u_free, g * TOPK + (half + 1) * RING + RING)
                eng.activation(gelus[half][:, :], dots[half][:, :], ACT.Gelu).then_inc(gelu_done, 1)
                eng.wait_ge(weight_done, 2 * g + half + 1)
                for k in range(RING):
                    n = g * TOPK + half * RING + k
                    eng.wait_ge(v_free, n - DIAGS + 1 + RING)
                    eng.activation(diag[k % DIAGS][:, :], ident[:, :], ACT.Copy, scale=weight[half][:, k:k + 1]).then_inc(diag_done, 1)

            norm(0)
            route(0)
            softmax(0, 0)
            for tile in range(TILES):
                with eng.Fori(0, PEER_HEADS // 2 - 1) as i:
                    for par in range(2):
                        g = tile * PEER_HEADS + 2 * i + par
                        route(g + 1)
                        half_head(g, 0)
                        softmax(g + 1, 1 - par)
                        half_head(g, 1)
                for par in range(2):
                    g = tile * PEER_HEADS + PEER_HEADS - 2 + par
                    more = g + 1 < TILES * PEER_HEADS
                    if more:
                        route(g + 1)
                    half_head(g, 0)
                    if more:
                        softmax(g + 1, 1 - par)
                    half_head(g, 1)
                    if par == 0 and tile + 1 < TILES:
                        norm(tile + 1)

        @block.tensor
        def _(eng):
            eng.wait_ge(keys_in, 32)
            for side in range(2):
                last = eng.transpose(qT_ps[:, side * P:(side + 1) * P], keys_sb[:, side, :], ident[:, :])
            last.then_inc(keys_tr, 1)
            eng.wait_ge(keys_ev, 1)

            def transpose_x(tile):
                eng.wait_ge(x_ready, tile + 1)
                for half in range(2):
                    if tile:
                        eng.wait_ge(xT_ready, 2 * tile - 1 + half)
                    for k in range(4 * half, 4 * half + 4):
                        last = eng.transpose(xT_ps[:, k, :], x[tile % 2][:, k * P:(k + 1) * P], ident[:, :])
                    last.then_inc(xT_tr, 1)

            def route(r, head, tile):
                if isinstance(head, int) and head == 0:
                    eng.wait_ge(xT_ready, 2 * tile + 2)
                first = isinstance(r, int) and r == 0
                if not first:
                    eng.wait_ge(q_ev, r)
                for k in range(KD):
                    last = eng.matmul(q_ps[:, 0:2 * P], xT[:, k, :], wq_sb[:, k, bass.ds(head * 2 * P, 2 * P)],
                                      start=(k == 0), stop=(k == KD - 1))
                last.then_inc(q_mm, 1)
                eng.wait_ge(q_ev, r + 1)
                if not first:
                    eng.wait_ge(qT_ev, r)
                for side in range(2):
                    last = eng.transpose(qT_ps[:, side * P:(side + 1) * P], q_sb[:, side * P:(side + 1) * P], ident[:, :])
                last.then_inc(qT_tr, 1)
                eng.wait_ge(qT_ev, r + 1)
                if not first:
                    eng.wait_ge(s_ev, r)
                for side in range(2):
                    last = eng.matmul(s_ps[:, side * P:(side + 1) * P], qT_sb[:, side, :], keysT[:, side, :], start=True, stop=True)
                last.then_inc(s_mm, 1)

            def half_head(g, half):
                for k in range(RING):
                    n = g * TOPK + half * RING + k
                    eng.wait_ge(v_in[k], (2 * g + half + 1) * 16)
                    eng.wait_ge(diag_done, n + 1)
                    for c in range(2):
                        last = eng.matmul(acc[:, c * BANK:(c + 1) * BANK], diag[k % DIAGS][:, :],
                                          v_ring[k][:, c * BANK:(c + 1) * BANK], start=False, stop=False)
                    last.then_inc(v_free, 1)

            def bound_sum(start):
                for c in range(2):
                    last = eng.matmul(acc[:, c * BANK:(c + 1) * BANK], zeros[:, 0:P], zeros[:, :], start=start, stop=not start)
                return last

            transpose_x(0)
            eng.wait_ge(consts, 2)
            eng.wait_ge(wq_in, 16 * KD)
            route(0, 0, 0)
            for tile in range(TILES):
                if tile:
                    eng.wait_ge(y_done, tile)
                bound_sum(True)
                with eng.Fori(0, PEER_HEADS // 2 - 1) as i:
                    for par in range(2):
                        g = tile * PEER_HEADS + 2 * i + par
                        route(g + 1, 2 * i + par + 1, tile)
                        half_head(g, 0)
                        half_head(g, 1)
                for par in range(2):
                    head = PEER_HEADS - 2 + par
                    g = tile * PEER_HEADS + head
                    if g + 1 < TILES * PEER_HEADS:
                        route(g + 1, (head + 1) % PEER_HEADS, tile + (head + 1) // PEER_HEADS)
                    half_head(g, 0)
                    half_head(g, 1)
                    if par == 0 and tile + 1 < TILES:
                        transpose_x(tile + 1)
                bound_sum(False).then_inc(acc_done, 1)
def build_program(nc, dram, outs):
    y_prompt, y_sample, new_ckv, new_kpe = outs
    mod_rows = nc.dram_tensor("modulation_rows", [DEPTH, 2, 6 * D], F32, kind="Internal").ap()
    with ExitStack() as ctx:
        h = ctx.enter_context(nc.sbuf_tensor("residual", [P, TILES, D], F32))
        ident = ctx.enter_context(nc.sbuf_tensor("identity", [P, P], F32))
        loaded = ctx.enter_context(nc.semaphore("loaded"))
        with nc.Block() as block:
            @block.sync
            def _(eng):
                eng.dma_start(h[:, 0:SAMPLE_TILES, :], dram["x_sample"][0].rearrange("(t p) d -> p t d", p=P)).then_inc(loaded, 16)
                eng.dma_start(h[:, SAMPLE_TILES, :], dram["x_prompt"][0]).then_inc(loaded, 16)
                eng.dma_start(ident[:, :], dram["identity"]).then_inc(loaded, 16)
                eng.wait_ge(loaded, 48)
        y_tiles = [y_sample[0, t * P:(t + 1) * P, :] for t in range(SAMPLE_TILES)] + [y_prompt[0]]
        modulation_stage(nc, dram, 0, mod_rows)
        conv_stage(nc, dram, 0, 0, h, ident, mod_rows)
        peer_stage(nc, dram, 0, h, ident, mod_rows, None)
        modulation_stage(nc, dram, 1, mod_rows)
        attention_stage(nc, dram, 1, 0, h, ident, mod_rows, new_ckv[0, 0], new_kpe[0, 0])
        peer_stage(nc, dram, 1, h, ident, mod_rows, y_tiles)


_INPUTS = ["x_prompt", "x_sample", "cache_ckv", "cache_kpe", "c", "c_ctx", "mod_w", "mod_b", "norm1_g", "norm2_g",
           "conv_w_in", "conv_b_in", "conv_dw", "conv_dw_b", "conv_norm_g", "conv_w_out", "conv_b_out",
           "q_a_w", "q_a_norm", "q_b_w", "kv_a_w", "kv_a_norm", "kv_b_w", "q_norm", "k_norm", "o_w",
           "peer_wq", "peer_keys", "peer_u", "peer_v"]
_OUTPUTS = [("y_prompt", (1, SEQ, D)), ("y_sample", (1, DEC_SEQ, D)), ("new_ckv", (1, 1, SEQ, KV_LORA)), ("new_kpe", (1, 1, SEQ, ROPE))]


def _shape_constants():
    import numpy as np

    half = ROPE // 2
    row = np.repeat(np.arange(DEC_SEQ // GRID_W), GRID_W).astype(np.float32)
    col = np.tile(np.arange(GRID_W), DEC_SEQ // GRID_W).astype(np.float32)
    inv = (np.float32(ROPE_THETA) ** (-(np.arange(half // 2, dtype=np.float32) * np.float32(2.0) / np.float32(half)))).astype(np.float32)
    angle = np.concatenate([row[:, None] * inv, col[:, None] * inv], axis=-1).astype(np.float32)
    return {"identity": np.eye(P, dtype=np.float32), "rope_cos": np.cos(angle).astype(np.float32), "rope_sin": np.sin(angle).astype(np.float32)}


def kernel(**inputs):
    import numpy as np
    import concourse.bacc as bacc
    from concourse.bass_utils import run_bass_kernel_spmd

    nc = bacc.Bacc("TRN2", target_bir_lowering=False, num_devices=1)
    arrays, dram = {}, {}
    given = {name: np.ascontiguousarray(inputs[name]) for name in _INPUTS}
    given.update(_shape_constants())
    for name, a in given.items():
        arrays[f"in_{name}"] = a
        dram[name] = nc.dram_tensor(f"in_{name}", a.shape, mybir.dt.from_np(a.dtype), kind="ExternalInput").ap()
    outs = [nc.dram_tensor(f"out_{name}", shape, F32, kind="ExternalOutput").ap() for name, shape in _OUTPUTS]
    build_program(nc, dram, outs)
    r = run_bass_kernel_spmd(nc, [arrays], core_ids=[0])
    return tuple(r.results[0][f"out_{name}"] for name, _ in _OUTPUTS)
```

```python
from contextlib import ExitStack

import numpy as np

import concourse.bass as bass
from concourse import mybir

F32, BF16, I32, U32 = mybir.dt.float32, mybir.dt.bfloat16, mybir.dt.int32, mybir.dt.uint32
ALU = mybir.AluOpType
ACT = mybir.ActivationFunctionType
AX = mybir.AxisListType

P = 128
BANK = 512
HALF_BANK = BANK // 2
D = 1024
KD = D // P
SEQ, DEC_SEQ, PAST_LEN = 128, 512, 128
SAMPLE_TILES = DEC_SEQ // P
TILES = SAMPLE_TILES + SEQ // P
GRID_W, ROPE_THETA, DEPTH = 64, 10000.0, 2
CONV_K = 31
PAD = CONV_K // 2
HEADS, NOPE, ROPE, VH = 16, 64, 32, 64
QK = NOPE + ROPE
Q_LORA, KV_LORA = 512, 256
PEER_HEADS, PEER_QDIM, N_KEYS, TOPK = 8, 256, 128, 16
EPS = 1e-6
LOWEST = -3.4028234663852886e38
RING = 8
DIAGS = 4
FIRST_MOD = 3 * D
MOD_PER_C = 3


def done(eng, ins):
    eng.drain()
    return ins


def clear_semaphores(nc, sems):
    with nc.Block() as block:
        @block.gpsimd
        def _(eng):
            for s in sems:
                eng.sem_clear(s)


class Shared:

    def __init__(self, nc, ctx):
        def sb(name, shape):
            return ctx.enter_context(nc.sbuf_tensor(name, shape, F32))

        self.h = sb("residual", [P, TILES, D])
        self.ident = sb("identity", [P, P])
        self.silu = sb("silu_conditioning", [P, 2, KD])
        self.wide = sb("wide", [P, 5 * D])
        self.wq = sb("query_weights", [P, KD, PEER_HEADS * PEER_QDIM])
        self.wq_flat = self.wq[:, :, :].rearrange("p k n -> p (k n)")
        self.gain = [self.wide[:, g * D:(g + 1) * D] for g in range(2)]
        self.shift = [self.wide[:, (2 + g) * D:(3 + g) * D] for g in range(2)]
        self.x0 = self.wide[:, 4 * D:5 * D]
        self.wq_in = ctx.enter_context(nc.semaphore("wq_in"))
        self.peer_vec_in = ctx.enter_context(nc.semaphore("peer_vec_in"))

    def load_wq(self, eng, dram, layer, ks):
        for k in ks:
            eng.dma_start(self.wq[:, k, :], dram["peer_wq"][layer, k * P:(k + 1) * P, :]).then_inc(self.wq_in, 16)

    def load_peer_vectors(self, eng, mod_rows, layer):
        for g in range(2):
            for dst, part in ((self.gain, 4), (self.shift, 3)):
                eng.dma_start(dst[g], mod_rows[layer, g:g + 1, part * D:(part + 1) * D].broadcast_to([P, D])).then_inc(self.peer_vec_in, 16)


def modulation_stage(nc, dram, mod_rows, shared):
    h, ident, silu = shared.h, shared.ident, shared.silu
    chunks = FIRST_MOD // BANK
    w = dram["mod_w"][0].rearrange("(p j) n -> p j n", j=KD)
    with ExitStack() as ctx:
        def sb(name, shape, dt=F32):
            return ctx.enter_context(nc.sbuf_tensor(f"first_mod_{name}", shape, dt))

        sems = []

        def sem(name):
            sems.append(ctx.enter_context(nc.semaphore(f"m_{name}")))
            return sems[-1]

        cond = sb("cond", [P, 2, KD])
        in_wq = KD * PEER_HEADS * PEER_QDIM // (KD * BANK)
        w_sb = [shared.wq_flat[:, c * KD * BANK:(c + 1) * KD * BANK].rearrange("p (k n) -> p k n", k=KD) for c in range(in_wq)]
        w_sb += [sb(f"w{c}", [P, KD, BANK])[:, :, :] for c in range(in_wq, chunks)]
        bias = sb("bias", [2, FIRST_MOD])
        rows = sb("rows", [2, FIRST_MOD])
        ps = [ctx.enter_context(nc.psum_tensor(f"first_mod_ps{c}", [P, BANK], F32)) for c in range(chunks)]
        cond_in, silu_done, bias_in, consts_in, h_in = sem("cond_in"), sem("silu"), sem("bias_in"), sem("consts_in"), sem("h_in")
        w_in = [sem(f"w_in{c}") for c in range(chunks)]
        mm_done, rows_done, stored = sem("mm"), sem("rows"), sem("stored")
        ctx.callback(clear_semaphores, nc, sems)
        block = ctx.enter_context(nc.Block())

        @block.sync
        def _(eng):
            for c in range(chunks):
                eng.dma_start(w_sb[c][:, :, :], w[:, :, c * BANK:(c + 1) * BANK]).then_inc(w_in[c], 16)
            eng.wait_ge(rows_done, chunks)
            eng.dma_start(mod_rows[0, :, 0:FIRST_MOD], rows[:, :]).then_inc(stored, 16)
            eng.wait_ge(stored, 16)

        @block.scalar
        def _(eng):
            eng.dma_start(cond[:, 0, :], dram["c"].rearrange("a (p j) -> (a p) j", j=KD)).then_inc(cond_in, 16)
            eng.dma_start(cond[:, 1, :], dram["c_ctx"].rearrange("(p j) -> p j", j=KD)).then_inc(cond_in, 16)
            eng.dma_start(bias[:, :], dram["mod_b"][0:1, 0:FIRST_MOD].broadcast_to([2, FIRST_MOD])).then_inc(bias_in, 16)
            eng.dma_start(ident[:, :], dram["identity"]).then_inc(consts_in, 16)
            eng.wait_ge(cond_in, 32)
            eng.activation(silu[:, :, :], cond[:, :, :], ACT.Silu).then_inc(silu_done, 1)
            eng.wait_ge(w_in[chunks // 2], 16)
            eng.dma_start(h[:, 0:SAMPLE_TILES, :], dram["x_sample"][0].rearrange("(t p) d -> p t d", p=P)).then_inc(h_in, 16)
            eng.dma_start(h[:, SAMPLE_TILES, :], dram["x_prompt"][0]).then_inc(h_in, 16)
            eng.wait_ge(consts_in, 16)
            eng.wait_ge(h_in, 32)

        @block.tensor
        def _(eng):
            eng.wait_ge(silu_done, 1)
            for c in range(chunks):
                eng.wait_ge(w_in[c], 16)
                for j in range(KD):
                    last = eng.matmul(ps[c][0:2, :], silu[:, :, j], w_sb[c][:, j, :], start=(j == 0), stop=(j == KD - 1))
                last.then_inc(mm_done, 1)

        @block.vector
        def _(eng):
            eng.wait_ge(bias_in, 16)
            for c in range(chunks):
                eng.wait_ge(mm_done, c + 1)
                eng.tensor_tensor(rows[:, c * BANK:(c + 1) * BANK], ps[c][0:2, :], bias[:, c * BANK:(c + 1) * BANK], ALU.add).then_inc(rows_done, 1)


def conv_stage(nc, dram, layer, j, mod_rows, shared):
    h, ident, silu = shared.h, shared.ident, shared.silu
    w_in_d = dram["conv_w_in"][j].rearrange("(k p) n -> p k n", p=P)
    w_out_d = dram["conv_w_out"][j].rearrange("(k p) n -> p k n", p=P)
    T = TILES * P
    PROMPT_AT = DEC_SEQ + PAD
    OUT_LEN = PROMPT_AT + SEQ
    IN_LEN = OUT_LEN + 2 * PAD
    SEGMENTS = ((0, DEC_SEQ, 0), (DEC_SEQ, SEQ, PROMPT_AT))
    mod_w = [dram["mod_w"][l].rearrange("(p j) n -> p j n", j=KD) for l in range(DEPTH)]
    LEFT = 6 * D - FIRST_MOD
    MOD_COLS = LEFT + (DEPTH - 1) * 6 * D
    MOD_CHUNKS = MOD_PER_C * KD
    MOD_CHUNK = MOD_COLS // MOD_CHUNKS
    with ExitStack() as ctx:
        def sb(name, shape, dt=F32):
            return ctx.enter_context(nc.sbuf_tensor(f"conv_{name}", shape, dt))

        sems = []

        def sem(name):
            sems.append(ctx.enter_context(nc.semaphore(f"c_{name}")))
            return sems[-1]

        xT = sb("xT", [P, KD, T])
        x = [shared.x0, sb("x1", [P, D])[:, :]]
        w_out = sb("w_out", [P, KD, D])
        glu = [sb(f"glu{b}", [P, IN_LEN]) for b in range(2)]
        square = [sb(f"square{b}", [P, OUT_LEN]) for b in range(2)]
        rstd = sb("rstd", [P, 2, T])
        ones = sb("ones", [P, P])
        rows = sb("rows", [32, P])
        cols = sb("cols", [P, 32])
        taps_rows = sb("taps_rows", [CONV_K, D])
        taps = sb("taps", [P, KD, CONV_K])
        rms = sb("rms", [P, TILES, 4])
        gain, shift = shared.gain, shared.shift
        gate = [sb(f"gate{g}", [P, D])[:, :] for g in range(2)]
        norm_g = sb("norm_g", [P, D])
        b_out = sb("b_out", [P, D])
        MOD_LEN, AG_LEN = KD * MOD_CHUNK, 2 * KD * P
        MIXED_AT = 2 * MOD_LEN + 2 * AG_LEN
        mod_w_sb = [shared.wq_flat[:, b * MOD_LEN:(b + 1) * MOD_LEN].rearrange("p (k n) -> p k n", k=KD) for b in range(2)]
        w_ag = [shared.wq_flat[:, 2 * MOD_LEN + b * AG_LEN:2 * MOD_LEN + (b + 1) * AG_LEN].rearrange("p (a k n) -> p a k n", a=2, k=KD)
                for b in range(2)]
        mixed = shared.wq_flat[:, MIXED_AT:MIXED_AT + KD * OUT_LEN].rearrange("p (k n) -> p k n", k=KD)
        SIG_AT = MIXED_AT + KD * OUT_LEN
        sig = [shared.wq_flat[:, SIG_AT:SIG_AT + T], sb("sig1", [P, T])[:, :]]
        WQ_BEFORE_MIXED = MIXED_AT // (PEER_HEADS * PEER_QDIM)
        mod_bias = [sb(f"mod_bias{b}", [2, MOD_CHUNK]) for b in range(2)]
        mod_out = [sb(f"mod_out{b}", [2, MOD_CHUNK]) for b in range(2)]
        B_A, DW_B, NORM_G = 0, 16, 24

        psum = [ctx.enter_context(nc.psum_tensor(f"conv_ps{b}", [P, 2 * BANK], F32)) for b in range(4)]
        small_ps = psum[3]

        def ag_ps(b, half, segment):
            if segment == 0:
                return psum[b][:, half * BANK:half * BANK + DEC_SEQ]
            return psum[2][:, b * BANK + half * SEQ:b * BANK + (half + 1) * SEQ]

        vec_in, small_in, w_out_in = sem("vec_in"), sem("small_in"), sem("w_out_in")
        w_in = [sem(f"w_in{b}") for b in range(2)]
        gains_made, ones_made, pads_made = sem("gains"), sem("ones"), sem("pads")
        small_tr, small_ev = sem("small_tr"), sem("small_ev")
        ssq_done, std_done, rms_done, x_ready, xT_tr, xT_ready = (sem(n) for n in ("ssq", "std", "rms", "x_ready", "xT_tr", "xT_ready"))
        ag_mm, sig_done, glu_done, conv_done = (sem(n) for n in ("ag_mm", "sig", "glu", "conv"))
        sq_done, sq_used, var_done, csd_done, rstd_done = (sem(n) for n in ("sq", "sq_used", "var", "csd", "rstd"))
        mod_w_in = [sem(f"mod_w_in{b}") for b in range(2)]
        mod_stored = [sem(f"mod_st{b}") for b in range(2)]
        mod_mm, mod_ev, mod_made = sem("mod_mm"), sem("mod_ev"), sem("mod_made")
        scaled, swish_done, out_mm, out_used = (sem(n) for n in ("scaled", "swish", "out_mm", "out_used"))

        ctx.callback(clear_semaphores, nc, sems)
        block = ctx.enter_context(nc.Block())

        def group_of(tile):
            return 1 if tile == TILES - 1 else 0

        @block.sync
        def _(eng):
            eng.dma_start(norm_g[:, :], dram["norm1_g"][layer:layer + 1, :].broadcast_to([P, D])).then_inc(vec_in, 16)
            for g in range(2):
                for dst, part in ((shift, 0), (gain, 1), (gate, 2)):
                    eng.dma_start(dst[g], mod_rows[layer, g:g + 1, part * D:(part + 1) * D].broadcast_to([P, D])).then_inc(vec_in, 16)
            eng.dma_start(rows[0:16, :], dram["conv_b_in"][j].rearrange("(r p) -> r p", p=P)).then_inc(small_in, 16)
            eng.dma_start(rows[16:24, :], dram["conv_dw_b"][j].rearrange("(r p) -> r p", p=P)).then_inc(small_in, 16)
            eng.dma_start(rows[24:32, :], dram["conv_norm_g"][j].rearrange("(r p) -> r p", p=P)).then_inc(small_in, 16)
            eng.dma_start(taps_rows[:, :], dram["conv_dw"][j]).then_inc(small_in, 16)

            def load(c):
                for half in range(2):
                    eng.dma_start(w_ag[c % 2][:, half, :, :], w_in_d[:, :, half * D + c * P:half * D + (c + 1) * P]).then_inc(w_in[c % 2], 16)

            def mod_place(n):
                at = n * MOD_CHUNK
                return (0, FIRST_MOD + at) if at < LEFT else (1, at - LEFT)

            def load_mod(n):
                l, at = mod_place(n)
                eng.dma_start(mod_w_sb[n % 2][:, :, :], mod_w[l][:, :, at:at + MOD_CHUNK]).then_inc(mod_w_in[n % 2], 16)
                eng.dma_start(mod_bias[n % 2][:, :], dram["mod_b"][l:l + 1, at:at + MOD_CHUNK].broadcast_to([2, MOD_CHUNK])).then_inc(mod_w_in[n % 2], 16)

            load(0)
            load(1)
            load_mod(0)
            load_mod(1)
            eng.dma_start(b_out[:, :], dram["conv_b_out"][j:j + 1, :].broadcast_to([P, D])).then_inc(w_out_in, 16)
            for k in range(KD):
                eng.dma_start(w_out[:, k, :], w_out_d[:, k, :]).then_inc(w_out_in, 16)
            for c in range(KD):
                if c + 2 < KD:
                    eng.wait_ge(ag_mm, c + 1)
                    load(c + 2)
                for n in range(c * MOD_PER_C, (c + 1) * MOD_PER_C):
                    l, at = mod_place(n)
                    eng.wait_ge(mod_made, n + 1)
                    eng.dma_start(mod_rows[l, :, at:at + MOD_CHUNK], mod_out[n % 2][:, :]).then_inc(mod_stored[n % 2], 16)
                    if n + 2 < MOD_CHUNKS:
                        load_mod(n + 2)
            for b in range(2):
                eng.wait_ge(mod_stored[b], 16 * (MOD_CHUNKS // 2) + 16)
            eng.wait_ge(ag_mm, KD)
            shared.load_peer_vectors(eng, mod_rows, layer)
            shared.load_wq(eng, dram, layer, range(WQ_BEFORE_MIXED))
            eng.wait_ge(swish_done, KD)
            shared.load_wq(eng, dram, layer, range(WQ_BEFORE_MIXED, KD))

        @block.gpsimd
        def _(eng):
            eng.memset(ones[:, :], 1.0).then_inc(ones_made, 1)
            for b in range(2):
                for at in (0, PAD + DEC_SEQ, IN_LEN - PAD):
                    eng.memset(glu[b][:, at:at + PAD], 0.0).then_inc(pads_made, 1)
            eng.sem_inc(glu_done, 2)
            eng.sem_inc(mod_ev, 2)
            for b in range(2):
                eng.sem_inc(mod_stored[b], 16)
            with eng.Fori(0, MOD_CHUNKS // 2) as i:
                for b in range(2):
                    eng.wait_ge(mod_ev, 2 * i + b + 3)
                    eng.tensor_tensor(mod_out[b][:, :], mod_out[b][:, :], mod_bias[b][:, :], ALU.add).then_inc(mod_made, 1)

        @block.vector
        def _(eng):
            eng.wait_ge(vec_in, 16 * 7)
            for g in range(2):
                eng.scalar_tensor_tensor(out=gain[g], in0=gain[g], scalar=1.0, in1=norm_g[:, :], op0=ALU.add, op1=ALU.mult)
            eng.drain()
            for tile in range(TILES):
                xb, g = x[tile % 2], group_of(tile)
                eng.wait_ge(ssq_done, tile + 1)
                eng.tensor_scalar(rms[:, tile, 1:2], rms[:, tile, 0:1], 1.0 / D, EPS, ALU.mult, ALU.add).then_inc(rms_done, 1)
                eng.wait_ge(std_done, tile + 1)
                done(eng, eng.reciprocal(rms[:, tile, 3:4], rms[:, tile, 2:3]))
                if tile >= 2:
                    eng.wait_ge(xT_tr, 2 * (tile - 1))
                done(eng, eng.scalar_tensor_tensor(out=xb, in0=h[:, tile, :], scalar=rms[:, tile, 3:4], in1=gain[g], op0=ALU.mult, op1=ALU.mult))
                eng.tensor_tensor(xb, xb, shift[g], ALU.add).then_inc(x_ready, 1)

            eng.wait_ge(pads_made, 6)
            eng.wait_ge(small_ev, 2)
            with eng.Fori(0, KD // 2) as i:
                for b in range(2):
                    c = 2 * i + b
                    eng.wait_ge(sig_done, c + 1)
                    for segment, (start, n, at) in enumerate(SEGMENTS):
                        last = eng.scalar_tensor_tensor(out=glu[b][:, PAD + at:PAD + at + n], in0=ag_ps(b, 0, segment),
                                                        scalar=cols[:, bass.ds(c + B_A, 1)], in1=sig[b][:, start:start + n],
                                                        op0=ALU.add, op1=ALU.mult)
                    last.then_inc(glu_done, 1)
                    eng.drain()
                    out = mixed[:, bass.ds(c, 1), :].rearrange("p a n -> p (a n)")
                    tap = taps[:, bass.ds(c, 1), :].rearrange("p a k -> p (a k)")
                    done(eng, eng.tensor_scalar(out, glu[b][:, 0:OUT_LEN], tap[:, 0:1], cols[:, bass.ds(c + DW_B, 1)], ALU.mult, ALU.add))
                    for k in range(1, CONV_K):
                        last = done(eng, eng.scalar_tensor_tensor(out=out, in0=glu[b][:, k:k + OUT_LEN], scalar=tap[:, k:k + 1], in1=out,
                                                                  op0=ALU.mult, op1=ALU.add))
                    last.then_inc(conv_done, 1)

            eng.wait_ge(sq_used, KD)
            eng.tensor_scalar(rstd[:, 0, :], psum[2][:, 0:T], 1.0 / D, EPS, ALU.mult, ALU.add).then_inc(var_done, 1)
            eng.wait_ge(csd_done, 1)
            done(eng, eng.reciprocal(rstd[:, 0, :], rstd[:, 1, :]))
            for c in range(KD):
                for start, n, at in SEGMENTS:
                    last = eng.tensor_tensor(mixed[:, c, at:at + n], mixed[:, c, at:at + n], rstd[:, 0, start:start + n], ALU.mult)
                last.then_inc(scaled, 1)

            eng.wait_ge(w_out_in, 16 * (KD + 1))
            for tile in range(TILES):
                g, tmp = group_of(tile), x[tile % 2]
                eng.wait_ge(out_mm, tile + 1)
                eng.tensor_tensor(tmp, psum[tile % 2][:, :], b_out[:, :], ALU.add).then_inc(out_used, 1)
                eng.drain()
                done(eng, eng.tensor_tensor(tmp, tmp, gate[g], ALU.mult))
                eng.tensor_tensor(h[:, tile, :], h[:, tile, :], tmp, ALU.add)

        @block.scalar
        def _(eng):
            for tile in range(TILES):
                if tile >= 2:
                    eng.wait_ge(xT_tr, 2 * (tile - 1))
                eng.activation(x[tile % 2], h[:, tile, :], ACT.Square, accum_out=rms[:, tile, 0:1]).then_inc(ssq_done, 1)
                eng.wait_ge(rms_done, tile + 1)
                eng.activation(rms[:, tile, 2:3], rms[:, tile, 1:2], ACT.Sqrt).then_inc(std_done, 1)
                for half in range(2):
                    eng.wait_ge(xT_tr, 2 * tile + half + 1)
                    eng.activation(xT[:, 4 * half:4 * half + 4, tile * P:(tile + 1) * P],
                                   psum[half][:, 0:BANK].rearrange("p (k t) -> p k t", k=4), ACT.Copy).then_inc(xT_ready, 1)
                if tile == 0:
                    eng.wait_ge(small_tr, 1)
                    eng.activation(cols[:, :], small_ps[:, 0:32], ACT.Copy).then_inc(small_ev, 1)
                    eng.activation(taps[:, :, :], small_ps[:, BANK:BANK + KD * 32].rearrange("p (c k) -> p c k", c=KD)[:, :, 0:CONV_K], ACT.Copy).then_inc(small_ev, 1)
            eng.drain()
            with eng.Fori(0, KD // 2) as i:
                for b in range(2):
                    c = 2 * i + b
                    eng.wait_ge(ag_mm, c + 1)
                    eng.wait_ge(glu_done, c + 1)
                    for segment, (start, n, _) in enumerate(SEGMENTS):
                        last = eng.activation(sig[b][:, start:start + n], ag_ps(b, 1, segment), ACT.Sigmoid, bias=cols[:, bass.ds(c + B_A + KD, 1)])
                    last.then_inc(sig_done, 1)
                    for m in range(MOD_PER_C):
                        n, mb = i * (2 * MOD_PER_C) + b * MOD_PER_C + m, (b * MOD_PER_C + m) % 2
                        eng.wait_ge(mod_mm, n + 1)
                        eng.wait_ge(mod_stored[mb], 16 * MOD_PER_C * i + 16 * ((b * MOD_PER_C + m) // 2 + 1))
                        eng.activation(mod_out[mb][:, :], psum[3][0:2, mb * BANK:mb * BANK + MOD_CHUNK], ACT.Copy).then_inc(mod_ev, 1)
            for c in range(KD):
                eng.wait_ge(conv_done, c + 1)
                if c >= 2:
                    eng.wait_ge(sq_used, c - 1)
                eng.activation(square[c % 2][:, :], mixed[:, c, :], ACT.Square).then_inc(sq_done, 1)
            eng.wait_ge(var_done, 1)
            eng.activation(rstd[:, 1, :], rstd[:, 0, :], ACT.Sqrt).then_inc(csd_done, 1)
            for c in range(KD):
                eng.wait_ge(scaled, c + 1)
                for start, n, at in SEGMENTS:
                    last = eng.activation(xT[:, c, start:start + n], mixed[:, c, at:at + n], ACT.Silu, scale=cols[:, NORM_G + c:NORM_G + c + 1])
                last.then_inc(swish_done, 1)

        @block.tensor
        def _(eng):
            for tile in range(TILES):
                eng.wait_ge(x_ready, tile + 1)
                for half in range(2):
                    if tile:
                        eng.wait_ge(xT_ready, 2 * tile - 1 + half)
                    for k in range(4):
                        last = eng.transpose(psum[half][:, k * P:(k + 1) * P], x[tile % 2][:, (4 * half + k) * P:(4 * half + k + 1) * P], ident[:, :])
                    last.then_inc(xT_tr, 1)
                if tile == 0:
                    eng.wait_ge(small_in, 64)
                    eng.transpose(small_ps[:, 0:32], rows[:, :], ident[0:32, 0:32])
                    for c in range(KD):
                        last = eng.transpose(small_ps[:, BANK + c * 32:BANK + c * 32 + CONV_K], taps_rows[:, c * P:(c + 1) * P], ident[0:CONV_K, 0:CONV_K])
                    last.then_inc(small_tr, 1)
            eng.wait_ge(xT_ready, 2 * TILES)
            eng.wait_ge(small_ev, 2)

            def modulation_chunk(i, m):
                b = m % 2
                eng.wait_ge(mod_w_in[b], 32 * MOD_PER_C * i + 32 * (m // 2 + 1))
                eng.wait_ge(mod_ev, i * (2 * MOD_PER_C) + m + 1)
                for k in range(KD):
                    last = eng.matmul(psum[3][0:2, b * BANK:b * BANK + MOD_CHUNK], silu[:, :, k], mod_w_sb[b][:, k, :], start=(k == 0), stop=(k == KD - 1))
                last.then_inc(mod_mm, 1)

            with eng.Fori(0, KD // 2) as i:
                for b in range(2):
                    c = 2 * i + b
                    eng.wait_ge(w_in[b], 32 * i + 32)
                    eng.wait_ge(glu_done, c + 1)
                    for segment, half in ((0, 0), (0, 1), (1, 0), (1, 1)):
                        start, n, _ = SEGMENTS[segment]
                        for k in range(KD):
                            last = eng.matmul(ag_ps(b, half, segment), w_ag[b][:, half, k, :], xT[:, k, start:start + n],
                                              start=(k == 0), stop=(k == KD - 1))
                    last.then_inc(ag_mm, 1)
                    for m in range(MOD_PER_C):
                        modulation_chunk(i, b * MOD_PER_C + m)
            eng.wait_ge(glu_done, KD + 2)
            eng.wait_ge(ones_made, 1)
            for c in range(KD):
                eng.wait_ge(sq_done, c + 1)
                for start, n, at in SEGMENTS:
                    last = eng.matmul(psum[2][:, start:start + n], ones[:, :], square[c % 2][:, at:at + n], start=(c == 0), stop=(c == KD - 1))
                last.then_inc(sq_used, 1)
            eng.wait_ge(swish_done, KD)
            eng.wait_ge(w_out_in, 16 * (KD + 1))
            for tile in range(TILES):
                if tile >= 2:
                    eng.wait_ge(out_used, tile - 1)
                for half in range(2):
                    for k in range(KD):
                        last = eng.matmul(psum[tile % 2][:, half * BANK:(half + 1) * BANK], xT[:, k, tile * P:(tile + 1) * P],
                                          w_out[:, k, half * BANK:(half + 1) * BANK], start=(k == 0), stop=(k == KD - 1))
                last.then_inc(out_mm, 1)


def attention_stage(nc, dram, layer, j, mod_rows, ckv_out, kpe_out, shared):
    h, ident, wide = shared.h, shared.ident, shared.wide
    HALVES, HH = 2, HEADS // 2
    CACHE_KT, PROMPT_KT = SAMPLE_TILES, SAMPLE_TILES + 1
    KEY_TILES = SAMPLE_TILES + 2
    KV_W = NOPE + VH
    SCALE = float(QK) ** -0.5
    KQ, KL = Q_LORA // P, KV_LORA // P

    def group_of(tile):
        return 1 if tile == TILES - 1 else 0

    def key_tile(tile):
        return PROMPT_KT if tile == TILES - 1 else tile

    def keys_of(tile):
        return (PROMPT_KT * P, P) if tile == TILES - 1 else (0, (SAMPLE_TILES + 1) * P)

    with ExitStack() as ctx:
        def sb(name, shape, dt=F32):
            return ctx.enter_context(nc.sbuf_tensor(f"attn_{name}", shape, dt))

        sems = []

        def sem(name):
            sems.append(ctx.enter_context(nc.semaphore(f"a_{name}")))
            return sems[-1]

        gain, shift = shared.gain, shared.shift
        gate = [sb(f"gate{g}", [P, D]) for g in range(2)]
        q_a = sb("q_a", [P, KD, Q_LORA])
        kv_a = sb("kv_a", [P, KD, KV_LORA + ROPE])
        half_w = sb("half_w", [P, KQ * HH * QK + KL * HH * KV_W])
        q_b = half_w[:, 0:KQ * HH * QK].rearrange("p (k n) -> p k n", k=KQ)
        kv_b = half_w[:, KQ * HH * QK:].rearrange("p (k n) -> p k n", k=KL)
        o_w = [sb("o_w", [P, KD, BANK])[:, :, :], half_w[:, 0:KD * BANK].rearrange("p (k n) -> p k n", k=KD)]
        q_a_norm = sb("q_a_norm", [P, Q_LORA])
        kv_a_norm = sb("kv_a_norm", [P, KV_LORA])
        qk_gain = sb("qk_gain", [P, 2, QK])
        cos = sb("cos", [P, SAMPLE_TILES, ROPE // 2])
        sin = sb("sin", [P, SAMPLE_TILES, ROPE // 2])
        rms = sb("rms", [P, TILES, 12])
        taken = [0]

        def place(*shape):
            n = int(np.prod(shape))
            taken[0] += n
            assert taken[0] <= KD * PEER_HEADS * PEER_QDIM
            flat = shared.wq_flat[:, taken[0] - n:taken[0]]
            names = " ".join("abcd"[:len(shape)])
            return flat.rearrange(f"p ({names}) -> p {names}", **dict(zip("abcd", shape)))

        lat_q = [place(Q_LORA) for b in range(2)]
        lat_kv = [sb(f"lat_kv{b}", [P, KV_LORA]) for b in range(2)]
        latT_q = place(TILES, KQ, P)
        latT_kv = place(KEY_TILES, KL, P)
        kpe = sb("kpe", [P, KEY_TILES, ROPE])
        heads_sb = [place(HH, QK) for b in range(2)]
        heads_sq = [sb(f"heads_sq{b}", [P, HH, QK]) for b in range(2)]
        head_ms = [sb(f"head_ms{b}", [P, 3, HH]) for b in range(2)]
        rope_tmp = place(4, HH, ROPE // 2)
        kT = place(HH, KEY_TILES * P)[0:QK]
        qT = wide[0:QK, :].rearrange("p (t n q) -> p t n q", t=TILES, n=HH)
        v = sb("v", [P, KEY_TILES, HH, VH])
        probs = [place(5 * P) for b in range(2)]
        probsT = [place(5, P) for b in range(2)]
        neg_max = [sb(f"neg_max{b}", [P, 2]) for b in range(2)]
        sums = [sb(f"sums{b}", [P, 2, HH]) for b in range(2)]
        out_a = q_a[:, :, :].rearrange("p k n -> p (k n)")
        out_heads = [out_a[:, t * D:(t + 1) * D] for t in range(4)] + [kv_a[:, :, :].rearrange("p k n -> p (k n)")[:, 0:D]]
        v_flat = v[:, :, :, :].rearrange("p a n w -> p (a n w)")
        x = [shared.x0, v_flat[:, 0:D]]
        xT = [sb("xT", [P, KD, P])[:, :, :], v_flat[:, D:2 * D].rearrange("p (k t) -> p k t", k=KD)]
        cache_kv = v_flat[:, 2 * D:2 * D + KV_LORA]

        def bank_pair(name):
            return ctx.enter_context(nc.psum_tensor(f"attn_{name}", [P, 2 * BANK], F32))

        ps_a, ps_b, ps_c, ps_d = (bank_pair(n) for n in "abcd")
        ps_ab, ps_cd = (ps_a, ps_b), (ps_c, ps_d)

        vec_in = [sem(f"vec_in{g}") for g in range(2)]
        lat_w_in, small_in, cache_in = (sem(n) for n in ("lat_w", "small_in", "cache_in"))
        ow_in = [sem(f"ow_in{b}") for b in range(2)]
        half_w_in, half_w_used = sem("half_w"), sem("half_w_used")
        ssq_done, std_done, rms_done, x_ready, xT_tr, xT_ready = (sem(n) for n in ("ssq", "std", "rms", "x_ready", "xT_tr", "xT_ready"))
        lat_mm, lat_sq, lat_ms, lat_std, lat_ready, lat_tr, lat_ev = (sem(n) for n in ("lat_mm", "lat_sq", "lat_ms", "lat_std", "lat_ready", "lat_tr", "lat_ev"))
        new_stored, gains_made = sem("new_stored"), sem("gains")
        hd_mm, hd_sq, v_copied, hd_ms, hd_std, hd_scaled, hd_ready, hd_tr, hd_ev = (sem(n) for n in ("hd_mm", "hd_sq", "v_cp", "hd_ms", "hd_std", "hd_scaled", "hd_ready", "hd_tr", "hd_ev"))
        s_mm, max_done, exp_done, p_tr, p_ev, pv_mm, o_used = (sem(n) for n in ("s_mm", "max", "exp", "p_tr", "p_ev", "pv", "o_used"))
        oT_tr, oT_ev, out_mm, out_used = (sem(n) for n in ("oT_tr", "oT_ev", "out_mm", "out_used"))

        ctx.callback(clear_semaphores, nc, sems)
        block = ctx.enter_context(nc.Block())
        STEPS = KEY_TILES + TILES
        RUNS = TILES * HH

        @block.sync
        def _(eng):
            eng.dma_start(x[1], dram["norm1_g"][layer:layer + 1, :].broadcast_to([P, D])).then_inc(vec_in[0], 16)
            for g in range(2):
                for dst, part in ((gain, 1), (shift, 0)):
                    eng.dma_start(dst[g], mod_rows[layer, g:g + 1, part * D:(part + 1) * D].broadcast_to([P, D])).then_inc(vec_in[g], 16)
                if g == 0:
                    eng.dma_start(q_a[:, :, :], dram["q_a_w"][j].rearrange("(k p) n -> p k n", p=P)).then_inc(lat_w_in, 16)
                    eng.dma_start(kv_a[:, :, :], dram["kv_a_w"][j].rearrange("(k p) n -> p k n", p=P)).then_inc(lat_w_in, 16)
                    eng.dma_start(q_a_norm[:, :], dram["q_a_norm"][j:j + 1, :].broadcast_to([P, Q_LORA])).then_inc(small_in, 16)
                    eng.dma_start(kv_a_norm[:, :], dram["kv_a_norm"][j:j + 1, :].broadcast_to([P, KV_LORA])).then_inc(small_in, 16)
            eng.dma_start(qk_gain[:, 0, :], dram["q_norm"][j:j + 1, :].broadcast_to([P, QK])).then_inc(small_in, 16)
            eng.dma_start(qk_gain[:, 1, :], dram["k_norm"][j:j + 1, :].broadcast_to([P, QK])).then_inc(small_in, 16)
            eng.dma_start(cos[:, :, :], dram["rope_cos"].rearrange("(t p) f -> p t f", p=P)).then_inc(small_in, 16)
            eng.dma_start(sin[:, :, :], dram["rope_sin"].rearrange("(t p) f -> p t f", p=P)).then_inc(small_in, 16)
            eng.dma_start(cache_kv, dram["cache_ckv"][0, j]).then_inc(cache_in, 16)
            eng.dma_start(kpe[:, CACHE_KT, :], dram["cache_kpe"][0, j]).then_inc(cache_in, 16)

            def load_half(hh):
                eng.dma_start(kv_b, dram["kv_b_w"][j].rearrange("(k p) n -> p k n", p=P)[:, :, hh * HH * KV_W:(hh + 1) * HH * KV_W]).then_inc(half_w_in, 16)
                eng.dma_start(q_b, dram["q_b_w"][j].rearrange("(k p) n -> p k n", p=P)[:, :, hh * HH * QK:(hh + 1) * HH * QK]).then_inc(half_w_in, 16)

            def load_output(c):
                eng.dma_start(o_w[c], dram["o_w"][j].rearrange("(k p) n -> p k n", p=P)[:, :, c * BANK:(c + 1) * BANK]).then_inc(ow_in[c], 16)

            load_half(0)
            for g in range(2):
                eng.dma_start(gate[g][:, :], mod_rows[layer, g:g + 1, 2 * D:3 * D].broadcast_to([P, D])).then_inc(ow_in[0], 16)
            load_output(0)
            eng.wait_ge(lat_ready, TILES)
            eng.dma_start(ckv_out, lat_kv[(TILES - 1) % 2][:, :]).then_inc(new_stored, 16)
            eng.dma_start(kpe_out, kpe[:, PROMPT_KT, :]).then_inc(new_stored, 16)
            eng.wait_ge(half_w_used, 1)
            load_half(1)
            eng.wait_ge(half_w_used, 2)
            load_output(1)
            eng.wait_ge(pv_mm, HALVES * RUNS)
            shared.load_peer_vectors(eng, mod_rows, layer)
            shared.load_wq(eng, dram, layer, range(KD))
            eng.wait_ge(new_stored, 32)

        @block.tensor
        def _(eng):
            def transpose_x(tile):
                eng.wait_ge(x_ready, tile + 1)
                for half in range(2):
                    if tile:
                        eng.wait_ge(xT_ready, 2 * tile - 1 + half)
                    for k in range(4 * half, 4 * half + 4):
                        last = eng.transpose(ps_c[:, k * P:(k + 1) * P], x[tile % 2][:, k * P:(k + 1) * P], ident[:, :])
                    last.then_inc(xT_tr, 1)

            def latents(tile):
                eng.wait_ge(xT_ready, 2 * tile + 2)
                if tile >= 2:
                    eng.wait_ge(lat_ready, tile - 1)
                out = ps_ab[tile % 2]
                for k in range(KD):
                    eng.matmul(out[:, 0:Q_LORA], xT[tile % 2][:, k, :], q_a[:, k, :], start=(k == 0), stop=(k == KD - 1))
                for k in range(KD):
                    last = eng.matmul(out[:, BANK:BANK + KV_LORA + ROPE], xT[tile % 2][:, k, :], kv_a[:, k, :], start=(k == 0), stop=(k == KD - 1))
                last.then_inc(lat_mm, 1)

            def transpose_latents(tile):
                eng.wait_ge(lat_ready, tile + 1)
                if tile:
                    eng.wait_ge(lat_ev, 2 * tile)
                for k in range(KQ):
                    eng.transpose(ps_d[:, k * P:(k + 1) * P], lat_q[tile % 2][:, k * P:(k + 1) * P], ident[:, :])
                for k in range(KL):
                    last = eng.transpose(ps_d[:, BANK + k * P:BANK + (k + 1) * P], lat_kv[tile % 2][:, k * P:(k + 1) * P], ident[:, :])
                last.then_inc(lat_tr, 1)

            transpose_x(0)
            eng.wait_ge(lat_w_in, 32)
            for tile in range(TILES):
                latents(tile)
                if tile + 1 < TILES:
                    transpose_x(tile + 1)
                if tile:
                    transpose_latents(tile - 1)
            transpose_latents(TILES - 1)
            eng.wait_ge(cache_in, 32)
            eng.wait_ge(lat_ev, 2 * TILES)
            for k in range(KL):
                last = eng.transpose(ps_d[:, BANK + k * P:BANK + (k + 1) * P], cache_kv[:, k * P:(k + 1) * P], ident[:, :])
            last.then_inc(lat_tr, 1)
            eng.wait_ge(lat_ev, 2 * TILES + 1)

            with eng.Fori(0, HALVES) as hh:
                def project(s):
                    out = ps_ab[s % 2]
                    if s >= 2:
                        eng.wait_ge(hd_scaled, hh * STEPS + s - 1)
                        eng.wait_ge(v_copied, hh * KEY_TILES + min(s - 1, KEY_TILES))
                    for c in range(2):
                        if s < KEY_TILES:
                            for k in range(KL):
                                last = eng.matmul(out[:, c * BANK:(c + 1) * BANK], latT_kv[:, s, k, :], kv_b[:, k, c * BANK:(c + 1) * BANK],
                                                  start=(k == 0), stop=(k == KL - 1))
                        else:
                            n = HH * QK // 2
                            for k in range(KQ):
                                last = eng.matmul(out[:, c * BANK:c * BANK + n], latT_q[:, s - KEY_TILES, k, :], q_b[:, k, c * n:(c + 1) * n],
                                                  start=(k == 0), stop=(k == KQ - 1))
                    last.then_inc(hd_mm, 1)

                def transpose_heads(s):
                    eng.wait_ge(hd_ready, hh * STEPS + s + 1)
                    if s >= 2:
                        eng.wait_ge(hd_ev, hh * STEPS + s - 1)
                    for n in range(HH):
                        last = eng.transpose(ps_cd[s % 2][0:QK, n * P:(n + 1) * P], heads_sb[s % 2][:, n, :], ident[:, :])
                    last.then_inc(hd_tr, 1)

                eng.wait_ge(half_w_in, 32 * hh + 32)
                project(0)
                for s in range(STEPS):
                    if s + 1 < STEPS:
                        project(s + 1)
                    transpose_heads(s)
                eng.wait_ge(hd_ev, hh * STEPS + STEPS)
                eng.sem_inc(half_w_used, 1)

                def scores(r):
                    tile, n = r // HH, r % HH
                    first_key, n_keys = keys_of(tile)
                    if r >= 2:
                        eng.wait_ge(exp_done, hh * RUNS + r - 1)
                    for c in range(0, n_keys, BANK):
                        m = min(BANK, n_keys - c)
                        last = eng.matmul(ps_ab[r % 2][:, c:c + m], qT[:, tile, n, :], kT[:, n, first_key + c:first_key + c + m], start=True, stop=True)
                    last.then_inc(s_mm, 1)

                def transpose_probs(r):
                    _, n_keys = keys_of(r // HH)
                    eng.wait_ge(exp_done, hh * RUNS + r + 1)
                    if r:
                        eng.wait_ge(p_ev, hh * RUNS + r)
                    for c in range(n_keys // P):
                        last = eng.transpose(ps_c[:, c * P:(c + 1) * P], probs[r % 2][:, c * P:(c + 1) * P], ident[:, :])
                    last.then_inc(p_tr, 1)

                def weigh_values(r):
                    tile, n = r // HH, r % HH
                    first_key, n_keys = keys_of(tile)
                    if n == 0 and tile >= 2:
                        eng.wait_ge(o_used, hh * TILES + tile - 1)
                    eng.wait_ge(p_ev, hh * RUNS + r + 1)
                    at = (tile % 2) * BANK + n * VH
                    for c in range(n_keys // P):
                        last = eng.matmul(ps_d[:, at:at + VH], probsT[r % 2][:, c, :], v[:, first_key // P + c, n, :],
                                          start=(c == 0), stop=(c == n_keys // P - 1))
                    last.then_inc(pv_mm, 1)

                scores(0)
                scores(1)
                for r in range(RUNS):
                    transpose_probs(r)
                    if r + 2 < RUNS:
                        scores(r + 2)
                    if r:
                        weigh_values(r - 1)
                weigh_values(RUNS - 1)
                eng.wait_ge(o_used, hh * TILES + TILES)

            def transpose_outputs(tile):
                if tile >= 2:
                    eng.wait_ge(oT_ev, 2 * (tile - 1))
                for half in range(2):
                    for k in range(4 * half, 4 * half + 4):
                        last = eng.transpose(ps_cd[tile % 2][:, k * P:(k + 1) * P], out_heads[tile][:, k * P:(k + 1) * P], ident[:, :])
                    last.then_inc(oT_tr, 1)

            transpose_outputs(0)
            eng.wait_ge(ow_in[0], 48)
            eng.wait_ge(ow_in[1], 16)
            for tile in range(TILES):
                if tile + 1 < TILES:
                    transpose_outputs(tile + 1)
                eng.wait_ge(oT_ev, 2 * tile + 2)
                if tile >= 2:
                    eng.wait_ge(out_used, tile - 1)
                for c in range(2):
                    for k in range(KD):
                        last = eng.matmul(ps_ab[tile % 2][:, c * BANK:(c + 1) * BANK], xT[tile % 2][:, k, :], o_w[c][:, k, :], start=(k == 0), stop=(k == KD - 1))
                last.then_inc(out_mm, 1)

        @block.scalar
        def _(eng):
            def copy_xT(tile, dst, src, transposed, copied, older):
                for half in range(2):
                    eng.wait_ge(transposed, 2 * tile + half + 1)
                    if tile >= 2:
                        eng.wait_ge(older, tile - 1)
                    eng.activation(dst[:, 4 * half:4 * half + 4, :].rearrange("p k t -> p (k t)"),
                                   src[:, half * BANK:(half + 1) * BANK], ACT.Copy).then_inc(copied, 1)

            def norm(tile):
                if tile >= 2:
                    eng.wait_ge(xT_tr, 2 * (tile - 1))
                if tile == 1:
                    eng.wait_ge(gains_made, 1)
                eng.activation(x[tile % 2], h[:, tile, :], ACT.Square, accum_out=rms[:, tile, 0:1]).then_inc(ssq_done, 1)
                eng.wait_ge(rms_done, tile + 1)
                eng.activation(rms[:, tile, 2:3], rms[:, tile, 1:2], ACT.Sqrt).then_inc(std_done, 1)
                copy_xT(tile, xT[tile % 2], ps_c, xT_tr, xT_ready, lat_mm)

            def square_latents(tile):
                eng.wait_ge(lat_mm, tile + 1)
                if tile >= 2:
                    eng.wait_ge(lat_tr, tile - 1)
                eng.activation(lat_q[tile % 2][:, :], ps_ab[tile % 2][:, 0:Q_LORA], ACT.Square, accum_out=rms[:, tile, 4:5]).then_inc(lat_sq, 1)
                eng.activation(lat_kv[tile % 2][:, :], ps_ab[tile % 2][:, BANK:BANK + KV_LORA], ACT.Square, accum_out=rms[:, tile, 5:6]).then_inc(lat_sq, 1)
                eng.wait_ge(lat_ms, tile + 1)
                eng.activation(rms[:, tile, 8:10], rms[:, tile, 6:8], ACT.Sqrt).then_inc(lat_std, 1)

            def copy_latents(tile):
                eng.wait_ge(lat_tr, tile + 1)
                eng.activation(latT_q[:, tile, :, :].rearrange("p k t -> p (k t)"), ps_d[:, 0:Q_LORA], ACT.Copy).then_inc(lat_ev, 1)
                eng.activation(latT_kv[:, key_tile(tile), :, :].rearrange("p k t -> p (k t)"), ps_d[:, BANK:BANK + KV_LORA], ACT.Copy).then_inc(lat_ev, 1)

            norm(0)
            for tile in range(TILES):
                if tile + 1 < TILES:
                    norm(tile + 1)
                if tile:
                    copy_latents(tile - 1)
                square_latents(tile)
            copy_latents(TILES - 1)
            eng.wait_ge(lat_tr, TILES + 1)
            eng.activation(latT_kv[:, CACHE_KT, :, :].rearrange("p k t -> p (k t)"), ps_d[:, BANK:BANK + KV_LORA], ACT.Copy).then_inc(lat_ev, 1)

            with eng.Fori(0, HALVES) as hh:
                def square_heads(s):
                    eng.wait_ge(hd_mm, hh * STEPS + s + 1)
                    if s < KEY_TILES:
                        heads = ps_ab[s % 2][:, :].rearrange("p (n w) -> p n w", n=HH)
                        eng.activation(heads_sq[s % 2][:, :, 0:NOPE], heads[:, :, 0:NOPE], ACT.Square)
                        eng.activation(heads_sq[s % 2][:, :, NOPE:QK], kpe[:, s, :].unsqueeze(1).broadcast_to([P, HH, ROPE]), ACT.Square).then_inc(hd_sq, 1)
                        eng.activation(v[:, s, :, :], heads[:, :, NOPE:KV_W], ACT.Copy).then_inc(v_copied, 1)
                    else:
                        eng.activation(heads_sq[s % 2][:, :, :].rearrange("p (c n) w -> p c (n w)", c=2),
                                       ps_ab[s % 2][:, :].rearrange("p (c n) -> p c n", c=2)[:, :, 0:HH * QK // 2], ACT.Square).then_inc(hd_sq, 1)

                def copy_heads(s):
                    eng.wait_ge(hd_tr, hh * STEPS + s + 1)
                    target = kT[:, :, s * P:(s + 1) * P] if s < KEY_TILES else qT[:, s - KEY_TILES, :, :]
                    eng.activation(target, ps_cd[s % 2][0:QK, :].rearrange("p (n t) -> p n t", n=HH), ACT.Copy).then_inc(hd_ev, 1)

                square_heads(0)
                for s in range(STEPS):
                    eng.wait_ge(hd_ms, hh * STEPS + s + 1)
                    eng.activation(head_ms[s % 2][:, 2, :], head_ms[s % 2][:, 1, :], ACT.Sqrt).then_inc(hd_std, 1)
                    if s + 1 < STEPS:
                        square_heads(s + 1)
                    if s:
                        copy_heads(s - 1)
                copy_heads(STEPS - 1)

                def exponentials(r):
                    _, n_keys = keys_of(r // HH)
                    eng.wait_ge(max_done, hh * RUNS + r + 1)
                    if r >= 2:
                        eng.wait_ge(p_tr, hh * RUNS + r - 1)
                    eng.activation(probs[r % 2][:, 0:n_keys], ps_ab[r % 2][:, 0:n_keys], ACT.Exp, bias=neg_max[r % 2][:, 1:2],
                                   scale=SCALE, accum_out=sums[(r // HH) % 2][:, 0, r % HH:r % HH + 1]).then_inc(exp_done, 1)

                exponentials(0)
                for r in range(RUNS):
                    if r + 1 < RUNS:
                        tile = (r + 1) // HH
                        if (r + 1) % HH == 0 and tile >= 2:
                            eng.wait_ge(o_used, hh * TILES + tile - 1)
                        exponentials(r + 1)

            for tile in range(TILES):
                copy_xT(tile, xT[tile % 2], ps_cd[tile % 2], oT_tr, oT_ev, out_mm)

        @block.vector
        def _(eng):
            def make_gain(g):
                eng.wait_ge(vec_in[g], 48 if g == 0 else 32)
                return eng.scalar_tensor_tensor(out=gain[g], in0=gain[g], scalar=1.0, in1=x[1], op0=ALU.add, op1=ALU.mult)

            def norm(tile):
                g, xb = group_of(tile), x[tile % 2]
                eng.wait_ge(ssq_done, tile + 1)
                eng.tensor_scalar(rms[:, tile, 1:2], rms[:, tile, 0:1], 1.0 / D, EPS, ALU.mult, ALU.add).then_inc(rms_done, 1)
                eng.wait_ge(std_done, tile + 1)
                done(eng, eng.reciprocal(rms[:, tile, 3:4], rms[:, tile, 2:3]))
                done(eng, eng.scalar_tensor_tensor(out=xb, in0=h[:, tile, :], scalar=rms[:, tile, 3:4], in1=gain[g], op0=ALU.mult, op1=ALU.mult))
                eng.tensor_tensor(xb, xb, shift[g], ALU.add).then_inc(x_ready, 1)

            def latents(tile):
                ps, b = ps_ab[tile % 2], tile % 2
                eng.wait_ge(lat_sq, 2 * tile + 2)
                eng.tensor_scalar(rms[:, tile, 6:7], rms[:, tile, 4:5], 1.0 / Q_LORA, EPS, ALU.mult, ALU.add)
                eng.tensor_scalar(rms[:, tile, 7:8], rms[:, tile, 5:6], 1.0 / KV_LORA, EPS, ALU.mult, ALU.add).then_inc(lat_ms, 1)
                eng.tensor_copy(kpe[:, key_tile(tile), :], ps[:, BANK + KV_LORA:BANK + KV_LORA + ROPE])
                eng.wait_ge(lat_std, tile + 1)
                done(eng, eng.reciprocal(rms[:, tile, 10:12], rms[:, tile, 8:10]))
                eng.scalar_tensor_tensor(out=lat_q[b][:, :], in0=ps[:, 0:Q_LORA], scalar=rms[:, tile, 10:11], in1=q_a_norm[:, :], op0=ALU.mult, op1=ALU.mult)
                eng.scalar_tensor_tensor(out=lat_kv[b][:, :], in0=ps[:, BANK:BANK + KV_LORA], scalar=rms[:, tile, 11:12], in1=kv_a_norm[:, :],
                                         op0=ALU.mult, op1=ALU.mult).then_inc(lat_ready, 1)

            make_gain(0)
            eng.drain()
            norm(0)
            make_gain(1).then_inc(gains_made, 1)
            eng.wait_ge(small_in, 16 * 6)
            for tile in range(TILES):
                if tile + 1 < TILES:
                    norm(tile + 1)
                latents(tile)
            eng.drain()

            def over_heads(row):
                return row.unsqueeze(1).broadcast_to([P, HH, row.shape[1]])

            def over_dims(col, n):
                return col.unsqueeze(2).broadcast_to([P, HH, n])

            with eng.Fori(0, HALVES) as hh:
                for s in range(STEPS):
                    is_key, ps, out, ms = s < KEY_TILES, ps_ab[s % 2], heads_sb[s % 2], head_ms[s % 2]
                    eng.wait_ge(hd_sq, hh * STEPS + s + 1)
                    done(eng, eng.tensor_reduce(ms[:, 0, :], heads_sq[s % 2][:, :, :], AX.X, ALU.add))
                    eng.tensor_scalar(ms[:, 1, :], ms[:, 0, :], 1.0 / QK, EPS, ALU.mult, ALU.add).then_inc(hd_ms, 1)
                    eng.wait_ge(hd_std, hh * STEPS + s + 1)
                    done(eng, eng.reciprocal(ms[:, 0, :], ms[:, 2, :]))
                    if s >= 2:
                        eng.wait_ge(hd_tr, hh * STEPS + s - 1)
                    if is_key:
                        eng.tensor_tensor(out[:, :, NOPE:QK], over_heads(kpe[:, s, :]), over_dims(ms[:, 0, :], ROPE), ALU.mult)
                        eng.tensor_tensor(out[:, :, 0:NOPE], ps[:, :].rearrange("p (n w) -> p n w", n=HH)[:, :, 0:NOPE],
                                          over_dims(ms[:, 0, :], NOPE), ALU.mult).then_inc(hd_scaled, 1)
                    else:
                        for c in range(2):
                            m = HH // 2
                            last = eng.tensor_tensor(out[:, c * m:(c + 1) * m, :], ps[:, c * BANK:c * BANK + m * QK].rearrange("p (n w) -> p n w", n=m),
                                                     ms[:, 0, c * m:(c + 1) * m].unsqueeze(2).broadcast_to([P, m, QK]), ALU.mult)
                        last.then_inc(hd_scaled, 1)
                    eng.drain()
                    tile = s if is_key else s - KEY_TILES
                    ready = eng.tensor_tensor(out[:, :, :], out[:, :, :], over_heads(qk_gain[:, int(is_key), :]), ALU.mult)
                    if tile < SAMPLE_TILES:
                        eng.drain()
                        pairs = out[:, :, NOPE:QK].rearrange("p n (f two) -> p n f two", two=2)
                        x1, x2 = pairs[:, :, :, 0], pairs[:, :, :, 1]
                        c, d = over_heads(cos[:, tile, :]), over_heads(sin[:, tile, :])
                        eng.tensor_tensor(rope_tmp[:, 0, :, :], x1, c, ALU.mult)
                        eng.tensor_tensor(rope_tmp[:, 1, :, :], x2, d, ALU.mult)
                        eng.tensor_tensor(rope_tmp[:, 2, :, :], x1, d, ALU.mult)
                        done(eng, eng.tensor_tensor(rope_tmp[:, 3, :, :], x2, c, ALU.mult))
                        eng.tensor_tensor(x1, rope_tmp[:, 0, :, :], rope_tmp[:, 1, :, :], ALU.subtract)
                        ready = eng.tensor_tensor(x2, rope_tmp[:, 2, :, :], rope_tmp[:, 3, :, :], ALU.add)
                    ready.then_inc(hd_ready, 1)
                    eng.drain()

                def finish_heads(tile):
                    eng.wait_ge(pv_mm, hh * RUNS + (tile + 1) * HH)
                    done(eng, eng.reciprocal(sums[tile % 2][:, 1, :], sums[tile % 2][:, 0, :]))
                    eng.tensor_tensor(out_heads[tile][:, bass.ds(hh * (HH * VH), HH * VH)].rearrange("p (n w) -> p n w", n=HH),
                                      ps_d[:, (tile % 2) * BANK:(tile % 2 + 1) * BANK].rearrange("p (n w) -> p n w", n=HH),
                                      over_dims(sums[tile % 2][:, 1, :], VH), ALU.mult).then_inc(o_used, 1)

                def maximum(r):
                    _, n_keys = keys_of(r // HH)
                    eng.wait_ge(s_mm, hh * RUNS + r + 1)
                    done(eng, eng.tensor_reduce(neg_max[r % 2][:, 0:1], ps_ab[r % 2][:, 0:n_keys], AX.X, ALU.max))
                    eng.tensor_scalar(neg_max[r % 2][:, 1:2], neg_max[r % 2][:, 0:1], -SCALE, None, ALU.mult).then_inc(max_done, 1)

                def copy_probs(r):
                    _, n_keys = keys_of(r // HH)
                    eng.wait_ge(p_tr, hh * RUNS + r + 1)
                    if r >= 2:
                        eng.wait_ge(pv_mm, hh * RUNS + r - 1)
                    eng.tensor_copy(probsT[r % 2][:, 0:n_keys // P, :].rearrange("p c t -> p (c t)"), ps_c[:, 0:n_keys]).then_inc(p_ev, 1)

                maximum(0)
                for r in range(RUNS):
                    if r + 1 < RUNS:
                        maximum(r + 1)
                    copy_probs(r)
                    if r % HH == 2 and r > HH:
                        finish_heads(r // HH - 1)
                finish_heads(TILES - 1)

            eng.wait_ge(ow_in[0], 48)
            for tile in range(TILES):
                tmp = heads_sq[tile % 2][:, :, :].rearrange("p n w -> p (n w)")[:, 0:BANK]
                eng.wait_ge(out_mm, tile + 1)
                for c in range(2):
                    cols = slice(c * BANK, (c + 1) * BANK)
                    last = eng.tensor_tensor(tmp, ps_ab[tile % 2][:, cols], gate[group_of(tile)][:, cols], ALU.mult)
                    if c == 1:
                        last.then_inc(out_used, 1)
                    eng.drain()
                    done(eng, eng.tensor_tensor(h[:, tile, cols], h[:, tile, cols], tmp, ALU.add))


def peer_stage(nc, dram, layer, mod_rows, y_out, shared):
    h, ident, wq_sb, gain, shift = shared.h, shared.ident, shared.wq, shared.gain, shared.shift
    u_rows, v_rows = (dram[n].rearrange("l e d -> (l e) d") for n in ("peer_u", "peer_v"))
    first_row = layer * N_KEYS * N_KEYS
    with ExitStack() as ctx:
        def sb(name, shape, dt=F32):
            return ctx.enter_context(nc.sbuf_tensor(f"peer{layer}_{name}", shape, dt))

        def pb(name, shape, dt=F32):
            return ctx.enter_context(nc.psum_tensor(f"peer{layer}_{name}", shape, dt))

        sems = []

        def sem(name):
            sems.append(ctx.enter_context(nc.semaphore(f"p{layer}_{name}")))
            return sems[-1]

        u_ring = [sb(f"u{k}", [P, D]) for k in range(RING)]
        v_ring = [sb(f"v{k}", [P, D]) for k in range(RING)]
        x = [shared.x0, sb("x1", [P, D])[:, :]]
        xT = sb("xT", [P, KD, P])
        product = sb("product", [P, D], BF16)
        gate = [sb(f"gate{g}", [P, D]) for g in range(2)]
        keys_sb = sb("keys", [P, 2, P])
        keysT = sb("keysT", [P, 2, P])
        iota = sb("iota", [P, TOPK])
        zeros = sb("zeros", [P, HALF_BANK * 2], BF16)
        rms = sb("rms", [P, 4])
        q_sb = sb("q", [P, 2 * P])
        qT_sb = sb("qT", [P, 2, P])
        s_sb = sb("s", [P, 2, P])
        s_rest = sb("s_rest", [P, 2, P])
        top = sb("top", [P, 2, TOPK])
        top_at = sb("top_at", [P, 2, TOPK], U32)
        top_atf = sb("top_atf", [P, 2, TOPK])
        cand = sb("cand", [P, TOPK * TOPK])
        cand_rest = sb("cand_rest", [P, TOPK * TOPK])
        best = sb("best", [P, TOPK])
        best_at = sb("best_at", [P, TOPK], U32)
        side_at = sb("side_at", [P, TOPK, 2], U32)
        one_hot = sb("one_hot", [P, TOPK, 2, TOPK])
        picked = sb("picked", [P, TOPK, 2])
        expert = [sb(f"expert{b}", [P, TOPK], I32) for b in range(2)]
        neg_max = sb("neg_max", [P, 1])
        exps = [sb(f"exps{b}", [P, TOPK]) for b in range(2)]
        exp_sum = [sb(f"exp_sum{b}", [P, 1]) for b in range(2)]
        inv_sum = sb("inv_sum", [P, 1])
        dots = [sb(f"dots{b}", [P, RING]) for b in range(2)]
        gelus = [sb(f"gelus{b}", [P, RING]) for b in range(2)]
        weight = [sb(f"weight{b}", [P, RING]) for b in range(2)]
        diag = [sb(f"diag{b}", [P, P]) for b in range(DIAGS)]

        acc = pb("acc", [P, D])
        q_ps = pb("q_ps", [P, HALF_BANK * 2])
        qT_ps = pb("qT_ps", [P, HALF_BANK * 2])
        s_ps = pb("s_ps", [P, HALF_BANK * 2])
        xT_ps = pb("xT_ps", [P, KD, P])

        keys_in, gain_in = sem("keys_in"), sem("gain_in")
        gate_in = sem("gate_in")
        gains_made, consts = sem("gains_made"), sem("consts")
        keys_tr, keys_ev = sem("keys_tr"), sem("keys_ev")
        ssq_done, std_done, rms_done = sem("ssq"), sem("std"), sem("rms")
        x_ready, xT_tr, xT_ready = sem("x_ready"), sem("xT_tr"), sem("xT_ready")
        q_mm, q_ev, qT_tr, qT_ev, s_mm, s_ev = (sem(n) for n in ("q_mm", "q_ev", "qT_tr", "qT_ev", "s_mm", "s_ev"))
        best_done, exp_done, expert_done = sem("best"), sem("exp"), sem("expert")
        u_free, v_free = sem("u_free"), sem("v_free")
        gather_go = sem("gather_go")
        u_in = [sem(f"u_in{k}") for k in range(RING)]
        v_in = [sem(f"v_in{k}") for k in range(RING)]
        gelu_done, weight_done, diag_done = sem("gelu"), sem("weight"), sem("diag")
        acc_done, acc_used, y_done, y_stored = sem("acc_done"), sem("acc_used"), sem("y_done"), sem("y_st")

        ctx.callback(clear_semaphores, nc, sems)
        block = ctx.enter_context(nc.Block())

        @block.sync
        def _(eng):
            eng.dma_start(x[1], dram["norm2_g"][layer:layer + 1, :].broadcast_to([P, D])).then_inc(gain_in, 16)
            for side in range(2):
                eng.dma_start(keys_sb[:, side, :], dram["peer_keys"][layer, side]).then_inc(keys_in, 16)
            for g in range(2):
                eng.dma_start(gate[g][:, :], mod_rows[layer, g:g + 1, 5 * D:6 * D].broadcast_to([P, D])).then_inc(gate_in, 16)
            if y_out is not None:
                for tile in range(TILES):
                    eng.wait_ge(y_done, tile + 1)
                    eng.dma_start(y_out[tile], h[:, tile, :]).then_inc(y_stored, 16)
                eng.wait_ge(y_stored, 16 * TILES)

        @block.gpsimd
        def _(eng):
            eng.iota(iota[:, :], [[1, TOPK]], base=0, channel_multiplier=0, allow_small_or_imprecise_dtypes=True).then_inc(consts, 1)
            eng.memset(zeros[:, :], 0.0).then_inc(consts, 1)
            eng.sem_inc(u_free, RING)
            eng.sem_inc(v_free, RING)

            def head(g, par):
                eng.wait_ge(expert_done, g + 1)
                eng.sem_inc(gather_go, 1)
                for half in range(2):
                    for rows, ring, free, landed in ((u_rows, u_ring, u_free, u_in), (v_rows, v_ring, v_free, v_in)):
                        for k in range(RING):
                            slot = half * RING + k
                            eng.wait_ge(free, g * TOPK + slot + 1)
                            eng.sem_inc(gather_go, 1)
                            eng.indirect_dma_start(
                                out=ring[k][:, :], out_offset=None, in_=rows,
                                in_offset=bass.IndirectOffsetOnAxis(ap=expert[par][:, slot:slot + 1], axis=0),
                            ).then_inc(landed[k], 16)

            with eng.Fori(0, TILES * PEER_HEADS // 2) as i:
                head(2 * i, 0)
                head(2 * i + 1, 1)

        def group_of(tile):
            return 1 if tile == TILES - 1 else 0

        @block.vector
        def _(eng):
            eng.wait_ge(gain_in, 16)
            eng.wait_ge(shared.peer_vec_in, 64 * (layer + 1))
            for g in range(2):
                eng.scalar_tensor_tensor(out=gain[g], in0=gain[g], scalar=1.0, in1=x[1], op0=ALU.add, op1=ALU.mult).then_inc(gains_made, 1)
            eng.wait_ge(gains_made, 2)

            def norm(tile):
                xb = x[tile % 2]
                eng.wait_ge(ssq_done, tile + 1)
                done(eng, eng.tensor_scalar(rms[:, 1:2], rms[:, 0:1], 1.0 / D, EPS, ALU.mult, ALU.add))
                eng.tensor_scalar(rms[:, 2:3], rms[:, 1:2], 1.0, None, ALU.mult).then_inc(rms_done, 1)
                eng.wait_ge(std_done, tile + 1)
                done(eng, eng.reciprocal(rms[:, 3:4], rms[:, 1:2]))
                done(eng, eng.scalar_tensor_tensor(out=xb, in0=h[:, tile, :], scalar=rms[:, 3:4], in1=gain[group_of(tile)], op0=ALU.mult, op1=ALU.mult))
                eng.tensor_tensor(xb, xb, shift[group_of(tile)], ALU.add).then_inc(x_ready, 1)
                eng.wait_ge(x_ready, tile + 1)

            def top16(values, rest, vals, at):
                done(eng, eng.max(vals[:, 0:8], values))
                done(eng, eng.match_replace(out=rest, in_to_replace=vals[:, 0:8], in_values=values, imm_value=LOWEST))
                eng.max_index(at[:, 0:8], vals[:, 0:8], values)
                done(eng, eng.max(vals[:, 8:16], rest))
                done(eng, eng.max_index(at[:, 8:16], vals[:, 8:16], rest))

            def route(r, par, first=False):
                eng.wait_ge(s_mm, r + 1)
                eng.tensor_copy(s_sb[:, :, :].rearrange("p s n -> p (s n)"), s_ps[:, 0:2 * P]).then_inc(s_ev, 1)
                eng.drain()
                for side in range(2):
                    top16(s_sb[:, side, :], s_rest[:, side, :], top[:, side, :], top_at[:, side, :])
                if not first:
                    eng.wait_ge(exp_done, r)
                eng.tensor_scalar(top_atf[:, 0, :], top_at[:, 0, :], float(N_KEYS), float(first_row), ALU.mult, ALU.add)
                done(eng, eng.tensor_copy(top_atf[:, 1, :], top_at[:, 1, :]))
                done(eng, eng.tensor_tensor(cand[:, :].rearrange("p (a b) -> p a b", a=TOPK),
                                           top[:, 0, :].unsqueeze(2).broadcast_to([P, TOPK, TOPK]),
                                           top[:, 1, :].unsqueeze(1).broadcast_to([P, TOPK, TOPK]), ALU.add))
                top16(cand[:, :], cand_rest[:, :], best[:, :], best_at[:, :])
                eng.tensor_scalar(neg_max[:, :], best[:, 0:1], -1.0, None, ALU.mult).then_inc(best_done, 1)
                done(eng, eng.tensor_scalar(side_at[:, :, 0], best_at[:, :], 4, None, ALU.logical_shift_right))
                done(eng, eng.tensor_scalar(side_at[:, :, 1], best_at[:, :], 15, None, ALU.bitwise_and))
                hot = one_hot[:, :, :, :].rearrange("p k s a -> p (k s) a")
                done(eng, eng.tensor_tensor(hot, iota[:, :].unsqueeze(1).broadcast_to([P, 2 * TOPK, TOPK]),
                                           side_at[:, :, :].rearrange("p k s -> p (k s)").unsqueeze(2).broadcast_to([P, 2 * TOPK, TOPK]),
                                           ALU.is_equal))
                done(eng, eng.tensor_tensor(one_hot[:, :, :, :].rearrange("p k s a -> p k (s a)"),
                                           one_hot[:, :, :, :].rearrange("p k s a -> p k (s a)"),
                                           top_atf[:, :, :].rearrange("p s a -> p (s a)").unsqueeze(1).broadcast_to([P, TOPK, 2 * TOPK]),
                                           ALU.mult))
                done(eng, eng.tensor_reduce(picked[:, :, :].rearrange("p k s -> p (k s)"), hot, AX.X, ALU.add))
                if not first:
                    eng.wait_ge(v_free, r * TOPK - TOPK + RING)
                eng.tensor_tensor(expert[par][:, :], picked[:, :, 0], picked[:, :, 1], ALU.add).then_inc(expert_done, 1)

            def half_head(g, par, half, b):
                for k in range(RING):
                    n = g * TOPK + half * RING + k
                    eng.wait_ge(u_in[k], (2 * g + half + 1) * 16)
                    eng.wait_ge(u_free, n + RING)
                    eng.tensor_tensor_reduce(out=product[:, :], in0=u_ring[k][:, :], in1=x[b], scale=1.0, scalar=0.0,
                                             op0=ALU.mult, op1=ALU.add, accum_out=dots[half][:, k:k + 1]).then_inc(u_free, 1)
                if half == 0:
                    eng.wait_ge(exp_done, g + 1)
                    done(eng, eng.reciprocal(inv_sum[:, :], exp_sum[par][:, :]))
                eng.wait_ge(gelu_done, 2 * g + half + 1)
                eng.scalar_tensor_tensor(out=weight[half][:, :], in0=gelus[half][:, :], scalar=inv_sum[:, :],
                                         in1=exps[par][:, half * RING:(half + 1) * RING],
                                         op0=ALU.mult, op1=ALU.mult).then_inc(weight_done, 1)
                eng.wait_ge(weight_done, 2 * g + half + 1)

            def finish_tile(tile):
                eng.wait_ge(acc_done, tile + 1)
                tmp = x[tile % 2]
                done(eng, eng.tensor_tensor(tmp, acc[:, :], gate[group_of(tile)][:, :], ALU.mult))
                eng.tensor_tensor(h[:, tile, :], h[:, tile, :], tmp, ALU.add).then_inc(y_done, 1)
                eng.wait_ge(y_done, tile + 1)

            eng.wait_ge(consts, 2)
            norm(0)
            route(0, 0, first=True)
            eng.wait_ge(gate_in, 32)
            for tile in range(TILES):
                b = tile % 2
                if tile:
                    finish_tile(tile - 1)
                with eng.Fori(0, PEER_HEADS // 2 - 1) as i:
                    for par in range(2):
                        g = tile * PEER_HEADS + 2 * i + par
                        half_head(g, par, 0, b)
                        route(g + 1, 1 - par)
                        half_head(g, par, 1, b)
                for par in range(2):
                    g = tile * PEER_HEADS + PEER_HEADS - 2 + par
                    half_head(g, par, 0, b)
                    if g + 1 < TILES * PEER_HEADS:
                        route(g + 1, 1 - par)
                    half_head(g, par, 1, b)
                    if par == 0 and tile + 1 < TILES:
                        norm(tile + 1)
            finish_tile(TILES - 1)

        @block.scalar
        def _(eng):
            eng.wait_ge(keys_tr, 1)
            eng.activation(keysT[:, :, :].rearrange("p s n -> p (s n)"), qT_ps[:, 0:2 * P], ACT.Copy).then_inc(keys_ev, 1)

            def norm(tile):
                if tile == 1:
                    eng.wait_ge(gains_made, 2)
                eng.activation(x[tile % 2], h[:, tile, :], ACT.Square, accum_out=rms[:, 0:1]).then_inc(ssq_done, 1)
                eng.wait_ge(rms_done, tile + 1)
                eng.activation(rms[:, 1:2], rms[:, 2:3], ACT.Sqrt).then_inc(std_done, 1)
                for half in range(2):
                    eng.wait_ge(xT_tr, 2 * tile + half + 1)
                    eng.activation(xT[:, 4 * half:4 * half + 4, :].rearrange("p k t -> p (k t)"),
                                   xT_ps[:, 4 * half:4 * half + 4, :].rearrange("p k t -> p (k t)"), ACT.Copy).then_inc(xT_ready, 1)

            def route(r):
                eng.wait_ge(q_mm, r + 1)
                eng.activation(q_sb[:, :], q_ps[:, 0:2 * P], ACT.Copy).then_inc(q_ev, 1)
                eng.wait_ge(qT_tr, r + 1)
                eng.activation(qT_sb[:, :, :].rearrange("p s t -> p (s t)"), qT_ps[:, 0:2 * P], ACT.Copy).then_inc(qT_ev, 1)

            def softmax(r, par):
                eng.wait_ge(best_done, r + 1)
                eng.activation(exps[par][:, :], best[:, :], ACT.Exp, bias=neg_max[:, :], accum_out=exp_sum[par][:, :]).then_inc(exp_done, 1)

            def half_head(g, half):
                eng.wait_ge(u_free, g * TOPK + (half + 1) * RING + RING)
                eng.activation(gelus[half][:, :], dots[half][:, :], ACT.Gelu).then_inc(gelu_done, 1)
                eng.wait_ge(weight_done, 2 * g + half + 1)
                for k in range(RING):
                    n = g * TOPK + half * RING + k
                    eng.wait_ge(v_free, n - DIAGS + 1 + RING)
                    eng.activation(diag[k % DIAGS][:, :], ident[:, :], ACT.Copy, scale=weight[half][:, k:k + 1]).then_inc(diag_done, 1)

            norm(0)
            route(0)
            softmax(0, 0)
            for tile in range(TILES):
                with eng.Fori(0, PEER_HEADS // 2 - 1) as i:
                    for par in range(2):
                        g = tile * PEER_HEADS + 2 * i + par
                        route(g + 1)
                        half_head(g, 0)
                        softmax(g + 1, 1 - par)
                        half_head(g, 1)
                for par in range(2):
                    g = tile * PEER_HEADS + PEER_HEADS - 2 + par
                    more = g + 1 < TILES * PEER_HEADS
                    if more:
                        route(g + 1)
                    half_head(g, 0)
                    if more:
                        softmax(g + 1, 1 - par)
                    half_head(g, 1)
                    if par == 0 and tile + 1 < TILES:
                        norm(tile + 1)

        @block.tensor
        def _(eng):
            eng.wait_ge(keys_in, 32)
            for side in range(2):
                last = eng.transpose(qT_ps[:, side * P:(side + 1) * P], keys_sb[:, side, :], ident[:, :])
            last.then_inc(keys_tr, 1)
            eng.wait_ge(keys_ev, 1)

            def transpose_x(tile):
                eng.wait_ge(x_ready, tile + 1)
                for half in range(2):
                    if tile:
                        eng.wait_ge(xT_ready, 2 * tile - 1 + half)
                    for k in range(4 * half, 4 * half + 4):
                        last = eng.transpose(xT_ps[:, k, :], x[tile % 2][:, k * P:(k + 1) * P], ident[:, :])
                    last.then_inc(xT_tr, 1)

            def route(r, head, tile):
                if isinstance(head, int) and head == 0:
                    eng.wait_ge(xT_ready, 2 * tile + 2)
                first = isinstance(r, int) and r == 0
                if not first:
                    eng.wait_ge(q_ev, r)
                for k in range(KD):
                    last = eng.matmul(q_ps[:, 0:2 * P], xT[:, k, :], wq_sb[:, k, bass.ds(head * 2 * P, 2 * P)],
                                      start=(k == 0), stop=(k == KD - 1))
                last.then_inc(q_mm, 1)
                eng.wait_ge(q_ev, r + 1)
                if not first:
                    eng.wait_ge(qT_ev, r)
                for side in range(2):
                    last = eng.transpose(qT_ps[:, side * P:(side + 1) * P], q_sb[:, side * P:(side + 1) * P], ident[:, :])
                last.then_inc(qT_tr, 1)
                eng.wait_ge(qT_ev, r + 1)
                if not first:
                    eng.wait_ge(s_ev, r)
                for side in range(2):
                    last = eng.matmul(s_ps[:, side * P:(side + 1) * P], qT_sb[:, side, :], keysT[:, side, :], start=True, stop=True)
                last.then_inc(s_mm, 1)

            def half_head(g, half):
                for k in range(RING):
                    n = g * TOPK + half * RING + k
                    eng.wait_ge(v_in[k], (2 * g + half + 1) * 16)
                    eng.wait_ge(diag_done, n + 1)
                    for c in range(2):
                        last = eng.matmul(acc[:, c * BANK:(c + 1) * BANK], diag[k % DIAGS][:, :],
                                          v_ring[k][:, c * BANK:(c + 1) * BANK], start=False, stop=False)
                    last.then_inc(v_free, 1)

            def bound_sum(start):
                for c in range(2):
                    last = eng.matmul(acc[:, c * BANK:(c + 1) * BANK], zeros[:, 0:P], zeros[:, :], start=start, stop=not start)
                return last

            transpose_x(0)
            eng.wait_ge(consts, 2)
            eng.wait_ge(shared.wq_in, 16 * KD * (layer + 1))
            route(0, 0, 0)
            for tile in range(TILES):
                if tile:
                    eng.wait_ge(y_done, tile)
                bound_sum(True)
                with eng.Fori(0, PEER_HEADS // 2 - 1) as i:
                    for par in range(2):
                        g = tile * PEER_HEADS + 2 * i + par
                        route(g + 1, 2 * i + par + 1, tile)
                        half_head(g, 0)
                        half_head(g, 1)
                for par in range(2):
                    head = PEER_HEADS - 2 + par
                    g = tile * PEER_HEADS + head
                    if g + 1 < TILES * PEER_HEADS:
                        route(g + 1, (head + 1) % PEER_HEADS, tile + (head + 1) // PEER_HEADS)
                    half_head(g, 0)
                    half_head(g, 1)
                    if par == 0 and tile + 1 < TILES:
                        transpose_x(tile + 1)
                bound_sum(False).then_inc(acc_done, 1)
def build_program(nc, dram, outs):
    y_prompt, y_sample, new_ckv, new_kpe = outs
    mod_rows = nc.dram_tensor("modulation_rows", [DEPTH, 2, 6 * D], F32, kind="Internal").ap()
    with ExitStack() as ctx:
        shared = Shared(nc, ctx)
        y_tiles = [y_sample[0, t * P:(t + 1) * P, :] for t in range(SAMPLE_TILES)] + [y_prompt[0]]
        modulation_stage(nc, dram, mod_rows, shared)
        conv_stage(nc, dram, 0, 0, mod_rows, shared)
        peer_stage(nc, dram, 0, mod_rows, None, shared)
        attention_stage(nc, dram, 1, 0, mod_rows, new_ckv[0, 0], new_kpe[0, 0], shared)
        peer_stage(nc, dram, 1, mod_rows, y_tiles, shared)


_INPUTS = ["x_prompt", "x_sample", "cache_ckv", "cache_kpe", "c", "c_ctx", "mod_w", "mod_b", "norm1_g", "norm2_g",
           "conv_w_in", "conv_b_in", "conv_dw", "conv_dw_b", "conv_norm_g", "conv_w_out", "conv_b_out",
           "q_a_w", "q_a_norm", "q_b_w", "kv_a_w", "kv_a_norm", "kv_b_w", "q_norm", "k_norm", "o_w",
           "peer_wq", "peer_keys", "peer_u", "peer_v"]
_OUTPUTS = [("y_prompt", (1, SEQ, D)), ("y_sample", (1, DEC_SEQ, D)), ("new_ckv", (1, 1, SEQ, KV_LORA)), ("new_kpe", (1, 1, SEQ, ROPE))]


def _shape_constants():
    import numpy as np

    half = ROPE // 2
    row = np.repeat(np.arange(DEC_SEQ // GRID_W), GRID_W).astype(np.float32)
    col = np.tile(np.arange(GRID_W), DEC_SEQ // GRID_W).astype(np.float32)
    inv = (np.float32(ROPE_THETA) ** (-(np.arange(half // 2, dtype=np.float32) * np.float32(2.0) / np.float32(half)))).astype(np.float32)
    angle = np.concatenate([row[:, None] * inv, col[:, None] * inv], axis=-1).astype(np.float32)
    return {"identity": np.eye(P, dtype=np.float32), "rope_cos": np.cos(angle).astype(np.float32), "rope_sin": np.sin(angle).astype(np.float32)}


def kernel(**inputs):
    import numpy as np
    import concourse.bacc as bacc
    from concourse.bass_utils import run_bass_kernel_spmd

    nc = bacc.Bacc("TRN2", target_bir_lowering=False, num_devices=1)
    arrays, dram = {}, {}
    given = {name: np.ascontiguousarray(inputs[name]) for name in _INPUTS}
    given.update(_shape_constants())
    for name, a in given.items():
        arrays[f"in_{name}"] = a
        dram[name] = nc.dram_tensor(f"in_{name}", a.shape, mybir.dt.from_np(a.dtype), kind="ExternalInput").ap()
    outs = [nc.dram_tensor(f"out_{name}", shape, F32, kind="ExternalOutput").ap() for name, shape in _OUTPUTS]
    build_program(nc, dram, outs)
    r = run_bass_kernel_spmd(nc, [arrays], core_ids=[0])
    return tuple(r.results[0][f"out_{name}"] for name, _ in _OUTPUTS)
```
